# Optimizing a Trainium2 kernel written in Bass

```python
import jax, jax.numpy as jnp
from jax import lax
import numpy as np

D_MODEL = 1024
BATCH = 1
SEQ = 128
DEPTH = 2
DEC_BATCH = 1
DEC_SEQ = 256
PAST_LEN = 128

GRID_W = 64
HEAD_DIM = 64
ATT_DIM = D_MODEL // 2
RWKV_DIM = D_MODEL // 4
CONV_DIM = D_MODEL // 4
MIX_DIM = ATT_DIM + RWKV_DIM + CONV_DIM
ATT_HEADS = ATT_DIM // HEAD_DIM
ATT_KV_HEADS = 2
ATT_GROUP = ATT_HEADS // ATT_KV_HEADS
KV_DIM = ATT_KV_HEADS * HEAD_DIM
WINDOW = 128
ATT_BLOCK = 128
ROPE_THETA = 10000.0
RWKV_HEADS = RWKV_DIM // HEAD_DIM
W_RANK = 32
A_RANK = 32
G_RANK = 64
RWKV_LNX_EPS = 64e-5
CONV_WIDTH = 3
CONV_GROUPS = CONV_DIM // HEAD_DIM
PEER_HEADS = 8
PEER_NKEYS = 128
PEER_EXPERTS = PEER_NKEYS * PEER_NKEYS
PEER_TOPK = 16
PEER_DKEY = 256
PEER_HALF = PEER_DKEY // 2
PEER_CHUNK = 128
LN_EPS = 1e-5
ALPHA = (2 * DEPTH) ** 0.25
BETA = (8 * DEPTH) ** -0.25
NEG = -1e30
IN_WIDTHS = (ATT_DIM, KV_DIM, KV_DIM,
             RWKV_DIM, RWKV_DIM, RWKV_DIM, 2 * W_RANK, 2 * A_RANK, G_RANK,
             CONV_DIM, CONV_DIM, CONV_DIM)
IN_TOTAL = sum(IN_WIDTHS)
SPLIT_POINTS = tuple(int(s) for s in np.cumsum(IN_WIDTHS)[:-1])

kernel_name = 'hybrid_diffusion_rwkv7_conv_swa_peer_step'

def layer_norm(x, g, b, eps=LN_EPS):
    xf = x.astype(jnp.float32)
    mu = jnp.mean(xf, axis=-1, keepdims=True)
    var = jnp.mean(jnp.square(xf - mu), axis=-1, keepdims=True)
    return ((xf - mu) * lax.rsqrt(var + eps)).astype(x.dtype) * g + b

def _rope_axis(x, pos):
    half = x.shape[-1] // 2
    freqs = ROPE_THETA ** (-jnp.arange(half, dtype=jnp.float32) / half)
    ang = pos.astype(jnp.float32)[:, None] * freqs[None, :]
    cos = jnp.cos(ang)[None, :, None, :]
    sin = jnp.sin(ang)[None, :, None, :]
    x1, x2 = x[..., :half], x[..., half:]
    return jnp.concatenate([x1 * cos - x2 * sin, x1 * sin + x2 * cos], axis=-1).astype(x.dtype)

def rope_2d(x):
    n = x.shape[1]
    rows = n // GRID_W
    t = jnp.arange(rows * GRID_W)
    row, col = t // GRID_W, t % GRID_W
    ax = x.shape[-1] // 2
    return jnp.concatenate([_rope_axis(x[..., :ax], row), _rope_axis(x[..., ax:], col)], axis=-1)

def context_attention(q, k, v, sink):
    b, c = q.shape[:2]
    qg = q.reshape(b, c, ATT_KV_HEADS, ATT_GROUP, HEAD_DIM)
    s = jnp.einsum('bqhgd,bkhd->bhgqk', qg, k).astype(jnp.float32) * (HEAD_DIM ** -0.5)
    sink_l = jnp.broadcast_to(sink.astype(jnp.float32).reshape(1, ATT_KV_HEADS, ATT_GROUP, 1, 1), s.shape[:-1] + (1,))
    p = jax.nn.softmax(jnp.concatenate([sink_l, s], axis=-1), axis=-1)[..., 1:].astype(v.dtype)
    out = jnp.einsum('bhgqk,bkhd->bqhgd', p, v)
    return out.reshape(b, c, ATT_DIM)

def window_attention(q, k, v, ck, cv, sink):
    b, s = q.shape[:2]
    nb = s // ATT_BLOCK
    c = ck.shape[1]
    qb = q.reshape(b, nb, ATT_BLOCK, ATT_KV_HEADS, ATT_GROUP, HEAD_DIM)

    def band(t):
        tb = t.reshape(b, nb, ATT_BLOCK, ATT_KV_HEADS, HEAD_DIM)
        tp = jnp.pad(tb, ((0, 0), (1, 1), (0, 0), (0, 0), (0, 0)))
        return jnp.concatenate([tp[:, :-2], tp[:, 1:-1], tp[:, 2:]], axis=2)

    kw, vw = band(k), band(v)
    scale = HEAD_DIM ** -0.5
    s_win = jnp.einsum('bnqhgd,bnkhd->bnhgqk', qb, kw).astype(jnp.float32) * scale
    s_ctx = jnp.einsum('bnqhgd,bchd->bnhgqc', qb, ck).astype(jnp.float32) * scale
    qi = jnp.arange(ATT_BLOCK)[:, None]
    kj = jnp.arange(3 * ATT_BLOCK)[None, :]
    rel = kj - ATT_BLOCK - qi
    kpos = (jnp.arange(nb)[:, None, None] - 1) * ATT_BLOCK + kj[None]
    mask = (jnp.abs(rel) <= WINDOW)[None] & (kpos >= 0) & (kpos < s)
    s_win = jnp.where(mask[None, :, None, None], s_win, NEG)
    sink_l = jnp.broadcast_to(sink.astype(jnp.float32).reshape(1, 1, ATT_KV_HEADS, ATT_GROUP, 1, 1), s_ctx.shape[:-1] + (1,))
    p = jax.nn.softmax(jnp.concatenate([sink_l, s_ctx, s_win], axis=-1), axis=-1).astype(v.dtype)
    p_ctx, p_win = p[..., 1:1 + c], p[..., 1 + c:]
    out = jnp.einsum('bnhgqc,bchd->bnqhgd', p_ctx, cv) + jnp.einsum('bnhgqk,bnkhd->bnqhgd', p_win, vw)
    return out.reshape(b, s, ATT_DIM)

def rwkv_scan(r, w, k, v, a, b, s0, reverse):
    xs = tuple(jnp.moveaxis(z.astype(jnp.float32), 1, 0) for z in (r, w, k, v, a, b))

    def step(s, inp):
        r_t, w_t, k_t, v_t, a_t, b_t = inp
        sa = jnp.einsum('bhij,bhj->bhi', s, a_t)
        s = s * w_t[:, :, None, :] + sa[..., None] * b_t[:, :, None, :] + v_t[..., None] * k_t[:, :, None, :]
        return s, jnp.einsum('bhij,bhj->bhi', s, r_t)

    s_fin, ys = lax.scan(step, s0.astype(jnp.float32), xs, reverse=reverse)
    return jnp.moveaxis(ys, 0, 1), s_fin

def rwkv_time_mix(r, k, v, w_down, a_down, g_down, s0, w0, w_up, a0, a_up, g_up, k_k, k_a, r_k, lnx_g, lnx_b):
    bsz, t = r.shape[:2]

    def heads(z):
        return z.reshape(bsz, t, RWKV_HEADS, HEAD_DIM)

    kk = heads(k * k_k).astype(jnp.float32)
    kk = kk * lax.rsqrt(jnp.maximum(jnp.sum(kk * kk, axis=-1, keepdims=True), 1e-24))
    rh, vh = heads(r), heads(v)
    rk_h = r_k.reshape(RWKV_HEADS, HEAD_DIM)
    ys, bonus, finals = [], [], []
    for d in range(2):
        w_log = -jax.nn.softplus(-(w0[d] + jnp.tanh(w_down[..., d * W_RANK:(d + 1) * W_RANK]) @ w_up[d])) - 0.5
        w = jnp.exp(-jnp.exp(w_log.astype(jnp.float32)))
        a = jax.nn.sigmoid(a0[d] + a_down[..., d * A_RANK:(d + 1) * A_RANK] @ a_up[d])
        kd = heads(k * (1.0 + (a - 1.0) * k_a))
        y, s_fin = rwkv_scan(rh, heads(w), kd, vh, -kk, kk * heads(a).astype(jnp.float32), s0[:, d], reverse=(d == 1))
        ys.append(y)
        finals.append(s_fin)
        bonus.append(jnp.sum(rh * kd * rk_h, axis=-1, keepdims=True) * vh)
    y = ys[0] + ys[1]
    mu = jnp.mean(y, axis=-1, keepdims=True)
    var = jnp.mean(jnp.square(y - mu), axis=-1, keepdims=True)
    yn = ((y - mu) * lax.rsqrt(var + RWKV_LNX_EPS)).reshape(bsz, t, RWKV_DIM).astype(r.dtype) * lnx_g + lnx_b
    g = jax.nn.sigmoid(g_down) @ g_up
    out = (yn + (bonus[0] + bonus[1]).reshape(bsz, t, RWKV_DIM)) * g
    return out, jnp.stack(finals, axis=1).astype(r.dtype)

def short_conv(bg, cg, u, w):
    z = cg * u
    zp = jnp.pad(z, ((0, 0), (1, 1), (0, 0)))
    y = w[0] * zp[:, :-2] + w[1] * zp[:, 1:-1] + w[2] * zp[:, 2:]
    return bg * y

def peer_ffn(h, wq, subkeys, u_tab, v_tab):
    b, s, d = h.shape
    xc = h.reshape(-1, PEER_CHUNK, d)

    def chunk(xt):
        q = (xt @ wq).reshape(PEER_CHUNK, PEER_HEADS, 2, PEER_HALF)
        sc = jnp.einsum('thpd,hpnd->thpn', q, subkeys).astype(jnp.float32)
        s_top, i_top = lax.top_k(sc, PEER_TOPK)
        cand = (s_top[:, :, 0, :, None] + s_top[:, :, 1, None, :]).reshape(PEER_CHUNK, PEER_HEADS, PEER_TOPK * PEER_TOPK)
        cidx = (i_top[:, :, 0, :, None] * PEER_NKEYS + i_top[:, :, 1, None, :]).reshape(PEER_CHUNK, PEER_HEADS, PEER_TOPK * PEER_TOPK)
        f_s, f_i = lax.top_k(cand, PEER_TOPK)
        e = jnp.take_along_axis(cidx, f_i, axis=-1)
        g = jax.nn.softmax(f_s, axis=-1).astype(xt.dtype)
        act = jax.nn.gelu(jnp.einsum('thkd,td->thk', u_tab[e], xt))
        return jnp.einsum('thk,thkd->td', g * act, v_tab[e])

    return lax.map(chunk, xc).reshape(b, s, d)

def trunk_layer(x, mod, ctx, w_in, w_out, sink, rw_w0, rw_w_up, rw_a0, rw_a_up, rw_g_up, rw_kk, rw_ka, rw_rk,
                rw_lnx_g, rw_lnx_b, conv_w, ln1_g, ln1_b, ln2_g, ln2_b, peer_wq, peer_subkeys, peer_u, peer_v):
    sh1, sc1, g1, sh2, sc2, g2 = jnp.split(mod, 6, axis=-1)
    b, s = x.shape[:2]
    h = x * (1.0 + sc1) + sh1
    p = h @ w_in
    aq, ak, av, rr, rk, rv, wd, ad, gd, cb, cc, cu = jnp.split(p, SPLIT_POINTS, axis=-1)
    aq = aq.reshape(b, s, ATT_HEADS, HEAD_DIM)
    ak = ak.reshape(b, s, ATT_KV_HEADS, HEAD_DIM)
    av = av.reshape(b, s, ATT_KV_HEADS, HEAD_DIM)
    if ctx is None:
        att = context_attention(aq, ak, av, sink)
        s0 = jnp.zeros((b, 2, RWKV_HEADS, HEAD_DIM, HEAD_DIM), jnp.float32)
    else:
        ck, cv, s0 = ctx
        att = window_attention(rope_2d(aq), rope_2d(ak), av, ck, cv, sink)
    rw, s_fin = rwkv_time_mix(rr, rk, rv, wd, ad, gd, s0, rw_w0, rw_w_up, rw_a0, rw_a_up, rw_g_up,
                              rw_kk, rw_ka, rw_rk, rw_lnx_g, rw_lnx_b)
    cvo = short_conv(cb, cc, cu, conv_w)
    mix = jnp.concatenate([att, rw, cvo], axis=-1) @ w_out
    x = layer_norm(ALPHA * x + g1 * mix, ln1_g, ln1_b)
    h = x * (1.0 + sc2) + sh2
    x = layer_norm(ALPHA * x + g2 * peer_ffn(h, peer_wq, peer_subkeys, peer_u, peer_v), ln2_g, ln2_b)
    if ctx is None:
        return x, (ak, av, s_fin)
    return x, None

def setup_inputs(seed: int = 0) -> dict:
    key = jax.random.key(seed)
    ks = jax.random.split(key, 40)
    f32 = jnp.float32
    D = D_MODEL

    def nrm(i, shape, scale=1.0):
        return scale * jax.random.normal(ks[i], shape, f32)

    return {
        'x_prompt': nrm(0, (BATCH, SEQ, D)),
        'x_sample': nrm(1, (DEC_BATCH, DEC_SEQ, D)),
        'cache_k': nrm(2, (DEC_BATCH, DEPTH, PAST_LEN, ATT_KV_HEADS, HEAD_DIM)),
        'cache_v': nrm(3, (DEC_BATCH, DEPTH, PAST_LEN, ATT_KV_HEADS, HEAD_DIM)),
        'state_rwkv': nrm(4, (DEC_BATCH, DEPTH, 2, RWKV_HEADS, HEAD_DIM, HEAD_DIM), 0.3),
        'c': nrm(5, (DEC_BATCH, D)),
        'c_ctx': nrm(6, (D,)),
        'ln_in_g': 1.0 + nrm(7, (D,), 0.02),
        'ln_in_b': nrm(8, (D,), 0.02),
        'w_ada': nrm(9, (DEPTH, D, 6 * D), 0.5 * D ** -0.5),
        'b_ada': nrm(10, (DEPTH, 6 * D), 0.02),
        'w_in': nrm(11, (DEPTH, D, IN_TOTAL), D ** -0.5),
        'w_out': nrm(12, (DEPTH, MIX_DIM, D), BETA * MIX_DIM ** -0.5),
        'att_sink': nrm(13, (DEPTH, ATT_HEADS), 0.5),
        'rw_w0': jax.random.uniform(ks[14], (DEPTH, 2, RWKV_DIM), f32, -6.0, 0.0),
        'rw_w_up': nrm(15, (DEPTH, 2, W_RANK, RWKV_DIM), 0.1),
        'rw_a0': nrm(16, (DEPTH, 2, RWKV_DIM), 0.5),
        'rw_a_up': nrm(17, (DEPTH, 2, A_RANK, RWKV_DIM), 0.5 * A_RANK ** -0.5),
        'rw_g_up': nrm(18, (DEPTH, G_RANK, RWKV_DIM), G_RANK ** -0.5),
        'rw_kk': 0.85 + nrm(19, (DEPTH, RWKV_DIM), 0.1),
        'rw_ka': 1.0 + nrm(20, (DEPTH, RWKV_DIM), 0.1),
        'rw_rk': nrm(21, (DEPTH, RWKV_DIM), 0.1),
        'rw_lnx_g': 1.0 + nrm(22, (DEPTH, RWKV_DIM), 0.02),
        'rw_lnx_b': nrm(23, (DEPTH, RWKV_DIM), 0.02),
        'conv_w': nrm(24, (DEPTH, CONV_WIDTH, CONV_DIM), CONV_WIDTH ** -0.5),
        'ln1_g': 1.0 + nrm(25, (DEPTH, D), 0.02),
        'ln1_b': nrm(26, (DEPTH, D), 0.02),
        'ln2_g': 1.0 + nrm(27, (DEPTH, D), 0.02),
        'ln2_b': nrm(28, (DEPTH, D), 0.02),
        'peer_wq': nrm(29, (DEPTH, D, PEER_HEADS * PEER_DKEY), D ** -0.5),
        'peer_subkeys': nrm(30, (DEPTH, PEER_HEADS, 2, PEER_NKEYS, PEER_HALF), PEER_HALF ** -0.5),
        'peer_u': nrm(31, (DEPTH, PEER_EXPERTS, D), D ** -0.5),
        'peer_v': nrm(32, (DEPTH, PEER_EXPERTS, D), BETA),
    }

def reference(x_prompt, x_sample, cache_k, cache_v, state_rwkv, c, c_ctx, ln_in_g, ln_in_b, w_ada, b_ada,
              w_in, w_out, att_sink, rw_w0, rw_w_up, rw_a0, rw_a_up, rw_g_up, rw_kk, rw_ka, rw_rk,
              rw_lnx_g, rw_lnx_b, conv_w, ln1_g, ln1_b, ln2_g, ln2_b, peer_wq, peer_subkeys, peer_u, peer_v):
    xp = layer_norm(x_prompt, ln_in_g, ln_in_b)
    xs = layer_norm(x_sample, ln_in_g, ln_in_b)
    ks, vs, sts = [], [], []
    for l in range(DEPTH):
        mod_ctx = (jax.nn.silu(c_ctx) @ w_ada[l] + b_ada[l])[None, None, :]
        mod_lat = (jax.nn.silu(c) @ w_ada[l] + b_ada[l])[:, None, :]
        wl = (w_in[l], w_out[l], att_sink[l], rw_w0[l], rw_w_up[l], rw_a0[l], rw_a_up[l], rw_g_up[l],
              rw_kk[l], rw_ka[l], rw_rk[l], rw_lnx_g[l], rw_lnx_b[l], conv_w[l], ln1_g[l], ln1_b[l],
              ln2_g[l], ln2_b[l], peer_wq[l], peer_subkeys[l], peer_u[l], peer_v[l])
        xp, (k_l, v_l, s_l) = trunk_layer(xp, mod_ctx, None, *wl)
        ks.append(k_l)
        vs.append(v_l)
        sts.append(s_l)
        xs, _ = trunk_layer(xs, mod_lat, (cache_k[:, l], cache_v[:, l], state_rwkv[:, l]), *wl)
    new_k = jnp.stack(ks, axis=1)
    new_v = jnp.stack(vs, axis=1)
    new_s = jnp.stack(sts, axis=1)
    return (xp, xs, new_k, new_v, new_s)


_drawn_inputs = setup_inputs


def setup_inputs(seed=0):
    import zlib

    import numpy as np

    out = dict(_drawn_inputs(seed))
    spreads = {}
    factors = {'cache_k': 6.156,
     'cache_v': 5.569,
     'state_rwkv': 8.0,
     'att_sink': 41.878,
     'rw_lnx_g': 43.432,
     'rw_lnx_b': 44.083}
    for name, (base, spread) in spreads.items():
        noise = np.random.default_rng([zlib.crc32(name.encode()), seed]).standard_normal(out[name].shape)
        drawn = base * np.exp(spread * noise) if base else spread * noise
        out[name] = __import__('jax').numpy.asarray(drawn.astype(out[name].dtype))
    for name, factor in factors.items():
        out[name] = (out[name] * factor).astype(out[name].dtype)
    return out
```

```python
import numpy as np
import concourse.bass as bass
from concourse import mybir
from concourse.alu_op_type import AluOpType as ALU
from contextlib import ExitStack

ACT = mybir.ActivationFunctionType
AX = mybir.AxisListType
F32, F32R, BF16, U32 = mybir.dt.float32, mybir.dt.float32r, mybir.dt.bfloat16, mybir.dt.uint32

P = 128
D = 1024
KD = D // P
DEPTH = 2
TILES = 3
TOK = TILES * P
SEQ_OF_TILE = (0, 1, 1)
HD = 64
RANK = 32
CHUNK = 64
N_LEVELS = 6
HEADS = 8
N_IN = 20
QB, KB, VB, RB, RKB, RVB, WAB, GB, CBB, CCB, CUB = 0, 4, 5, 6, 8, 10, 12, 13, 14, 16, 18
NEG = -1e30
LN_EPS, LNX_EPS = 1e-5, 64e-5
ALPHA = (2 * DEPTH) ** 0.25
TOPK = 16
NK = 128
PH = 8
JG = 32
JSTEP = TOK * 1 // JG

SLOTS = 4
PIECE = 2048
N_ADA, N_PIN, N_POUT, N_PQ, N_PEXP = 24, 10, 4, 8, 128
AT_IN = N_ADA
AT_OUT = AT_IN + N_PIN
AT_Q = AT_OUT + N_POUT
AT_EXP = AT_Q + N_PQ
C_W0, C_A0, C_KK, C_KA, C_RK, C_LG, C_LB, C_CW, N_COLS = 0, 4, 8, 10, 12, 14, 16, 18, 24


def slot(n):
    return n % SLOTS


def filled(n):
    return 16 * (n // SLOTS + 1)


class Turns:

    def __init__(self, names, banks):
        self.n = {name: i for i, name in enumerate(names)}
        self.banks = banks

    def at(self, *name):
        i = self.n[name]
        return i % self.banks, i // self.banks


def layer_row(ap, l):
    row = ap[bass.ds(l, 1)]
    names = " ".join(f"x{i}" for i in range(len(ap.shape) - 1))
    first, rest = names.split(" ", 1) if " " in names else (names, "")
    return row.rearrange(f"a {names} -> (a {first}) {rest}")


def norm_steps(nc, dve, link, x, stats, mv, rstd, var_ready, std_ready, count, g, b, out):
    for h in range(2):
        ins = nc.vector.bn_stats(stats[:, 6 * h:6 * h + 6], x[:, 512 * h:512 * h + 512])
    link(ins)
    link(nc.vector.bn_aggr(mv, stats))
    nc.vector.tensor_scalar(mv[:, 1:2], mv[:, 1:2], LN_EPS, None, ALU.add).then_inc(var_ready, 1)
    dve.wait_ge(std_ready, count)
    link(nc.vector.reciprocal(rstd, rstd))
    link(nc.vector.tensor_scalar(out, x, mv[:, 0:1], rstd, ALU.subtract, ALU.mult))
    link(nc.vector.tensor_tensor(out, out, g, ALU.mult))
    return nc.vector.tensor_tensor(out, out, b, ALU.add)


def clear(nc, sems):
    for s in sems:
        nc.sync.sem_clear(s)
    nc.all_engine_barrier()


class Core:
    pass


def make_core(nc, ctx, dram):
    c = Core()
    c.nc, c.dram = nc, dram
    sb = lambda name, shape, dt=F32: ctx.enter_context(nc.sbuf_tensor(name, shape, dt))
    sem = lambda name: ctx.enter_context(nc.semaphore(name))
    c.ring = sb("ring", [P, SLOTS, PIECE])
    c.ident = sb("ident", [P, P])
    c.mod_cols = sb("mod_cols", [P, 4, KD, 2])
    c.ring_full = [sem(f"ring_full{i}") for i in range(SLOTS)]
    c.x_dram = nc.dram_tensor("x_between_blocks", [TILES, P, D], F32, kind="Internal").ap()
    c.gate_dram = nc.dram_tensor("gate_rows", [2, 2, D], F32, kind="Internal").ap()
    return c


def piece_source(c, l, n):
    for first, name in ((AT_EXP, "u"), (AT_Q, "wq"), (AT_OUT, "w_out"), (AT_IN, "w_in"), (0, "w_ada")):
        if n >= first:
            break
    m = n - first
    if name == "u":
        name, m = ("u", "v")[m % 2], m // 2
    return c.dram[name][bass.ds(l, 1), m].rearrange("a p n -> (a p) n")


def fill_slot(c, sp, l, n):
    sp.dma_start(c.ring[:, slot(n), :], piece_source(c, l, n)).then_inc(c.ring_full[slot(n)], 16)


def input_norm(c):
    nc, dram = c.nc, c.dram
    with ExitStack() as ctx:
        sb = lambda name, shape, dt=F32: ctx.enter_context(nc.sbuf_tensor(name, shape, dt))
        sem = lambda name: ctx.enter_context(nc.semaphore(name))
        x = sb("in_x", [P, TILES, D])
        gb = sb("in_gb", [P, 2, D])
        stats, mv, rstd = sb("in_stats", [P, TILES, 12]), sb("in_mv", [P, TILES, 2]), sb("in_rstd", [P, TILES])
        loaded, var_ready, std_ready, normed, stored, vdone = map(
            sem, ("in_loaded", "in_var_ready", "in_std_ready", "in_normed", "in_stored", "in_vdone"))
        with nc.Block() as block:

            @block.sync
            def _(sp):
                sp.dma_start(c.ident[:, :], dram["ident"]).then_inc(loaded, 16)
                for t in range(TILES):
                    sp.dma_start(x[:, t, :], dram["x_in"][t]).then_inc(loaded, 16)
                for i in range(2):
                    sp.dma_start(gb[:, i, :], dram["ln_in"][i].partition_broadcast(P)).then_inc(loaded, 16)
                for t in range(TILES):
                    sp.wait_ge(normed, t + 1)
                    sp.dma_start(c.x_dram[t], x[:, t, :]).then_inc(stored, 16)
                sp.wait_ge(stored, 16 * TILES)

            @block.scalar
            def _(act):
                for t in range(TILES):
                    act.wait_ge(var_ready, t + 1)
                    nc.scalar.activation(rstd[:, t:t + 1], mv[:, t, 1:2], ACT.Sqrt).then_inc(std_ready, 1)

            @block.vector
            def _(dve):
                count = [0]

                def link(ins):
                    count[0] += 1
                    ins.then_inc(vdone, 1)
                    dve.wait_ge(vdone, count[0])

                dve.wait_ge(loaded, 16 * (TILES + 3))
                for t in range(TILES):
                    norm_steps(nc, dve, link, x[:, t, :], stats[:, t, :], mv[:, t, :], rstd[:, t:t + 1],
                               var_ready, std_ready, t + 1, gb[:, 0, :], gb[:, 1, :], x[:, t, :]).then_inc(normed, 1)
        clear(nc, [loaded, var_ready, std_ready, normed, stored, vdone])


def modulation(c, l):
    nc, dram = c.nc, c.dram
    steps = Turns([("ada", n) for n in range(N_ADA)] + [("cols",)], 8)
    NW = PIECE // KD
    with ExitStack() as ctx:
        sb = lambda name, shape, dt=F32: ctx.enter_context(nc.sbuf_tensor(name, shape, dt))
        sem = lambda name: ctx.enter_context(nc.semaphore(name))
        cond, cexp, silu = sb("cond", [P, KD, 2]), sb("cond_exp", [P, KD, 2]), sb("cond_silu", [P, KD, 2])
        bias = sb("ada_bias", [2, 6 * D])
        mod = sb("mod_rows", [2, 6 * D])
        bank = [ctx.enter_context(nc.psum_tensor(f"mod_bank{i}", [P, 512], F32)) for i in range(8)]
        full = [sem(f"mod_full{i}") for i in range(8)]
        free = [sem(f"mod_free{i}") for i in range(8)]
        loaded, exp_ready, vdone, gates_stored = map(sem, ("mod_loaded", "mod_exp", "mod_vdone", "gates_stored"))
        cond_ready, gates_ready = sem("cond_ready"), sem("gates_ready")
        sems = full + free + [loaded, exp_ready, vdone, gates_stored, cond_ready, gates_ready]
        with nc.Block() as block:

            @block.sync
            def _(sp):
                for n in range(AT_IN + SLOTS):
                    if n >= SLOTS:
                        b, r = steps.at("ada", n - SLOTS)
                        sp.wait_ge(full[b], r + 1)
                    fill_slot(c, sp, l, n)

            @block.scalar
            def _(act):
                act.dma_start(cond[:, :, :], dram["cond"]).then_inc(loaded, 16)
                act.dma_start(bias[:, :], layer_row(dram["b_ada"], l)).then_inc(loaded, 16)
                act.wait_ge(loaded, 32)
                nc.scalar.activation(cexp[:, :, :], cond[:, :, :], ACT.Exp, scale=-1.0).then_inc(exp_ready, 1)
                act.wait_ge(gates_ready, 1)
                for i, q in enumerate((2, 5)):
                    act.dma_start(c.gate_dram[i], mod[:, q * D:(q + 1) * D]).then_inc(gates_stored, 16)
                act.wait_ge(gates_stored, 32)

            @block.vector
            def _(dve):
                dve.wait_ge(exp_ready, 1)
                nc.vector.tensor_scalar(cexp[:, :, :], cexp[:, :, :], 1.0, None, ALU.add).then_inc(vdone, 1)
                dve.wait_ge(vdone, 1)
                nc.vector.reciprocal(cexp[:, :, :], cexp[:, :, :]).then_inc(vdone, 1)
                dve.wait_ge(vdone, 2)
                nc.vector.tensor_tensor(silu[:, :, :], cond[:, :, :], cexp[:, :, :], ALU.mult).then_inc(cond_ready, 1)
                for n in range(N_ADA):
                    b, r = steps.at("ada", n)
                    dve.wait_ge(full[b], r + 1)
                    ins = nc.vector.tensor_tensor(mod[:, n * NW:(n + 1) * NW], bank[b][0:2, 0:NW],
                                                  bias[:, n * NW:(n + 1) * NW], ALU.add)
                    ins.then_inc(free[b], 1)
                b, r = steps.at("cols")
                dve.wait_ge(full[b], r + 1)
                cols = bank[b][:, 0:64].rearrange("p (q k s) -> p q k s", q=4, k=KD)
                nc.vector.tensor_copy(c.mod_cols[:, 0::2], cols[:, 0::2])
                nc.vector.tensor_scalar(c.mod_cols[:, 1::2], cols[:, 1::2], 1.0, None, ALU.add).then_inc(gates_ready, 1)

            @block.tensor
            def _(pe):
                pe.wait_ge(cond_ready, 1)
                for n in range(N_ADA):
                    b, r = steps.at("ada", n)
                    pe.wait_ge(c.ring_full[slot(n)], filled(n))
                    pe.wait_ge(free[b], r)
                    w = c.ring[:, slot(n), :].rearrange("p (k n) -> p k n", k=KD)
                    for k in range(KD):
                        ins = nc.tensor.matmul(bank[b][0:2, 0:NW], silu[:, k, :], w[:, k, :],
                                               start=(k == 0), stop=(k == KD - 1))
                    ins.then_inc(full[b], 1)
                b, r = steps.at("cols")
                for n in range(N_ADA - 8, N_ADA):
                    bb, rr = steps.at("ada", n)
                    pe.wait_ge(free[bb], rr + 1)
                for i, q in enumerate((0, 1, 3, 4)):
                    for k in range(KD):
                        ins = nc.tensor.transpose(bank[b][:, 2 * (i * KD + k):2 * (i * KD + k) + 2],
                                                  mod[:, q * D + k * P:q * D + (k + 1) * P], c.ident[0:2, 0:2])
                ins.then_inc(full[b], 1)
        clear(nc, sems)


class Stage:

    def __init__(self, c, ctx, name, turns, semaphores, banks=8):
        self.nc, self.ctx, self.name = c.nc, ctx, name
        self.steps = Turns(turns, banks)
        self.bank = [ctx.enter_context(c.nc.psum_tensor(f"{name}_bank{i}", [P, 512], F32)) for i in range(banks)]
        self.full = [self.sem(f"full{i}") for i in range(banks)]
        self.free = [self.sem(f"free{i}") for i in range(banks)]
        self.named = {n: self.sem(n) for n in semaphores}
        self.sems = self.full + self.free + list(self.named.values())

    def sem(self, name):
        return self.ctx.enter_context(self.nc.semaphore(f"{self.name}_{name}"))

    def sb(self, name, shape, dt=F32):
        return self.ctx.enter_context(self.nc.sbuf_tensor(f"{self.name}_{name}", shape, dt))


def in_order(eng, done):
    count = [0]

    def link(ins):
        count[0] += 1
        ins.then_inc(done, 1)
        eng.wait_ge(done, count[0])

    return link


def project(c, l, pT):
    nc, dram = c.nc, c.dram
    turns = [("xT", t, h) for t in range(TILES) for h in range(2)] + [("proj", b) for b in range(N_IN)]
    with ExitStack() as ctx:
        s = Stage(c, ctx, "project", turns, ["x_in"])
        at, bank, full, free, x_in = s.steps.at, s.bank, s.full, s.free, s.named["x_in"]
        x, hT = s.sb("x", [P, TILES, D]), s.sb("hT", [P, KD, TOK])
        with nc.Block() as block:

            @block.sync
            def _(sp):
                for n in range(AT_IN + SLOTS, AT_OUT + SLOTS):
                    b, r = at("proj", 2 * (n - SLOTS - AT_IN) + 1)
                    sp.wait_ge(full[b], r + 1)
                    fill_slot(c, sp, l, n)

            @block.scalar
            def _(act):
                for t in range(TILES):
                    act.dma_start(x[:, t, :], c.x_dram[t]).then_inc(x_in, 16)
                for n in range(0, N_IN, 2):
                    b, r = at("proj", n)
                    act.wait_ge(full[b], r + 1)
                    nc.scalar.copy(pT[:, n, :], bank[b][:, 0:TOK]).then_inc(free[b], 1)

            @block.vector
            def _(dve):
                modulate(c, s, dve, 0, hT)
                for n in range(1, N_IN, 2):
                    b, r = at("proj", n)
                    dve.wait_ge(full[b], r + 1)
                    nc.vector.tensor_copy(pT[:, n, :], bank[b][:, 0:TOK]).then_inc(free[b], 1)

            @block.tensor
            def _(pe):
                pe.wait_ge(x_in, 16 * TILES)
                transpose_x(c, s, pe, x)
                for t in range(TILES):
                    for h in range(2):
                        b, r = at("xT", t, h)
                        pe.wait_ge(free[b], r + 1)
                for n in range(N_IN):
                    b, r = at("proj", n)
                    m = AT_IN + n // 2
                    pe.wait_ge(c.ring_full[slot(m)], filled(m))
                    pe.wait_ge(free[b], r)
                    w = c.ring[:, slot(m), :].rearrange("p (h k n) -> p h k n", h=2, k=KD)
                    for k in range(KD):
                        ins = nc.tensor.matmul(bank[b][:, 0:TOK], w[:, n % 2, k, :], hT[:, k, :],
                                               start=(k == 0), stop=(k == KD - 1))
                    ins.then_inc(full[b], 1)
        clear(nc, s.sems)


def transpose_x(c, s, pe, x):
    for t in range(TILES):
        for h in range(2):
            b, r = s.steps.at("xT", t, h)
            pe.wait_ge(s.free[b], r)
            for k in range(4):
                f = 4 * h + k
                ins = c.nc.tensor.transpose(s.bank[b][:, k * P:(k + 1) * P], x[:, t, f * P:(f + 1) * P], c.ident[:, :])
            ins.then_inc(s.full[b], 1)


def modulate(c, s, dve, q, hT):
    for t in range(TILES):
        for h in range(2):
            b, r = s.steps.at("xT", t, h)
            dve.wait_ge(s.full[b], r + 1)
            for k in range(4):
                f, seq = 4 * h + k, SEQ_OF_TILE[t]
                ins = c.nc.vector.tensor_scalar(hT[:, f, t * P:(t + 1) * P], s.bank[b][:, k * P:(k + 1) * P],
                                                c.mod_cols[:, 2 * q + 1, f, seq:seq + 1],
                                                c.mod_cols[:, 2 * q, f, seq:seq + 1], ALU.mult, ALU.add)
            ins.then_inc(s.free[b], 1)


def attention(c, l, pT, mixT):
    nc, dram = c.nc, c.dram
    turns = [("rot", b) for b in range(5)] + [("avT",)]
    for t in range(TILES):
        turns += [("score", t, h) for h in range(HEADS)]
        for b in range(4):
            turns += [("probT", t, b, g) for g in range(2)] + [("att", t, b)]
    CONV = ((0, P), (P, TOK))
    with ExitStack() as ctx:
        s = Stage(c, ctx, "att", turns, ["tables_in", "k_out", "k_stored", "vdone", "pdone", "adone", "maxed", "expd",
                                         "sums", "scaled", "att_done", "conv_cols", "sink_exp"])
        at, bank, full, free, S = s.steps.at, s.bank, s.full, s.free, s.named
        cosT, sinT, rotate = s.sb("cosT", [P, 2 * P]), s.sb("sinT", [P, 2 * P]), s.sb("rotate", [P, P])
        mask, sink = s.sb("mask", [P, 2, 3 * P]), s.sb("sink", [P, HEADS])
        conv_w = s.sb("conv_w", [P, 2, 3])
        cacheT, vkey = s.sb("cacheT", [P, P]), s.sb("vkey", [P, 1 + TILES, P])
        turned = s.sb("turned", [P, 5, 2 * P])
        kctx = s.sb("kctx", [P, P])
        prob = s.sb("prob", [P, 2, HEADS, 3 * P])
        probT = s.sb("probT", [P, 4, 3, P])
        row = s.sb("row", [P, TILES, 5, HEADS])
        z, z1 = s.sb("conv_z", [P, 2, TOK]), s.sb("conv_z1", [P, 2, TOK])
        probT_turn = {}
        for t in range(TILES):
            for b in range(4):
                for g in range(2):
                    probT_turn[t, b, g] = len(probT_turn)
        with nc.Block() as block:

            @block.sync
            def _(sp):
                for dst, src in ((cosT, dram["cosT"]), (sinT, dram["sinT"]), (rotate, dram["rotate"])):
                    sp.dma_start(dst[:, :], src).then_inc(S["tables_in"], 16)
                sp.dma_start(mask[:, :, :], dram["att_mask"]).then_inc(S["tables_in"], 16)
                sp.dma_start(sink[:, :], layer_row(dram["sink"], l)).then_inc(S["tables_in"], 16)
                sp.dma_start(conv_w[:, :, :], layer_row(dram["conv_w"], l)).then_inc(S["tables_in"], 16)
                sp.dma_start(cacheT[:, :], layer_row(dram["cache_kT"], l)).then_inc(S["tables_in"], 16)
                sp.dma_start(vkey[:, 0, :], layer_row(dram["cache_v"], l)).then_inc(S["tables_in"], 16)
                sp.dma_start(layer_row(dram["new_k"], l), pT[:, KB, 0:P]).then_inc(S["k_stored"], 16)
                sp.dma_start(layer_row(dram["new_v"], l), pT[:, VB, 0:P]).then_inc(S["k_stored"], 16)
                sp.wait_ge(S["k_stored"], 32)

            @block.gpsimd
            def _(pool):
                link = in_order(pool, S["pdone"])
                pool.wait_ge(S["tables_in"], 16 * 8)
                link(nc.gpsimd.tensor_tensor(z[:, :, :], pT[:, CCB:CCB + 2, :], pT[:, CUB:CUB + 2, :], ALU.mult))
                for g in range(2):
                    link(nc.gpsimd.tensor_scalar(mixT[:, 6 + g, :], z[:, g, :], conv_w[:, g, 1:2], None, ALU.mult))
                for g in range(2):
                    for w, src, dst in ((0, 0, 1), (2, 1, 0)):
                        link(nc.gpsimd.tensor_scalar(z1[:, g, :], z[:, g, :], conv_w[:, g, w:w + 1], None, ALU.mult))
                        for lo, hi in CONV:
                            n = hi - lo - 1
                            out = mixT[:, 6 + g, lo + dst:lo + dst + n]
                            ins = nc.gpsimd.tensor_tensor(out, out, z1[:, g, lo + src:lo + src + n], ALU.add)
                        link(ins)
                    link(nc.gpsimd.tensor_tensor(mixT[:, 6 + g, :], mixT[:, 6 + g, :], pT[:, CBB + g, :], ALU.mult))

            @block.scalar
            def _(act):
                b, r = at("avT")
                act.wait_ge(full[b], r + 1)
                nc.scalar.copy(vkey[:, 1:4, :], bank[b][:, 0:TOK].rearrange("p (t n) -> p t n", t=TILES)).then_inc(free[b], 1)
                for t in range(TILES):
                    nk = 1 if t == 0 else 3
                    act.wait_ge(S["maxed"], t + 1)
                    for h in range(HEADS):
                        nc.scalar.activation(prob[:, t % 2, h, 0:nk * P], prob[:, t % 2, h, 0:nk * P], ACT.Exp,
                                             bias=row[:, t, 1, h:h + 1], accum_out=row[:, t, 2, h:h + 1])
                    nc.scalar.activation(row[:, t, 3, :], row[:, t, 3, :], ACT.Exp).then_inc(S["expd"], 1)
                    for bb in range(4):
                        for g in range(2):
                            b, r = at("probT", t, bb, g)
                            m = probT_turn[t, bb, g]
                            act.wait_ge(full[b], r + 1)
                            if m >= 4:
                                ab, ar = at("att", *[k for k, v in probT_turn.items() if v == m - 4][0][:2])
                                act.wait_ge(full[ab], ar + 1)
                            nc.scalar.copy(probT[:, m % 4, 0:nk, :],
                                           bank[b][:, 0:nk * P].rearrange("p (k n) -> p k n", k=nk)).then_inc(free[b], 1)

            @block.vector
            def _(dve):
                link = in_order(dve, S["vdone"])
                dve.wait_ge(S["tables_in"], 16 * 8)
                dve.wait_ge(S["k_stored"], 32)
                nc.vector.tensor_copy(kctx[:, :], pT[:, KB, 0:P])
                for b5 in range(5):
                    b, r = at("rot", b5)
                    dve.wait_ge(full[b], r + 1)
                    nc.vector.tensor_tensor(turned[:, b5, :], bank[b][:, 0:2 * P], sinT[:, :], ALU.mult).then_inc(free[b], 1)
                    link(nc.vector.tensor_tensor(pT[:, b5, P:TOK], pT[:, b5, P:TOK], cosT[:, :], ALU.mult))
                    ins = nc.vector.tensor_tensor(pT[:, b5, P:TOK], pT[:, b5, P:TOK], turned[:, b5, :], ALU.add)
                ins.then_inc(S["scaled"], 1)
                for t in range(TILES):
                    nk = 1 if t == 0 else 3
                    if t >= 2:
                        b, r = at("att", t - 2, 3)
                        dve.wait_ge(full[b], r + 1)
                    for h in range(HEADS):
                        b, r = at("score", t, h)
                        dve.wait_ge(full[b], r + 1)
                        if t == 0:
                            ins = nc.vector.tensor_scalar(prob[:, 0, h, 0:P], bank[b][:, 0:P], HD ** -0.5, None, ALU.mult)
                        else:
                            ins = nc.vector.scalar_tensor_tensor(prob[:, t % 2, h, :], bank[b][:, 0:3 * P], HD ** -0.5,
                                                                 mask[:, t - 1, :], ALU.mult, ALU.add)
                        ins.then_inc(free[b], 1)
                    for h in range(HEADS):
                        b, r = at("score", t, h)
                        dve.wait_ge(free[b], r + 1)
                    link(nc.vector.tensor_reduce(row[:, t, 0, :], prob[:, t % 2, :, 0:nk * P], AX.X, ALU.max))
                    link(nc.vector.tensor_tensor(row[:, t, 0, :], row[:, t, 0, :], sink[:, :], ALU.max))
                    nc.vector.tensor_scalar(row[:, t, 1, :], row[:, t, 0, :], -1.0, None, ALU.mult)
                    nc.vector.tensor_tensor(row[:, t, 3, :], sink[:, :], row[:, t, 0, :], ALU.subtract).then_inc(S["maxed"], 1)
                    dve.wait_ge(S["expd"], t + 1)
                    link(nc.vector.tensor_tensor(row[:, t, 2, :], row[:, t, 2, :], row[:, t, 3, :], ALU.add))
                    link(nc.vector.reciprocal(row[:, t, 4, :], row[:, t, 2, :]))
                    for h in range(HEADS):
                        ins = nc.vector.tensor_scalar(prob[:, t % 2, h, 0:nk * P], prob[:, t % 2, h, 0:nk * P],
                                                      row[:, t, 4, h:h + 1], None, ALU.mult)
                    ins.then_inc(S["scaled"], 1)
                    for bb in range(4):
                        b, r = at("att", t, bb)
                        dve.wait_ge(full[b], r + 1)
                        nc.vector.tensor_copy(mixT[:, bb, t * P:(t + 1) * P], bank[b][:, 0:P]).then_inc(free[b], 1)

            @block.tensor
            def _(pe):
                pe.wait_ge(S["tables_in"], 16 * 8)
                for b5 in range(5):
                    b, r = at("rot", b5)
                    pe.wait_ge(free[b], r)
                    nc.tensor.matmul(bank[b][:, 0:2 * P], rotate[:, :], pT[:, b5, P:TOK], start=True, stop=True).then_inc(full[b], 1)
                b, r = at("avT")
                pe.wait_ge(free[b], r)
                for t in range(TILES):
                    ins = nc.tensor.transpose(bank[b][:, t * P:(t + 1) * P], pT[:, VB, t * P:(t + 1) * P], c.ident[:, :])
                ins.then_inc(full[b], 1)
                b, r = at("avT")
                pe.wait_ge(free[b], r + 1)
                pe.wait_ge(S["scaled"], 1)
                for t in range(TILES):
                    for h in range(HEADS):
                        b, r = at("score", t, h)
                        pe.wait_ge(free[b], r)
                        rows = slice(HD * (h // 4), HD * (h // 4) + HD)
                        q = pT[rows, h % 4, t * P:(t + 1) * P]
                        if t == 0:
                            ins = nc.tensor.matmul(bank[b][:, 0:P], q, kctx[rows, :], start=True, stop=True)
                        else:
                            nc.tensor.matmul(bank[b][:, 0:P], q, cacheT[rows, :], start=True, stop=True)
                            ins = nc.tensor.matmul(bank[b][:, P:3 * P], q, pT[rows, KB, P:TOK], start=True, stop=True)
                        ins.then_inc(full[b], 1)
                    pe.wait_ge(S["scaled"], t + 2)
                    values = [1] if t == 0 else [0, 2, 3]
                    for bb in range(4):
                        for g in range(2):
                            b, r = at("probT", t, bb, g)
                            pe.wait_ge(free[b], r)
                            for k in range(len(values)):
                                ins = nc.tensor.transpose(bank[b][:, k * P:(k + 1) * P],
                                                          prob[:, t % 2, bb + 4 * g, k * P:(k + 1) * P], c.ident[:, :])
                            ins.then_inc(full[b], 1)
                        ab, ar = at("att", t, bb)
                        pe.wait_ge(free[ab], ar)
                        for g in range(2):
                            b, r = at("probT", t, bb, g)
                            pe.wait_ge(free[b], r + 1)
                            m = probT_turn[t, bb, g]
                            for k, v in enumerate(values):
                                ins = nc.tensor.matmul(bank[ab][HD * g:HD * g + HD, 0:P], vkey[:, v, HD * g:HD * g + HD],
                                                       probT[:, m % 4, k, :], start=(k == 0), stop=(k == len(values) - 1))
                        ins.then_inc(full[ab], 1)
        clear(nc, s.sems)


DECAY = float(np.exp(-0.5))


def rwkv(c, l, pT, mixT):
    nc, dram = c.nc, c.dram
    turns = [("decay", d, g) for d in range(2) for g in range(2)]
    turns += [("rate", d, g) for d in range(2) for g in range(2)]
    turns += [("gate", g) for g in range(2)] + [("kk2", g) for g in range(2)] + [("vT", g) for g in range(2)]
    GH = [(g, hh) for g in range(2) for hh in range(2)]
    GT = [(g, t) for g in range(2) for t in range(TILES)]
    chunks = {}
    for d in range(2):
        for s_, n0, n1 in ((0, 0, 2), (1, 2, 6)):
            chunks[d, s_] = list(range(n0, n1)) if d == 0 else list(range(n1 - 1, n0 - 1, -1))
    scans = [(s_, step) for step in range(4) for s_ in range(2) if (s_ == 1 or step == 1)]
    for d in range(2):
        for g, t in GT:
            turns += [("tokens", d, g, t)] + [("gram", d, g, t, hh) for hh in range(2)]
        turns += [("inv0", d, g, hh) for g, hh in GH]
        for lev in range(1, N_LEVELS):
            turns += [("invY", d, lev, g, hh) for g, hh in GH]
            for g, hh in GH:
                turns += ([("invX", d, lev, g, hh)] if lev < N_LEVELS - 1 else []) + [("invXT", d, lev, g, hh)]
        turns += [(n, d, g, t) for n in ("GW", "H", "EF", "QZ") for g, t in GT]
        turns += [("scan", d, s_, step, g) for s_, step in scans for g in range(2)]
    turns += [(n, g) for n in ("bonus", "mean", "var") for g in range(2)]

    with ExitStack() as ctx:
        s = Stage(c, ctx, "rwkv", turns, ["params_in", "zeroed", "states_in", "squashed", "sigmoids", "kk2_in", "kk_root",
                                          "vdone", "exps_asked", "exps", "chunk_ops", "levelled", "seeded",
                                          "states", "state_out", "sums_in", "centred", "var_root", "adone"])
        at, bank, full, free, S = s.steps.at, s.bank, s.full, s.free, s.named
        cols, one_ka = s.sb("cols", [P, N_COLS]), s.sb("one_ka", [P, 2])
        w_up, g_up = s.sb("w_up", [P, 2 * P]), s.sb("g_up", [HD, 2 * P])
        headones, resets = s.sb("headones", [P, P]), s.sb("resets", [P, 2 * TOK])
        gram_mask, level_mask = s.sb("gram_mask", [P, 2, 4 * P]), s.sb("level_mask", [P, 2, N_LEVELS, P])
        v_tok = s.sb("v_tok", [P, TILES, 2 * P])
        gate, kk, kdsum, y = (s.sb(n, [P, 2, TOK]) for n in ("gate", "kk", "kdsum", "y"))
        Lsum, kd = s.sb("Lsum", [P, 2, TOK]), s.sb("kd", [P, 2, TOK])
        rate1 = s.sb("rate1", [P, 2, TOK])
        AR = s.sb("AR", [P, 2, 2, TOK])
        Bf, Kf = s.sb("Bf", [P, 2, TOK]), s.sb("Kf", [P, 2, TOK])
        decayC = s.sb("decayC", [P, 2, 6])
        A_tok = s.sb("A_tok", [P, 2, TILES, P])
        BK_tok = s.sb("BK_tok", [P, 2, TILES, 2, 2, P])
        M = s.sb("M", [P, 2, 2, TILES, 4, P])
        Ak = s.sb("Ak", [P, 2, 2, TILES, P])
        Dm, DT, Ym = (s.sb(n, [P, 2, 2, TILES, P]) for n in ("Dm", "DT", "Ym"))
        GW, H = s.sb("GW", [P, 2, TILES, 2 * P]), s.sb("H", [P, 2, TILES, P])
        s_init = s.sb("s_init", [P, 2, 2, P])
        t_exc, t_inc, t_inv = pT[:, 0:2, :], pT[:, 2:4, :], pT[:, 4:6, :]
        sig = [pT[:, 14:16, :], pT[:, 16:18, :]]
        rate = [pT[:, 18:20, :], rate1[:, :, :]]
        r_, k_, v_ = pT[:, RB:RB + 2, :], pT[:, RKB:RKB + 2, :], pT[:, RVB:RVB + 2, :]
        ET = s.sb("ET", [P, 2, TILES, 2, P])
        F = Ym[:, :, :, :, :].rearrange("p g h t n -> p (g h t) n")
        QT = Ak[:, :, 0, :, :]
        state = Dm[:, :, :, :, :].rearrange("p g h t n -> p (g h t) n")

        def F_at(g, t, ch):
            return F[:, (g * TILES + t) * 2 + ch, :]

        def state_at(g, s_, step):
            return state[:, g * 6 + (step - 1 if s_ == 0 else 1 + step), :]

        def tile_cols(t):
            return slice(t * P, (t + 1) * P)

        with nc.Block() as block:

            @block.sync
            def _(sp):
                sp.wait_ge(S["zeroed"], 1)
                for d in range(2):
                    for h in range(4):
                        rows = slice(HD * (h % 2), HD * (h % 2) + HD)
                        sp.dma_start(s_init[rows, d, h // 2, rows],
                                     dram["state_T"][bass.ds(l, 1), d, h].rearrange("a p n -> (a p) n")).then_inc(S["states_in"], 16)
                for d in range(2):
                    sp.wait_ge(S["state_out"], 2 * (d + 1))
                    for h in range(4):
                        rows = slice(HD * (h % 2), HD * (h % 2) + HD)
                        sp.dma_start(dram["new_state_T"][bass.ds(l, 1), d, h].rearrange("a p n -> (a p) n"),
                                     state_at(h // 2, 0, 2)[rows, rows]).then_inc(S["states"], 16)
                    sp.wait_ge(S["states"], 64 * (d + 1))

            @block.gpsimd
            def _(pool):
                nc.gpsimd.memset(s_init[:, :, :, :], 0.0).then_inc(S["zeroed"], 1)
                nc.gpsimd.memset(BK_tok[:, :, :, :, :, :], 0.0).then_inc(S["zeroed"], 1)

            @block.scalar
            def _(act):
                for dst, src in ((cols, "cols"), (w_up, "w_up"), (g_up, "g_up")):
                    act.dma_start(dst[:, :], layer_row(dram[src], l)).then_inc(S["params_in"], 16)
                act.dma_start(headones[:, :], dram["headones"]).then_inc(S["params_in"], 16)
                act.dma_start(resets[:, :], dram["resets"]).then_inc(S["params_in"], 16)
                act.dma_start(gram_mask[:, :, :], dram["gram_mask"]).then_inc(S["params_in"], 16)
                act.dma_start(level_mask[:, :, :, :], dram["level_mask"]).then_inc(S["params_in"], 16)
                act.wait_ge(S["params_in"], 16 * 7)
                nc.scalar.activation(pT[0:HD, WAB, :], pT[0:HD, WAB, :], ACT.Tanh).then_inc(S["squashed"], 1)
                nc.scalar.activation(pT[0:HD, GB, :], pT[0:HD, GB, :], ACT.Sigmoid).then_inc(S["squashed"], 1)
                for name, dst, col in (("decay", sig, C_W0), ("rate", rate, C_A0)):
                    for d in range(2):
                        for g in range(2):
                            b, r = at(name, d, g)
                            act.wait_ge(full[b], r + 1)
                            nc.scalar.activation(dst[d][:, g, :], bank[b][:, 0:TOK], ACT.Sigmoid,
                                                 bias=cols[:, col + 2 * d + g:col + 2 * d + g + 1]).then_inc(free[b], 1)
                for g in range(2):
                    b, r = at("gate", g)
                    act.wait_ge(full[b], r + 1)
                    nc.scalar.copy(gate[:, g, :], bank[b][:, 0:TOK]).then_inc(free[b], 1)
                for g in range(2):
                    b, r = at("kk2", g)
                    act.wait_ge(free[b], r + 1)
                nc.scalar.activation(t_exc, t_exc, ACT.Sqrt).then_inc(S["kk_root"], 1)
                for g in range(2):
                    b, r = at("vT", g)
                    act.wait_ge(full[b], r + 1)
                    nc.scalar.copy(v_tok[:, :, g * P:(g + 1) * P],
                                   bank[b][:, 0:TOK].rearrange("p (t n) -> p t n", t=TILES)).then_inc(free[b], 1)
                act.wait_ge(S["zeroed"], 2)
                for d in range(2):
                    act.wait_ge(S["exps_asked"], d + 1)
                    inc = Lsum[:, :, :] if d == 0 else t_inc
                    tot = Lsum[:, :, :].rearrange("p g (k n) -> p g k n", n=CHUNK)[:, :, :, CHUNK - 1]
                    nc.scalar.activation(t_exc, t_exc, ACT.Exp, scale=-DECAY)
                    nc.scalar.activation(t_inv, inc, ACT.Exp, scale=DECAY)
                    nc.scalar.activation(decayC[:, :, :], tot, ACT.Exp, scale=-DECAY).then_inc(S["adone"], 1)
                    act.wait_ge(S["adone"], d + 1)
                    nc.scalar.activation(t_inc, inc, ACT.Exp, scale=-DECAY).then_inc(S["exps"], 1)
                    if d == 1:
                        b, r = at("QZ", 0, 1, 2)
                        act.wait_ge(full[b], r + 1)
                    for g, t in GT:
                        b, r = at("tokens", d, g, t)
                        act.wait_ge(full[b], r + 1)
                        nc.scalar.copy(A_tok[:, g, t, :], bank[b][:, 0:P])
                        for ch in range(2):
                            rows = slice(CHUNK * ch, CHUNK * ch + CHUNK)
                            ins = nc.scalar.copy(BK_tok[rows, g, t, :, ch, :],
                                                 bank[b][rows, P:3 * P].rearrange("p (w n) -> p w n", w=2))
                        ins.then_inc(free[b], 1)
                    for lev in range(1, N_LEVELS):
                        for g, hh in GH:
                            b, r = at("invY", d, lev, g, hh)
                            act.wait_ge(full[b], r + 1)
                            nc.scalar.copy(Ym[:, g, hh, :, :], bank[b][:, 0:TOK].rearrange("p (t n) -> p t n", t=TILES)).then_inc(free[b], 1)
                    for g, t in GT:
                        b, r = at("GW", d, g, t)
                        act.wait_ge(full[b], r + 1)
                        nc.scalar.copy(GW[:, g, t, :], bank[b][:, 0:2 * P]).then_inc(free[b], 1)
                    for g, t in GT:
                        b, r = at("H", d, g, t)
                        act.wait_ge(full[b], r + 1)
                        nc.scalar.copy(H[:, g, t, :], bank[b][:, 0:P]).then_inc(free[b], 1)
                for g in range(2):
                    b, r = at("var", g)
                    act.wait_ge(free[b], r + 1)
                nc.scalar.activation(t_exc, t_exc, ACT.Sqrt).then_inc(S["var_root"], 1)

            @block.vector
            def _(dve):
                link = in_order(dve, S["vdone"])
                dve.wait_ge(S["params_in"], 16 * 7)
                link(nc.vector.tensor_scalar(one_ka[:, :], cols[:, C_KA:C_KA + 2], -1.0, 1.0, ALU.mult, ALU.add))
                for g in range(2):
                    ins = nc.vector.tensor_scalar(kk[:, g, :], k_[:, g, :], cols[:, C_KK + g:C_KK + g + 1], None, ALU.mult)
                link(ins)
                nc.vector.tensor_tensor(t_inc, kk[:, :, :], kk[:, :, :], ALU.mult).then_inc(S["kk2_in"], 1)
                for g in range(2):
                    b, r = at("kk2", g)
                    dve.wait_ge(full[b], r + 1)
                    nc.vector.tensor_scalar(t_exc[:, g, :], bank[b][:, 0:TOK], 1e-24, None, ALU.max).then_inc(free[b], 1)
                dve.wait_ge(S["kk_root"], 1)
                link(nc.vector.reciprocal(t_exc, t_exc))
                link(nc.vector.tensor_tensor(kk[:, :, :], kk[:, :, :], t_exc, ALU.mult))
                for d in range(2):
                    for name in ("decay", "rate"):
                        for g in range(2):
                            b, r = at(name, d, g)
                            dve.wait_ge(free[b], r + 1)
                    flat = lambda ap: ap.rearrange("p g n -> p (g n)")
                    link(nc.vector.tensor_tensor_scan(flat(Lsum[:, :, :]), resets[:, :], flat(sig[d]), 0.0, ALU.mult, ALU.add))
                    if d == 0:
                        nc.vector.tensor_tensor(t_exc, Lsum[:, :, :], sig[d], ALU.subtract).then_inc(S["exps_asked"], 1)
                    else:
                        by_chunk = flat(Lsum[:, :, :]).rearrange("p (k n) -> p k n", n=CHUNK)
                        tot = by_chunk[:, :, CHUNK - 1:CHUNK].to_broadcast([P, 2 * TOK // CHUNK, CHUNK])
                        link(nc.vector.tensor_tensor(flat(t_exc).rearrange("p (k n) -> p k n", n=CHUNK), tot, by_chunk, ALU.subtract))
                        nc.vector.tensor_tensor(t_inc, t_exc, sig[d], ALU.add).then_inc(S["exps_asked"], 1)
                    for g in range(2):
                        ins = nc.vector.tensor_scalar(kd[:, g, :], rate[d][:, g, :], cols[:, C_KA + g:C_KA + g + 1],
                                                      one_ka[:, g:g + 1], ALU.mult, ALU.add)
                    link(ins)
                    link(nc.vector.tensor_tensor(kd[:, :, :], kd[:, :, :], k_, ALU.mult))
                    if d == 0:
                        nc.vector.tensor_copy(kdsum[:, :, :], kd[:, :, :])
                    else:
                        nc.vector.tensor_tensor(kdsum[:, :, :], kdsum[:, :, :], kd[:, :, :], ALU.add)
                    link(nc.vector.tensor_tensor(rate[d], rate[d], kk[:, :, :], ALU.mult))
                    dve.wait_ge(S["exps"], d + 1)
                    nc.vector.scalar_tensor_tensor(AR[:, :, 0, :], kk[:, :, :], -1.0, t_exc, ALU.mult, ALU.mult)
                    nc.vector.tensor_tensor(AR[:, :, 1, :], r_, t_inc, ALU.mult)
                    nc.vector.tensor_tensor(Bf[:, :, :], rate[d], t_inv, ALU.mult)
                    nc.vector.tensor_tensor(Kf[:, :, :], kd[:, :, :], t_inv, ALU.mult).then_inc(S["chunk_ops"], 1)
                    for g, t in GT:
                        for hh in range(2):
                            b, r = at("gram", d, g, t, hh)
                            dve.wait_ge(full[b], r + 1)
                            nc.vector.tensor_tensor(M[:, g, hh, t, :, :].rearrange("p q n -> p (q n)"), bank[b][:, :],
                                                    gram_mask[:, d, :], ALU.mult).then_inc(free[b], 1)
                    for g, t in GT:
                        b, r = at("gram", d, g, t, 1)
                        dve.wait_ge(free[b], r + 1)

                    def level(lev, g, hh):
                        lm = level_mask[:, d, lev, :].unsqueeze(1).to_broadcast([P, TILES, P])
                        return nc.vector.tensor_tensor(Ak[:, g, hh, :, :], M[:, g, hh, :, 0, :], lm, ALU.mult).then_inc(S["levelled"], 1)

                    def levels_done(lev):
                        return 4 * (d * N_LEVELS + lev + 1)

                    eye = c.ident[:, :].unsqueeze(1).to_broadcast([P, TILES, P])
                    for g, hh in GH:
                        level(0, g, hh)
                    dve.wait_ge(S["levelled"], levels_done(0))
                    for g, hh in GH:
                        b, r = at("inv0", d, g, hh)
                        dve.wait_ge(full[b], r + 1)
                        nc.vector.tensor_tensor(DT[:, g, hh, :, :], Ak[:, g, hh, :, :], eye, ALU.add)
                        nc.vector.tensor_tensor(Dm[:, g, hh, :, :], bank[b][:, 0:TOK].rearrange("p (t n) -> p t n", t=TILES),
                                                eye, ALU.add).then_inc(free[b], 1)
                    for g, hh in GH:
                        b, r = at("inv0", d, g, hh)
                        dve.wait_ge(free[b], r + 1)
                        level(1, g, hh)
                    for lev in range(1, N_LEVELS):
                        for g, hh in GH:
                            for name, dst in (("invX", Dm), ("invXT", DT)):
                                if name == "invX" and lev == N_LEVELS - 1:
                                    continue
                                b, r = at(name, d, lev, g, hh)
                                dve.wait_ge(full[b], r + 1)
                                nc.vector.tensor_tensor(dst[:, g, hh, :, :], dst[:, g, hh, :, :],
                                                        bank[b][:, 0:TOK].rearrange("p (t n) -> p t n", t=TILES),
                                                        ALU.add).then_inc(free[b], 1)
                            if lev < N_LEVELS - 1:
                                level(lev + 1, g, hh)
                    for g, t in GT:
                        b, r = at("EF", d, g, t)
                        dve.wait_ge(full[b], r + 1)
                        ones2 = headones[:, :].unsqueeze(1).to_broadcast([P, 2, P])
                        eye2 = c.ident[:, :].unsqueeze(1).to_broadcast([P, 2, P])
                        link(nc.vector.tensor_tensor(ET[:, g, t, :, :], bank[b][:, 0:2 * P].rearrange("p (c n) -> p c n", c=2),
                                                     ones2, ALU.mult))
                        nc.vector.tensor_tensor(ET[:, g, t, :, :], ET[:, g, t, :, :], eye2, ALU.add)
                        for ch in range(2):
                            ins = nc.vector.scalar_tensor_tensor(F_at(g, t, ch), bank[b][:, (2 + ch) * P:(3 + ch) * P],
                                                                 decayC[:, g, 2 * t + ch:2 * t + ch + 1], headones[:, :],
                                                                 ALU.mult, ALU.mult)
                        ins.then_inc(free[b], 1)
                    for g, t in GT:
                        b, r = at("QZ", d, g, t)
                        dve.wait_ge(full[b], r + 1)
                        nc.vector.tensor_tensor(QT[:, g, t, :], bank[b][:, 0:P], AR[:, g, 1, tile_cols(t)], ALU.add)
                        if d == 0:
                            ins = nc.vector.tensor_copy(y[:, g, tile_cols(t)], bank[b][:, P:2 * P])
                        else:
                            ins = nc.vector.tensor_tensor(y[:, g, tile_cols(t)], y[:, g, tile_cols(t)], bank[b][:, P:2 * P], ALU.add)
                        ins.then_inc(free[b], 1)
                    for g in range(2):
                        t0, ch0 = divmod(chunks[d, 0][0], 2)
                        dve.wait_ge(free[at("EF", d, g, t0)[0]], at("EF", d, g, t0)[1] + 1)
                        nc.vector.tensor_copy(state_at(g, 0, 1), F_at(g, t0, ch0)).then_inc(S["seeded"], 1)
                    for g, t in GT:
                        b, r = at("QZ", d, g, t)
                        dve.wait_ge(free[b], r + 1)
                    for s_, step in scans:
                        chunk = chunks[d, s_][step]
                        t, ch = divmod(chunk, 2)
                        for g in range(2):
                            b, r = at("scan", d, s_, step, g)
                            dve.wait_ge(full[b], r + 1)
                            ycols = slice(chunk * CHUNK, (chunk + 1) * CHUNK)
                            ins = None
                            if step < len(chunks[d, s_]) - 1 or s_ == 0:
                                ins = nc.vector.scalar_tensor_tensor(state_at(g, s_, step + 1), bank[b][:, CHUNK:CHUNK + P],
                                                                     decayC[:, g, chunk:chunk + 1], F_at(g, t, ch), ALU.mult, ALU.add)
                            if s_ == 0:
                                ins.then_inc(S["state_out"], 1)
                            nc.vector.tensor_tensor(y[:, g, ycols], y[:, g, ycols], bank[b][:, 0:CHUNK], ALU.add).then_inc(free[b], 1)
                    for g in range(2):
                        b, r = at("scan", d, 1, 3, g)
                        dve.wait_ge(free[b], r + 1)
                    if d == 0:
                        dve.wait_ge(S["states"], 64)
                for g in range(2):
                    ins = nc.vector.scalar_tensor_tensor(t_inc[:, g, :], kdsum[:, g, :], cols[:, C_RK + g:C_RK + g + 1],
                                                         r_[:, g, :], ALU.mult, ALU.mult)
                ins.then_inc(S["sums_in"], 1)
                for g in range(2):
                    b, r = at("bonus", g)
                    dve.wait_ge(full[b], r + 1)
                    nc.vector.tensor_tensor(t_inv[:, g, :], bank[b][:, 0:TOK], v_[:, g, :], ALU.mult).then_inc(free[b], 1)
                for g in range(2):
                    b, r = at("mean", g)
                    dve.wait_ge(full[b], r + 1)
                    nc.vector.scalar_tensor_tensor(y[:, g, :], bank[b][:, 0:TOK], -1.0 / HD, y[:, g, :], ALU.mult, ALU.add).then_inc(free[b], 1)
                for g in range(2):
                    b, r = at("mean", g)
                    dve.wait_ge(free[b], r + 1)
                nc.vector.tensor_tensor(t_inc, y[:, :, :], y[:, :, :], ALU.mult).then_inc(S["centred"], 1)
                for g in range(2):
                    b, r = at("var", g)
                    dve.wait_ge(full[b], r + 1)
                    ins = nc.vector.tensor_scalar(t_exc[:, g, :], bank[b][:, 0:TOK], 1.0 / HD, LNX_EPS, ALU.mult, ALU.add)
                    ins.then_inc(free[b], 1)
                dve.wait_ge(S["var_root"], 1)
                link(nc.vector.reciprocal(t_exc, t_exc))
                link(nc.vector.tensor_tensor(y[:, :, :], y[:, :, :], t_exc, ALU.mult))
                for g in range(2):
                    ins = nc.vector.tensor_scalar(y[:, g, :], y[:, g, :], cols[:, C_LG + g:C_LG + g + 1],
                                                  cols[:, C_LB + g:C_LB + g + 1], ALU.mult, ALU.add)
                link(ins)
                link(nc.vector.tensor_tensor(y[:, :, :], y[:, :, :], t_inv, ALU.add))
                for g in range(2):
                    b, r = at("gate", g)
                    dve.wait_ge(free[b], r + 1)
                nc.vector.tensor_tensor(mixT[:, 4:6, :], y[:, :, :], gate[:, :, :], ALU.mult)

            @block.tensor
            def _(pe):
                mm, tr = nc.tensor.matmul, nc.tensor.transpose
                pe.wait_ge(S["params_in"], 16 * 7)
                pe.wait_ge(S["squashed"], 2)
                for name, base in (("decay", 0), ("rate", 2 * RANK)):
                    for d in range(2):
                        rows = slice(base + RANK * d, base + RANK * d + RANK)
                        for g in range(2):
                            b, r = at(name, d, g)
                            pe.wait_ge(free[b], r)
                            mm(bank[b][:, 0:TOK], w_up[rows, g * P:(g + 1) * P], pT[rows, WAB, :], start=True, stop=True).then_inc(full[b], 1)
                for g in range(2):
                    b, r = at("gate", g)
                    pe.wait_ge(free[b], r)
                    mm(bank[b][:, 0:TOK], g_up[:, g * P:(g + 1) * P], pT[0:HD, GB, :], start=True, stop=True).then_inc(full[b], 1)
                pe.wait_ge(S["kk2_in"], 1)
                for g in range(2):
                    b, r = at("kk2", g)
                    pe.wait_ge(free[b], r)
                    mm(bank[b][:, 0:TOK], headones[:, :], t_inc[:, g, :], start=True, stop=True).then_inc(full[b], 1)
                for g in range(2):
                    b, r = at("vT", g)
                    pe.wait_ge(free[b], r)
                    for t in range(TILES):
                        ins = tr(bank[b][:, tile_cols(t)], v_[:, g, tile_cols(t)], c.ident[:, :])
                    ins.then_inc(full[b], 1)
                for g in range(2):
                    pe.wait_ge(free[at("vT", g)[0]], at("vT", g)[1] + 1)
                for d in range(2):
                    pe.wait_ge(S["chunk_ops"], d + 1)
                    for g, t in GT:
                        b, r = at("tokens", d, g, t)
                        pe.wait_ge(free[b], r)
                        for i, src in enumerate((AR[:, g, 0, tile_cols(t)], Bf[:, g, tile_cols(t)], Kf[:, g, tile_cols(t)])):
                            ins = tr(bank[b][:, tile_cols(i)], src, c.ident[:, :])
                        ins.then_inc(full[b], 1)
                        for hh in range(2):
                            b, r = at("gram", d, g, t, hh)
                            pe.wait_ge(free[b], r)
                            rows = slice(HD * hh, HD * hh + HD)
                            for i, src in enumerate((Bf, Kf)):
                                ins = mm(bank[b][:, 2 * i * P:2 * (i + 1) * P].rearrange("p (w n) -> p w n", w=2),
                                         src[rows, g, tile_cols(t)], AR[rows, g, :, tile_cols(t)], start=True, stop=True)
                            ins.then_inc(full[b], 1)
                    lv = lambda lev, g, hh: 4 * (d * N_LEVELS + lev) + 2 * g + hh + 1
                    for g, hh in GH:
                        b, r = at("inv0", d, g, hh)
                        pe.wait_ge(S["levelled"], lv(0, g, hh))
                        pe.wait_ge(free[b], r)
                        for t in range(TILES):
                            ins = tr(bank[b][:, tile_cols(t)], Ak[:, g, hh, t, :], c.ident[:, :])
                        ins.then_inc(full[b], 1)
                    for lev in range(1, N_LEVELS):
                        for g, hh in GH:
                            b, r = at("invY", d, lev, g, hh)
                            pe.wait_ge(S["levelled"], lv(lev, g, hh))
                            pe.wait_ge(free[b], r)
                            for t in range(TILES):
                                ins = mm(bank[b][:, tile_cols(t)], Ak[:, g, hh, t, :], Dm[:, g, hh, t, :], start=True, stop=True)
                            ins.then_inc(full[b], 1)
                        for g, hh in GH:
                            yb, yr = at("invY", d, lev, g, hh)
                            pe.wait_ge(free[yb], yr + 1)
                            for name in ("invX", "invXT"):
                                if name == "invX" and lev == N_LEVELS - 1:
                                    continue
                                b, r = at(name, d, lev, g, hh)
                                pe.wait_ge(free[b], r)
                                for t in range(TILES):
                                    Yt, Dt = Ym[:, g, hh, t, :], DT[:, g, hh, t, :]
                                    ins = mm(bank[b][:, tile_cols(t)], *((Dt, Yt) if name == "invX" else (Yt, Dt)), start=True, stop=True)
                                ins.then_inc(full[b], 1)
                    for g, hh in GH:
                        b, r = at("invXT", d, N_LEVELS - 1, g, hh)
                        pe.wait_ge(free[b], r + 1)
                    for g, t in GT:
                        b, r = at("tokens", d, g, t)
                        pe.wait_ge(free[b], r + 1)
                        b, r = at("GW", d, g, t)
                        pe.wait_ge(free[b], r)
                        for hh in range(2):
                            h0 = HD * hh
                            mm(bank[b][:, h0:h0 + HD], DT[:, g, hh, t, :], A_tok[:, g, t, h0:h0 + HD], start=True, stop=True)
                            ins = mm(bank[b][:, P + h0:P + h0 + HD], M[:, g, hh, t, 2, :], v_tok[:, t, g * P + h0:g * P + h0 + HD],
                                     start=True, stop=True)
                        ins.then_inc(full[b], 1)
                    for g, t in GT:
                        b, r = at("GW", d, g, t)
                        pe.wait_ge(free[b], r + 1)
                        b, r = at("H", d, g, t)
                        pe.wait_ge(free[b], r)
                        for hh in range(2):
                            h0 = HD * hh
                            ins = mm(bank[b][:, h0:h0 + HD], DT[:, g, hh, t, :], GW[:, g, t, P + h0:P + h0 + HD], start=True, stop=True)
                        ins.then_inc(full[b], 1)
                    for g, t in GT:
                        b, r = at("H", d, g, t)
                        pe.wait_ge(free[b], r + 1)
                        b, r = at("EF", d, g, t)
                        pe.wait_ge(free[b], r)
                        mm(bank[b][:, 0:2 * P], GW[:, g, t, 0:P], BK_tok[:, g, t, 0, :, :].rearrange("p c n -> p (c n)"), start=True, stop=True)
                        for ch in range(2):
                            out = bank[b][:, (2 + ch) * P:(3 + ch) * P]
                            mm(out, BK_tok[:, g, t, 0, ch, :], H[:, g, t, :], start=True, stop=False)
                            ins = mm(out, BK_tok[:, g, t, 1, ch, :], v_tok[:, t, g * P:(g + 1) * P], start=False, stop=True)
                        ins.then_inc(full[b], 1)
                    for g, t in GT:
                        b, r = at("QZ", d, g, t)
                        pe.wait_ge(free[b], r)
                        for hh in range(2):
                            rows = slice(HD * hh, HD * hh + HD)
                            mm(bank[b][rows, 0:P], GW[:, g, t, rows], M[:, g, hh, t, 1, :], start=True, stop=True)
                        for hh in range(2):
                            rows = slice(HD * hh, HD * hh + HD)
                            mm(bank[b][rows, P:2 * P], H[:, g, t, rows], M[:, g, hh, t, 1, :], start=True, stop=False)
                            ins = mm(bank[b][rows, P:2 * P], v_tok[:, t, g * P + HD * hh:g * P + HD * hh + HD],
                                     M[:, g, hh, t, 3, :], start=False, stop=True)
                        ins.then_inc(full[b], 1)
                    pe.wait_ge(S["states_in"], 16 * 8)
                    pe.wait_ge(S["seeded"], 2 * (d + 1))
                    for g, t in GT:
                        b, r = at("QZ", d, g, t)
                        pe.wait_ge(free[b], r + 1)
                    for s_, step in scans:
                        chunk = chunks[d, s_][step]
                        t, ch = divmod(chunk, 2)
                        for g in range(2):
                            if step > 0 and (s_, step) != (0, 1):
                                pb, pr = at("scan", d, s_, step - 1, g)
                                pe.wait_ge(free[pb], pr + 1)
                            S_in = s_init[:, d, g, :] if step == 0 else state_at(g, s_, step)
                            b, r = at("scan", d, s_, step, g)
                            pe.wait_ge(free[b], r)
                            ins = mm(bank[b][:, 0:CHUNK], S_in, QT[:, g, t, ch * CHUNK:(ch + 1) * CHUNK], start=True, stop=True)
                            if step < len(chunks[d, s_]) - 1 or s_ == 0:
                                ins = mm(bank[b][:, CHUNK:CHUNK + P], ET[:, g, t, ch, :], S_in, start=True, stop=True)
                            ins.then_inc(full[b], 1)
                pe.wait_ge(S["sums_in"], 1)
                for name, src in (("bonus", t_inc), ("mean", y), ("var", t_inc)):
                    if name == "var":
                        pe.wait_ge(S["centred"], 1)
                    for g in range(2):
                        b, r = at(name, g)
                        pe.wait_ge(free[b], r)
                        mm(bank[b][:, 0:TOK], headones[:, :], src[:, g, :], start=True, stop=True).then_inc(full[b], 1)
        clear(nc, s.sems)


def output(c, l, mixT):
    nc, dram = c.nc, c.dram
    turns = [("out", n, t) for n in range(N_POUT) for t in range(TILES)]
    NW = PIECE // KD
    with ExitStack() as ctx:
        s = Stage(c, ctx, "output", turns, ["x_in", "vdone", "var_ready", "std_ready", "normed", "stored"])
        at, bank, full, free, S = s.steps.at, s.bank, s.full, s.free, s.named
        x, part, gates, gb = s.sb("x", [P, TILES, D]), s.sb("part", [P, TILES, D]), s.sb("gates", [P, 2, D]), s.sb("gb", [P, 2, D])
        stats, mv, rstd = s.sb("stats", [P, TILES, 12]), s.sb("mv", [P, TILES, 2]), s.sb("rstd", [P, TILES])
        with nc.Block() as block:

            @block.sync
            def _(sp):
                for n in range(AT_OUT + SLOTS, AT_Q + SLOTS):
                    b, r = at("out", n - SLOTS - AT_OUT, TILES - 1)
                    sp.wait_ge(full[b], r + 1)
                    fill_slot(c, sp, l, n)

            @block.scalar
            def _(act):
                load_for_norm(c, l, act, S["x_in"], x, gates, 0, gb, "ln1")
                for t in range(TILES):
                    act.wait_ge(S["var_ready"], t + 1)
                    nc.scalar.activation(rstd[:, t:t + 1], mv[:, t, 1:2], ACT.Sqrt).then_inc(S["std_ready"], 1)
                for t in range(TILES):
                    act.wait_ge(S["normed"], t + 1)
                    act.dma_start(c.x_dram[t], x[:, t, :]).then_inc(S["stored"], 16)
                act.wait_ge(S["stored"], 16 * TILES)

            @block.vector
            def _(dve):
                link = in_order(dve, S["vdone"])
                dve.wait_ge(S["x_in"], 16 * LOADS_FOR_NORM)
                for n in range(N_POUT):
                    for t in range(TILES):
                        b, r = at("out", n, t)
                        cols = slice(n * NW, (n + 1) * NW)
                        dve.wait_ge(full[b], r + 1)
                        nc.vector.tensor_tensor(part[:, t, cols], bank[b][:, 0:NW], gates[:, SEQ_OF_TILE[t], cols], ALU.mult).then_inc(free[b], 1)
                for n in range(N_POUT - 3, N_POUT):
                    for t in range(TILES):
                        b, r = at("out", n, t)
                        dve.wait_ge(free[b], r + 1)
                for t in range(TILES):
                    link(nc.vector.scalar_tensor_tensor(x[:, t, :], x[:, t, :], ALPHA, part[:, t, :], ALU.mult, ALU.add))
                    norm_steps(nc, dve, link, x[:, t, :], stats[:, t, :], mv[:, t, :], rstd[:, t:t + 1], S["var_ready"],
                               S["std_ready"], t + 1, gb[:, 0, :], gb[:, 1, :], x[:, t, :]).then_inc(S["normed"], 1)

            @block.tensor
            def _(pe):
                for n in range(N_POUT):
                    m = AT_OUT + n
                    pe.wait_ge(c.ring_full[slot(m)], filled(m))
                    w = c.ring[:, slot(m), :].rearrange("p (k n) -> p k n", k=KD)
                    for t in range(TILES):
                        b, r = at("out", n, t)
                        pe.wait_ge(free[b], r)
                        for k in range(KD):
                            ins = nc.tensor.matmul(bank[b][:, 0:NW], mixT[:, k, t * P:(t + 1) * P], w[:, k, :],
                                                   start=(k == 0), stop=(k == KD - 1))
                        ins.then_inc(full[b], 1)
        clear(nc, s.sems)


LOADS_FOR_NORM = TILES + 4


def load_for_norm(c, l, eng, loaded, x, gates, which, gb, name):
    for t in range(TILES):
        eng.dma_start(x[:, t, :], c.x_dram[t]).then_inc(loaded, 16)
    for i in range(2):
        eng.dma_start(gates[:, i, :], c.gate_dram[which, i].partition_broadcast(P)).then_inc(loaded, 16)
    for i in range(2):
        eng.dma_start(gb[:, i, :], layer_row(c.dram[name], l)[i].partition_broadcast(P)).then_inc(loaded, 16)


def routing(c, l, xs, route):
    nc, dram = c.nc, c.dram
    HP = 2 * PH
    turns = [("xT", t, h) for t in range(TILES) for h in range(2)] + [("q", n) for n in range(HP)]
    turns += [("sc", t, n) for t in range(TILES) for n in range(HP // 4)] + [("route", t) for t in range(TILES)]
    with ExitStack() as ctx:
        s = Stage(c, ctx, "route", turns, ["x_in", "keys_in", "vdone", "normed", "exp_asked", "exps", "routed", "split"])
        at, bank, full, free, S = s.steps.at, s.bank, s.full, s.free, s.named
        x, hT = s.sb("x", [P, TILES, D]), s.sb("hT", [P, KD, TOK])
        qT, keys, sc = s.sb("qT", [P, HP, TOK]), s.sb("keys", [P, HP, NK]), s.sb("sc", [P, HP, TILES, NK])
        top, idx, idxf = s.sb("top", [P, HP, TOPK]), s.sb("idx", [P, HP, TOPK], U32), s.sb("idxf", [P, HP, TOPK])
        cand = s.sb("cand", [P, PH, TOPK * TOPK])
        best, pos = s.sb("best", [P, PH, TOPK]), s.sb("pos", [P, PH, TOPK], U32)
        half, halff = s.sb("half", [P, 2, PH * TOPK], U32), s.sb("halff", [P, 2, PH * TOPK])
        iota16 = s.sb("iota16", [P, TOPK])
        pick = s.sb("pick", [P, PH * TOPK, TOPK])
        chosen = s.sb("chosen", [P, 3, PH * TOPK])
        rows = s.sb("rows", [P, 2, PH])
        rest = s.sb("rest", [P, TOK])
        gT = s.sb("gT", [P, TOK])
        with nc.Block() as block:

            @block.sync
            def _(sp):
                for n in range(AT_Q + SLOTS, AT_EXP + SLOTS):
                    b, r = at("q", 2 * (n - SLOTS - AT_Q) + 1)
                    sp.wait_ge(full[b], r + 1)
                    fill_slot(c, sp, l, n)

            @block.scalar
            def _(act):
                for t in range(TILES):
                    act.dma_start(x[:, t, :], c.x_dram[t]).then_inc(S["x_in"], 16)
                act.dma_start(keys[:, :, :], layer_row(dram["subkeys_T"], l)).then_inc(S["keys_in"], 16)
                act.dma_start(iota16[:, :], dram["iota16"]).then_inc(S["keys_in"], 16)
                for n in range(HP):
                    b, r = at("q", n)
                    act.wait_ge(full[b], r + 1)
                    nc.scalar.copy(qT[:, n, :], bank[b][:, 0:TOK]).then_inc(free[b], 1)
                for t in range(TILES):
                    for n in range(HP // 4):
                        b, r = at("sc", t, n)
                        act.wait_ge(full[b], r + 1)
                        nc.scalar.copy(sc[:, 4 * n:4 * n + 4, t, :], bank[b][:, :].rearrange("p (h n) -> p h n", h=4)).then_inc(free[b], 1)
                for t in range(TILES):
                    act.wait_ge(S["exp_asked"], t + 1)
                    nc.scalar.activation(chosen[:, 2, :], chosen[:, 2, :], ACT.Exp).then_inc(S["exps"], 1)

            @block.vector
            def _(dve):
                link = in_order(dve, S["vdone"])
                V = nc.vector
                modulate(c, s, dve, 1, hT)
                for t in range(TILES):
                    for h in range(2):
                        b, r = at("xT", t, h)
                        dve.wait_ge(free[b], r + 1)
                link(V.tensor_copy(xs[:, 0, :, :], hT[:, :, :]))
                V.tensor_tensor(xs[:, 1, :, :], hT[:, :, :], xs[:, 0, :, :].bitcast(F32), ALU.subtract)
                dve.wait_ge(S["keys_in"], 32)
                for t in range(TILES):
                    for n in range(HP // 4):
                        b, r = at("sc", t, n)
                        dve.wait_ge(free[b], r + 1)
                    for r8 in range(2):
                        part = slice(8 * r8, 8 * r8 + 8)
                        for n in range(HP):
                            ins = V.max(top[:, n, part], sc[:, n, t, :])
                        link(ins)
                        for n in range(HP):
                            ins = V.max_index(idx[:, n, part], top[:, n, part], sc[:, n, t, :])
                        if r8 == 0:
                            for n in range(HP):
                                ins = V.match_replace(sc[:, n, t, :], top[:, n, part], sc[:, n, t, :], NEG)
                        link(ins)
                    V.tensor_copy(idxf[:, :, :], idx[:, :, :])
                    tops = top[:, :, :].rearrange("p (h two) k -> p h two k", two=2)
                    for h in range(PH):
                        first = top[:, 2 * h, :].unsqueeze(2).to_broadcast([P, TOPK, TOPK])
                        second = top[:, 2 * h + 1, :].unsqueeze(1).to_broadcast([P, TOPK, TOPK])
                        ins = V.tensor_tensor(cand[:, h, :].rearrange("p (a b) -> p a b", a=TOPK), first, second, ALU.add)
                    link(ins)
                    for r8 in range(2):
                        part = slice(8 * r8, 8 * r8 + 8)
                        for h in range(PH):
                            ins = V.max(best[:, h, part], cand[:, h, :])
                        link(ins)
                        for h in range(PH):
                            ins = V.max_index(pos[:, h, part], best[:, h, part], cand[:, h, :])
                        if r8 == 0:
                            for h in range(PH):
                                ins = V.match_replace(cand[:, h, :], best[:, h, part], cand[:, h, :], NEG)
                        link(ins)
                    flat = pos[:, :, :].rearrange("p h k -> p (h k)")
                    V.tensor_scalar(half[:, 0, :], flat, 4, None, ALU.logical_shift_right)
                    link(V.tensor_scalar(half[:, 1, :], flat, TOPK - 1, None, ALU.bitwise_and))
                    if t > 0:
                        b, r = at("route", t - 1)
                        dve.wait_ge(full[b], r + 1)
                    link(V.tensor_copy(halff[:, :, :], half[:, :, :]))
                    for w in range(2):
                        place = halff[:, w, :].unsqueeze(2).to_broadcast([P, PH * TOPK, TOPK])
                        numbers = iota16[:, :].unsqueeze(1).to_broadcast([P, PH * TOPK, TOPK])
                        link(V.tensor_tensor(pick[:, :, :], place, numbers, ALU.is_equal))
                        for h in range(PH):
                            mine = pick[:, h * TOPK:(h + 1) * TOPK, :]
                            table = idxf[:, 2 * h + w, :].unsqueeze(1).to_broadcast([P, TOPK, TOPK])
                            ins = V.tensor_tensor(mine, mine, table, ALU.mult)
                        link(ins)
                        link(V.tensor_reduce(chosen[:, w, :], pick[:, :, :], AX.X, ALU.add))
                    c3 = chosen[:, 2, :].rearrange("p (h k) -> p h k", h=PH)
                    V.tensor_tensor(c3, best[:, :, :], best[:, :, 0:1].to_broadcast([P, PH, TOPK]),
                                    ALU.subtract).then_inc(S["exp_asked"], 1)
                    dve.wait_ge(S["exps"], t + 1)
                    link(V.tensor_reduce(rows[:, 0, :], c3, AX.X, ALU.add))
                    link(V.reciprocal(rows[:, 1, :], rows[:, 0, :]))
                    V.tensor_tensor(c3, c3, rows[:, 1, :].unsqueeze(2).to_broadcast([P, PH, TOPK]), ALU.mult).then_inc(S["routed"], 1)
                for t in range(TILES):
                    b, r = at("route", t)
                    dve.wait_ge(full[b], r + 1)
                    cols = slice(t * P, (t + 1) * P)
                    V.tensor_copy(route[:, 0:2, cols], bank[b][:, 0:2 * P].rearrange("p (w n) -> p w n", w=2))
                    link(V.tensor_copy(gT[:, cols], bank[b][:, 2 * P:3 * P]))
                link(V.tensor_copy(route[:, 2, :], gT[:, :]))
                link(V.tensor_tensor(rest[:, :], gT[:, :], route[:, 2, :], ALU.subtract))
                link(V.tensor_copy(route[:, 3, :], rest[:, :]))
                V.tensor_tensor(route[:, 4, :], rest[:, :], route[:, 3, :], ALU.subtract)

            @block.tensor
            def _(pe):
                pe.wait_ge(S["x_in"], 16 * TILES)
                transpose_x(c, s, pe, x)
                for t in range(TILES):
                    for h in range(2):
                        b, r = at("xT", t, h)
                        pe.wait_ge(free[b], r + 1)
                for n in range(HP):
                    b, r = at("q", n)
                    m = AT_Q + n // 2
                    pe.wait_ge(c.ring_full[slot(m)], filled(m))
                    pe.wait_ge(free[b], r)
                    w = c.ring[:, slot(m), :].rearrange("p (h k n) -> p h k n", h=2, k=KD)
                    for k in range(KD):
                        ins = nc.tensor.matmul(bank[b][:, 0:TOK], w[:, n % 2, k, :], hT[:, k, :],
                                               start=(k == 0), stop=(k == KD - 1))
                    ins.then_inc(full[b], 1)
                pe.wait_ge(S["keys_in"], 32)
                for n in range(HP):
                    b, r = at("q", n)
                    pe.wait_ge(free[b], r + 1)
                for t in range(TILES):
                    for n in range(HP // 4):
                        b, r = at("sc", t, n)
                        pe.wait_ge(free[b], r)
                        for i in range(4):
                            ins = nc.tensor.matmul(bank[b][:, i * P:(i + 1) * P], qT[:, 4 * n + i, t * P:(t + 1) * P],
                                                   keys[:, 4 * n + i, :], start=True, stop=True)
                        ins.then_inc(full[b], 1)
                for t in range(TILES):
                    b, r = at("route", t)
                    pe.wait_ge(S["routed"], t + 1)
                    pe.wait_ge(free[b], r)
                    for w in range(3):
                        ins = nc.tensor.transpose(bank[b][:, w * P:(w + 1) * P], chosen[:, w, :], c.ident[:, :])
                    ins.then_inc(full[b], 1)
        clear(nc, s.sems)


def experts(c, l, xs, route, acc):
    nc, dram = c.nc, c.dram
    STEPS = NK
    BT = TOK // JG
    UN = 4
    with ExitStack() as ctx:
        sem = lambda name: ctx.enter_context(nc.semaphore("exp_" + name))
        sb = lambda name, shape, dt=F32: ctx.enter_context(nc.sbuf_tensor("exp_" + name, shape, dt))
        W = sb("W", [P, 2, TOK, JG])
        Us, Vs = sb("Us", [P, 2, 2, D], F32R), sb("Vs", [P, 2, D], F32R)
        gel, wa = sb("gelu", [P, TOK]), sb("wa", [P, TOK])
        was = sb("was", [P, 2, 2, TOK], F32R)
        Ai, Bj = sb("Ai", [P, 2, BT, NK], BF16), sb("Bj", [P, 2, 4, BT, JG], BF16)
        iota = sb("iota", [P, NK + JG], BF16)
        act_bank = ctx.enter_context(nc.psum_tensor("exp_act", [P, 512], F32))
        w_bank = ctx.enter_context(nc.psum_tensor("exp_w", [P, 512], F32))
        iota_in, zeroed = sem("iota_in"), sem("zeroed")
        u_hi, u_lo, v_hi, v_lo = sem("u_hi"), sem("u_lo"), sem("v_hi"), sem("v_lo")
        act_done, acc_done, w_done = sem("act_done"), sem("acc_done"), sem("w_done")
        gelu_done, wa_done, wa_hi, wa_lo = sem("gelu_done"), sem("wa_done"), sem("wa_hi"), sem("wa_lo")
        ai_ready, bj_hot, bj_ready, w_stored = sem("ai_ready"), sem("bj_hot"), sem("bj_ready"), sem("w_stored")
        sems = [iota_in, zeroed, u_hi, u_lo, v_hi, v_lo, act_done, acc_done, w_done, gelu_done, wa_done, wa_hi, wa_lo,
                ai_ready, bj_hot, bj_ready, w_stored]
        U_PIECE, V_PIECE = (0, 2), (1, 3)

        def at_slot(q):
            return slot(AT_EXP + q)

        def have(q, it):
            return filled(AT_EXP + q) + 16 * it

        def part_of(q, u):
            return c.ring[:, at_slot(q), (u % 2) * D:(u % 2 + 1) * D]

        def main_loop(eng, body):
            per = JG // UN
            with eng.Fori(0, STEPS // JG // 2) as cc:
                for par in range(2):
                    with eng.Fori(0, per) as it8:
                        for u in range(UN):
                            it = cc * (2 * per) + par * per + it8
                            body(it, it8, par, cc * 2 + par, u, cc * (2 * JG) + (par * JG + u) + it8 * UN)

        with nc.Block() as block:

            @block.sync
            def _(sp):
                sp.dma_start(iota[:, :], dram["iota"]).then_inc(iota_in, 16)
                with sp.Fori(1, STEPS // UN) as it:
                    for q in range(4):
                        steps_split = it * UN - UN + 2 * (q // 2 + 1)
                        if q % 2 == 0:
                            sp.wait_ge(u_lo, steps_split)
                        else:
                            sp.wait_ge(v_lo, steps_split * 2 + 1)
                        src = dram["uv"[q % 2]][bass.ds(l, 1), bass.ds(it * 2 + q // 2, 1)]
                        sp.dma_start(c.ring[:, at_slot(q), :], src.rearrange("a b p n -> (a b p) n")).then_inc(c.ring_full[at_slot(q)], 16)

            @block.gpsimd
            def _(pool):
                nc.gpsimd.memset(was[:, 1, :, :].bitcast(F32), 0.0).then_inc(zeroed, 1)
                nc.gpsimd.memset(Vs[:, :, :].bitcast(F32), 0.0).then_inc(zeroed, 1)

                def scale_one_hot(m, it8, u):
                    tok = it8 * (UN * BT) + u * BT
                    pool.wait_ge(bj_hot, m + 1)
                    for i in range(3):
                        ins = nc.gpsimd.tensor_tensor(Bj[:, u % 2, 1 + i, :, :], Bj[:, u % 2, 0, :, :],
                                                      route[:, 2 + i, bass.ds(tok, BT)].unsqueeze(2).to_broadcast([P, BT, JG]), ALU.mult)
                    ins.then_inc(bj_ready, 1)

                pool.sem_inc(v_lo, 1)
                with pool.Fori(0, JG // UN) as it8:
                    for u in range(UN):
                        scale_one_hot(it8 * UN + u, it8, u)

                def step(it, it8, par, chunk, u, j):
                    scale_one_hot(j + JG, it8, u)
                    q = V_PIECE[u // 2]
                    for h in range(2):
                        cols = slice(512 * h, 512 * h + 512)
                        pool.wait_ge(v_hi, 2 * j + (h + 1))
                        nc.gpsimd.tensor_tensor(Vs[:, 1, cols], part_of(q, u)[:, cols], Vs[:, 0, cols].bitcast(F32),
                                                ALU.subtract).then_inc(v_lo, 1)

                main_loop(pool, step)

            @block.scalar
            def _(act):
                def step(it, it8, par, chunk, u, j):
                    act.wait_ge(act_done, j + 3)
                    nc.scalar.activation(gel[:, :], act_bank[:, 0:TOK], ACT.Gelu_apprx_tanh).then_inc(gelu_done, 1)
                    act.wait_ge(wa_done, j + 1)
                    act.wait_ge(acc_done, 2 * j + 1)
                    nc.scalar.copy(was[:, u % 2, 0, :], wa[:, :]).then_inc(wa_hi, 1)
                    q = V_PIECE[u // 2]
                    act.wait_ge(c.ring_full[at_slot(q)], have(q, it))
                    for h in range(2):
                        cols = slice(512 * h, 512 * h + 512)
                        act.wait_ge(acc_done, 2 * j + (h + 2))
                        nc.scalar.copy(Vs[:, 0, cols], part_of(q, u)[:, cols]).then_inc(v_hi, 1)

                act.sem_inc(gelu_done, 1)
                main_loop(act, step)

            @block.vector
            def _(dve):
                V = nc.vector

                def build_one_hot(m, it8, u, base):
                    tok = it8 * (UN * BT) + u * BT
                    numbers = iota[:, bass.ds(base, JG)].unsqueeze(1).to_broadcast([P, BT, JG])
                    dve.wait_ge(w_done, m + 1)
                    V.tensor_tensor(Bj[:, u % 2, 0, :, :], numbers,
                                    route[:, 1, bass.ds(tok, BT)].unsqueeze(2).to_broadcast([P, BT, JG]),
                                    ALU.is_equal).then_inc(bj_hot, 1)
                    for n in range(BT):
                        ins = V.tensor_scalar(Ai[:, u % 2, n, :], iota[:, 0:NK], route[:, 0, bass.ds(tok + n, 1)], None, ALU.is_equal)
                    ins.then_inc(ai_ready, 1)

                def store_w(m, it8, u, buf):
                    tok = it8 * (UN * BT) + u * BT
                    dve.wait_ge(w_done, m + 3)
                    V.tensor_copy(W[:, buf, bass.ds(tok, BT), :],
                                  w_bank[:, 0:BT * JG].rearrange("p (t n) -> p t n", t=BT)).then_inc(w_stored, 1)

                dve.sem_inc(wa_lo, 1)
                dve.sem_inc(w_stored, 1)
                dve.wait_ge(iota_in, 16)
                with dve.Fori(0, JG // UN) as it8:
                    for u in range(UN):
                        m = it8 * UN + u
                        build_one_hot(m, it8, u, 0)
                        store_w(m, it8, u, 0)

                def step(it, it8, par, chunk, u, j):
                    q = U_PIECE[u // 2]
                    dve.wait_ge(c.ring_full[at_slot(q)], have(q, it))
                    dve.wait_ge(act_done, j + 1)
                    V.tensor_copy(Us[:, u % 2, 0, :], part_of(q, u)).then_inc(u_hi, 1)
                    dve.wait_ge(u_hi, j + 1)
                    ins = V.tensor_tensor(Us[:, u % 2, 1, :], part_of(q, u), Us[:, u % 2, 0, :].bitcast(F32), ALU.subtract)
                    ins.then_inc(u_lo, 1)
                    build_one_hot(j + JG, it8, u, (chunk + 1) * JG)
                    dve.wait_ge(gelu_done, j + 2)
                    dve.wait_ge(w_stored, j + (JG + 1))
                    V.tensor_tensor(wa[:, :], gel[:, :], W[:, par, :, bass.ds(it8 * UN + u, 1)].rearrange("p t a -> p (t a)"),
                                    ALU.mult).then_inc(wa_done, 1)
                    dve.wait_ge(wa_hi, j + 1)
                    V.tensor_tensor(was[:, u % 2, 1, :], wa[:, :], was[:, u % 2, 0, :].bitcast(F32), ALU.subtract).then_inc(wa_lo, 1)
                    store_w(j + JG, it8, u, 1 - par)

                main_loop(dve, step)

            @block.tensor
            def _(pe):
                mm = nc.tensor.matmul

                def build_w(m, u):
                    pe.wait_ge(ai_ready, m + 1)
                    pe.wait_ge(bj_ready, m + 1)
                    pe.wait_ge(w_stored, m + 1)
                    for n in range(BT):
                        for i in range(3):
                            ins = mm(w_bank[:, n * JG:(n + 1) * JG], Ai[:, u % 2, n, :], Bj[:, u % 2, 1 + i, n, :],
                                     start=(i == 0), stop=(i == 2))
                    ins.then_inc(w_done, 1)

                def add_v(buf, first=False, last=False):
                    for h in range(2):
                        cols = slice(512 * h, 512 * h + 512)
                        for t in range(TILES):
                            tok = slice(t * P, (t + 1) * P)
                            for n, (a, v) in enumerate(((0, 0), (0, 1), (1, 0))):
                                ins = mm(acc[2 * t + h][:, :], was[:, buf, a, tok], Vs[:, v, cols],
                                         start=False, stop=last and n == 2)
                        ins.then_inc(acc_done, 1)

                pe.wait_ge(zeroed, 2)
                credits = [act_done, act_done, w_done, w_done, acc_done, None]
                for i, credit in enumerate(credits):
                    ins = mm(acc[i][:, :], was[:, 1, 0, 0:P], Vs[:, 0, 0:512], start=True, stop=False)
                    if credit is not None:
                        ins.then_inc(credit, 1)
                with pe.Fori(0, JG // UN) as it8:
                    for u in range(UN):
                        build_w(it8 * UN + u, u)

                def step(it, it8, par, chunk, u, j):
                    pe.wait_ge(u_lo, j + 1)
                    pe.wait_ge(gelu_done, j + 1)
                    for k in range(KD):
                        for n, (a, v) in enumerate(((0, 0), (0, 1), (1, 0))):
                            ins = mm(act_bank[:, 0:TOK], Us[:, u % 2, a, k * P:(k + 1) * P], xs[:, v, k, :],
                                     start=(k == 0 and n == 0), stop=(k == KD - 1 and n == 2))
                    ins.then_inc(act_done, 1)
                    build_w(j + JG, u)
                    pe.wait_ge(wa_lo, j + 1)
                    pe.wait_ge(v_lo, 2 * j + 1)
                    add_v((u + 1) % 2)

                main_loop(pe, step)
                pe.wait_ge(wa_lo, STEPS + 1)
                pe.wait_ge(v_lo, 2 * STEPS + 1)
                add_v(1, last=True)
        clear(nc, sems)


def finish(c, l, acc):
    nc, dram = c.nc, c.dram
    with ExitStack() as ctx:
        sem = lambda name: ctx.enter_context(nc.semaphore("fin_" + name))
        sb = lambda name, shape, dt=F32: ctx.enter_context(nc.sbuf_tensor("fin_" + name, shape, dt))
        x, part, gates, gb = sb("x", [P, TILES, D]), sb("part", [P, TILES, D]), sb("gates", [P, 2, D]), sb("gb", [P, 2, D])
        stats, mv, rstd = sb("stats", [P, TILES, 12]), sb("mv", [P, TILES, 2]), sb("rstd", [P, TILES])
        x_in, vdone, var_ready, std_ready, normed, stored = map(sem, ("x_in", "vdone", "var_ready", "std_ready", "normed", "stored"))
        with nc.Block() as block:

            @block.scalar
            def _(act):
                load_for_norm(c, l, act, x_in, x, gates, 1, gb, "ln2")
                for t in range(TILES):
                    act.wait_ge(var_ready, t + 1)
                    nc.scalar.activation(rstd[:, t:t + 1], mv[:, t, 1:2], ACT.Sqrt).then_inc(std_ready, 1)

            @block.sync
            def _(sp):
                for t in range(TILES):
                    sp.wait_ge(normed, t + 1)
                    sp.dma_start(c.x_dram[t], x[:, t, :]).then_inc(stored, 16)
                    sp.dma_start(dram["y"][t], x[:, t, :]).then_inc(stored, 16)
                sp.wait_ge(stored, 32 * TILES)

            @block.vector
            def _(dve):
                link = in_order(dve, vdone)
                dve.wait_ge(x_in, 16 * LOADS_FOR_NORM)
                for t in range(TILES):
                    for h in range(2):
                        cols = slice(512 * h, 512 * h + 512)
                        ins = nc.vector.tensor_tensor(part[:, t, cols], acc[2 * t + h][:, :], gates[:, SEQ_OF_TILE[t], cols], ALU.mult)
                    link(ins)
                    link(nc.vector.scalar_tensor_tensor(x[:, t, :], x[:, t, :], ALPHA, part[:, t, :], ALU.mult, ALU.add))
                    norm_steps(nc, dve, link, x[:, t, :], stats[:, t, :], mv[:, t, :], rstd[:, t:t + 1], var_ready,
                               std_ready, t + 1, gb[:, 0, :], gb[:, 1, :], x[:, t, :]).then_inc(normed, 1)
        clear(nc, [x_in, vdone, var_ready, std_ready, normed, stored] + c.ring_full)


def build(nc, dram):
    with ExitStack() as ctx:
        c = make_core(nc, ctx, dram)
        input_norm(c)
        with nc.Fori(0, DEPTH) as l:
            modulation(c, l)
            with ExitStack() as mid:
                pT = mid.enter_context(nc.sbuf_tensor("pT", [P, N_IN, TOK], F32))
                mixT = mid.enter_context(nc.sbuf_tensor("mixT", [P, KD, TOK], F32))
                project(c, l, pT)
                attention(c, l, pT, mixT)
                rwkv(c, l, pT, mixT)
                output(c, l, mixT)
            with ExitStack() as mid:
                xs = mid.enter_context(nc.sbuf_tensor("xs", [P, 2, KD, TOK], F32R))
                route = mid.enter_context(nc.sbuf_tensor("route", [P, 5, TOK], BF16))
                routing(c, l, xs, route)
                acc = [mid.enter_context(nc.psum_tensor(f"acc{i}", [P, 512], F32)) for i in range(6)]
                experts(c, l, xs, route, acc)
                finish(c, l, acc)


def shape_constants():
    f = np.float32
    half = HD // 4
    freqs = (f(10000.0) ** (-np.arange(half, dtype=f) / f(half))).astype(f)
    t = np.arange(2 * P)
    cosT, sinT = np.zeros((HD, 2 * P), f), np.zeros((HD, 2 * P), f)
    rot = np.zeros((P, P), f)
    for axis, pos in enumerate((t // HD, t % HD)):
        ang = pos.astype(f)[None, :] * freqs[:, None]
        for part in range(2):
            lo = axis * 2 * half + part * half
            cosT[lo:lo + half], sinT[lo:lo + half] = np.cos(ang), np.sin(ang)
    for head in range(2):
        for axis in range(2):
            for i in range(half):
                a = head * HD + axis * 2 * half + i
                rot[a + half, a], rot[a, a + half] = -1.0, 1.0
    q, k = np.arange(P)[:, None], np.arange(2 * P)[None, :]
    mask = np.zeros((P, 2, 3 * P), f)
    for n in range(2):
        mask[:, n, P:] = np.where(np.abs(k - (q + n * P)) <= 128, 0.0, NEG)
    s_, t_ = np.arange(P)[:, None], np.arange(P)[None, :]
    same = (s_ // CHUNK) == (t_ // CHUNK)
    gram, level = np.zeros((P, 2, 4, P), f), np.zeros((P, 2, N_LEVELS, P), f)
    for d in range(2):
        before = (s_ < t_) if d == 0 else (s_ > t_)
        strict, incl = same & before, same & (before | (s_ == t_))
        gram[:, d, 0], gram[:, d, 1], gram[:, d, 2], gram[:, d, 3] = strict, incl, strict, incl
        for lev in range(N_LEVELS):
            level[:, d, lev] = before & ((s_ >> (lev + 1)) == (t_ >> (lev + 1))) & ((s_ >> lev) != (t_ >> lev))
    resets = np.ones((P, 2 * TOK), f)
    resets[:, ::CHUNK] = 0.0
    return {
        "ident": np.eye(P, dtype=f), "cosT": np.tile(cosT, (2, 1)), "sinT": np.tile(sinT, (2, 1)), "rotate": rot,
        "att_mask": mask, "gram_mask": gram.reshape(P, 2, 4 * P), "level_mask": level,
        "headones": (s_ // HD == t_ // HD).astype(f), "resets": resets,
        "iota16": np.tile(np.arange(TOPK, dtype=f), (P, 1)),
    }


def lay_out(i):
    L = DEPTH
    cat, tile = np.concatenate, np.ascontiguousarray

    def blocks(w, n):
        N = w.shape[2]
        per = PIECE // KD // n
        return tile(w.reshape(L, KD, P, N // n // per, per, n).transpose(0, 3, 2, 4, 1, 5)).reshape(L, -1, P, PIECE)

    def halves(a):
        a = a.reshape(L, -1, 2, P)
        return a.transpose(0, 3, 1, 2).reshape(L, P, -1)

    order = np.concatenate([np.r_[b * HD:(b + 1) * HD, (4 + b) * HD:(5 + b) * HD] for b in range(4)])
    w_in = cat([i["w_in"][:, :, order], i["w_in"][:, :, 512:]], axis=2)
    starts = [0, 128, 256, 384, 512, 640, 768, 896, 1024, 1152, 1280, 1408, 1536, 1664, 1728, 1856, 1984, 2112, 2240, 2368]
    w_in = cat([w_in[:, :, a:a + P] for a in starts], axis=2)
    w_out = cat([i["w_out"][:, order, :], i["w_out"][:, 512:, :]], axis=1)
    out = {
        "x_in": cat([i["x_prompt"].reshape(1, P, D), i["x_sample"].reshape(2, P, D)]),
        "ln_in": np.stack([i["ln_in_g"], i["ln_in_b"]]),
        "cond": tile(np.stack([i["c_ctx"], i["c"][0]]).reshape(2, KD, P).transpose(2, 1, 0)),
        "b_ada": np.stack([i["b_ada"]] * 2, axis=1),
        "w_ada": blocks(i["w_ada"], PIECE // KD), "w_in": blocks(w_in, P), "w_out": blocks(w_out, PIECE // KD),
        "wq": blocks(i["peer_wq"], P),
        "u": tile(i["peer_u"].reshape(L, P, NK // 2, 2, KD, P).transpose(0, 2, 5, 3, 4, 1)).reshape(L, NK // 2, P, PIECE),
        "v": tile(i["peer_v"].reshape(L, P, NK // 2, 2 * D).transpose(0, 2, 1, 3)),
        "cache_kT": tile(i["cache_k"][0].reshape(L, P, P).transpose(0, 2, 1)),
        "cache_v": i["cache_v"][0].reshape(L, P, P),
        "sink": np.repeat(i["att_sink"][:, None, :], P, axis=1),
        "conv_w": tile(i["conv_w"].reshape(L, 3, 2, P).transpose(0, 3, 2, 1)),
        "cols": cat([halves(i[n]) for n in ("rw_w0", "rw_a0", "rw_kk", "rw_ka", "rw_rk", "rw_lnx_g", "rw_lnx_b")]
                    + [np.zeros((L, P, N_COLS - 18), np.float32)], axis=2),
        "w_up": cat([i["rw_w_up"].reshape(L, 2 * RANK, 256), i["rw_a_up"].reshape(L, 2 * RANK, 256)], axis=1),
        "g_up": i["rw_g_up"],
        "state_T": tile(i["state_rwkv"][0].transpose(0, 1, 2, 4, 3)),
        "ln1": np.stack([i["ln1_g"], i["ln1_b"]], axis=1), "ln2": np.stack([i["ln2_g"], i["ln2_b"]], axis=1),
        "subkeys_T": tile(i["peer_subkeys"].reshape(L, 2 * PH, NK, P).transpose(0, 3, 1, 2)),
    }
    out.update(shape_constants())
    return {k: tile(v) for k, v in out.items()}


OUTS = {"y": [TILES, P, D], "new_k": [DEPTH, P, P], "new_v": [DEPTH, P, P], "new_state_T": [DEPTH, 2, 4, HD, HD]}


def kernel(**inputs):
    import concourse.bacc as bacc
    from concourse.bass_utils import run_bass_kernel_spmd as run
    import ml_dtypes

    arrays = lay_out({k: np.asarray(v) for k, v in inputs.items()})
    arrays["iota"] = np.tile(np.arange(NK + JG, dtype=np.float32), (P, 1)).astype(ml_dtypes.bfloat16)
    nc = bacc.Bacc("TRN2", target_bir_lowering=False, num_devices=1)
    dram = {k: nc.dram_tensor("in_" + k, v.shape, mybir.dt.from_np(v.dtype), kind="ExternalInput").ap() for k, v in arrays.items()}
    dram.update({k: nc.dram_tensor("out_" + k, v, F32, kind="ExternalOutput").ap() for k, v in OUTS.items()})
    build(nc, dram)
    r = run(nc, [{"in_" + k: v for k, v in arrays.items()}], core_ids=[0]).results[0]
    y, nk, nv = r["out_y"], r["out_new_k"], r["out_new_v"]
    return (y[0:1], y[1:3].reshape(1, 2 * P, D),
            nk.transpose(0, 2, 1).reshape(1, DEPTH, P, 2, HD), nv.transpose(0, 2, 1).reshape(1, DEPTH, P, 2, HD),
            r["out_new_state_T"].transpose(0, 1, 2, 4, 3)[None])
```

```python
import numpy as np
import concourse.bass as bass
from concourse import mybir
from concourse.alu_op_type import AluOpType as ALU
from contextlib import ExitStack

ACT = mybir.ActivationFunctionType
AX = mybir.AxisListType
F32, F32R, BF16, U32 = mybir.dt.float32, mybir.dt.float32r, mybir.dt.bfloat16, mybir.dt.uint32

P = 128
D = 1024
KD = D // P
DEPTH = 2
TILES = 3
TOK = TILES * P
SEQ_OF_TILE = (0, 1, 1)
HD = 64
RANK = 32
CHUNK = 64
N_LEVELS = 6
HEADS = 8
N_IN = 20
QB, KB, VB, RB, RKB, RVB, WAB, GB, CBB, CCB, CUB = 0, 4, 5, 6, 8, 10, 12, 13, 14, 16, 18
NEG = -1e30
LN_EPS, LNX_EPS = 1e-5, 64e-5
ALPHA = (2 * DEPTH) ** 0.25
TOPK = 16
NK = 128
PH = 8
JG = 32
JSTEP = TOK * 1 // JG

SLOTS = 4
PIECE = 2048
N_ADA, N_PIN, N_POUT, N_PQ, N_PEXP = 24, 10, 4, 8, 128
AT_IN = 0
AT_OUT = AT_IN + N_PIN
AT_Q = AT_OUT + N_POUT
AT_ADA = AT_Q + N_PQ
AT_EXP = AT_ADA + N_ADA
NW_ADA = PIECE // KD
NEXT = DEPTH - 1
assert DEPTH == 2
C_W0, C_A0, C_KK, C_KA, C_RK, C_LG, C_LB, C_CW, N_COLS = 0, 4, 8, 10, 12, 14, 16, 18, 24


def slot(n):
    return n % SLOTS


def filled(n):
    return 16 * (n // SLOTS + 1)


class Turns:

    def __init__(self, names, banks):
        self.n = {name: i for i, name in enumerate(names)}
        self.banks = banks

    def at(self, *name):
        i = self.n[name]
        return i % self.banks, i // self.banks


def layer_row(ap, l):
    row = ap[bass.ds(l, 1)]
    names = " ".join(f"x{i}" for i in range(len(ap.shape) - 1))
    first, rest = names.split(" ", 1) if " " in names else (names, "")
    return row.rearrange(f"a {names} -> (a {first}) {rest}")


def norm_steps(nc, dve, link, x, stats, mv, rstd, var_ready, std_ready, count, g, b, out):
    for h in range(2):
        ins = nc.vector.bn_stats(stats[:, 6 * h:6 * h + 6], x[:, 512 * h:512 * h + 512])
    link(ins)
    link(nc.vector.bn_aggr(mv, stats))
    nc.vector.tensor_scalar(mv[:, 1:2], mv[:, 1:2], LN_EPS, None, ALU.add).then_inc(var_ready, 1)
    dve.wait_ge(std_ready, count)
    link(nc.vector.reciprocal(rstd, rstd))
    link(nc.vector.tensor_scalar(out, x, mv[:, 0:1], rstd, ALU.subtract, ALU.mult))
    link(nc.vector.tensor_tensor(out, out, g, ALU.mult))
    return nc.vector.tensor_tensor(out, out, b, ALU.add)


def clear(nc, sems):
    for s in sems:
        nc.sync.sem_clear(s)
    nc.all_engine_barrier()


class Core:
    pass


def make_core(nc, ctx, dram):
    c = Core()
    c.nc, c.dram = nc, dram
    sb = lambda name, shape, dt=F32: ctx.enter_context(nc.sbuf_tensor(name, shape, dt))
    sem = lambda name: ctx.enter_context(nc.semaphore(name))
    c.ring = sb("ring", [P, SLOTS, PIECE])
    c.ident = sb("ident", [P, P])
    c.mod_cols = sb("mod_cols", [P, 4, KD, 2])
    c.ring_full = [sem(f"ring_full{i}") for i in range(SLOTS)]
    c.late_in = sem("late_in")
    c.x_dram = nc.dram_tensor("x_between_blocks", [TILES, P, D], F32, kind="Internal").ap()
    c.gate_dram = nc.dram_tensor("gate_rows", [DEPTH + 1, 2, 2, D], F32, kind="Internal").ap()
    c.silu, c.ones = sb("cond_silu", [P, KD, 2]), sb("ones", [1, 2])
    return c


def piece_source(c, l, n):
    for first, name in ((AT_EXP, "u"), (AT_ADA, "w_ada"), (AT_Q, "wq"), (AT_OUT, "w_out"), (AT_IN, "w_in")):
        if n >= first:
            break
    m = n - first
    if name == "w_ada":
        return c.dram[name][NEXT, m]
    if name == "u":
        name, m = ("u", "v")[m % 2], m // 2
    return c.dram[name][bass.ds(l, 1), m].rearrange("a p n -> (a p) n")


def fill_slot(c, sp, l, n):
    sp.dma_start(c.ring[:, slot(n), :], piece_source(c, l, n)).then_inc(c.ring_full[slot(n)], 16)



def ada_product(c, s, pe, rows, piece_full, count, ring_slot, n):
    b, r = s.steps.at("ada", n)
    pe.wait_ge(piece_full, count)
    pe.wait_ge(s.free[b], r)
    out, w = s.bank[b][0:2, 0:NW_ADA], c.ring[:, ring_slot, :].rearrange("p (k n) -> p k n", k=KD)
    c.nc.tensor.matmul(out, c.ones[:, :], rows[0:1, n * NW_ADA:(n + 1) * NW_ADA], start=True, stop=False)
    for k in range(KD):
        ins = c.nc.tensor.matmul(out, c.silu[:, k, :], w[:, k, :], start=False, stop=(k == KD - 1))
    ins.then_inc(s.full[b], 1)


def ada_copy(c, s, act, rows, n):
    b, r = s.steps.at("ada", n)
    act.wait_ge(s.full[b], r + 1)
    c.nc.scalar.copy(rows[:, n * NW_ADA:(n + 1) * NW_ADA], s.bank[b][0:2, 0:NW_ADA]).then_inc(s.free[b], 1)


def ada_transposes(c, s, pe, rows):
    b, r = s.steps.at("cols")
    for n in range(N_ADA):
        bb, rr = s.steps.at("ada", n)
        pe.wait_ge(s.free[bb], rr + 1)
    pe.wait_ge(s.free[b], r)
    for i, q in enumerate((0, 1, 3, 4)):
        for k in range(KD):
            ins = c.nc.tensor.transpose(s.bank[b][:, 2 * (i * KD + k):2 * (i * KD + k) + 2],
                                        rows[:, q * D + k * P:q * D + (k + 1) * P], c.ident[0:2, 0:2])
    ins.then_inc(s.full[b], 1)


def ada_columns(c, s, dve):
    b, r = s.steps.at("cols")
    dve.wait_ge(s.full[b], r + 1)
    cols = s.bank[b][:, 0:64].rearrange("p (q k s) -> p q k s", q=4, k=KD)
    c.nc.vector.tensor_copy(c.mod_cols[:, 0::2], cols[:, 0::2])
    c.nc.vector.tensor_scalar(c.mod_cols[:, 1::2], cols[:, 1::2], 1.0, None, ALU.add).then_inc(s.free[b], 1)


def store_gates(c, s, act, rows, place, stored):
    for n in range(N_ADA):
        b, r = s.steps.at("ada", n)
        act.wait_ge(s.free[b], r + 1)
    for i, q in enumerate((2, 5)):
        act.dma_start(place[i], rows[:, q * D:(q + 1) * D]).then_inc(stored, 16)
    act.wait_ge(stored, 32)


def begin(c):
    nc, dram = c.nc, c.dram
    with ExitStack() as ctx:
        s = Stage(c, ctx, "begin", [("ada", n) for n in range(N_ADA)] + [("cols",)],
                  ["x_in", "gb_in", "cond_in", "bias_in", "var_ready", "std_ready", "normed", "stored", "vdone",
                   "exp_ready", "cond_ready", "gates_stored"])
        S = s.named
        piece_full = [s.sem(f"piece_full{i}") for i in range(SLOTS)]
        x, gb, rows = s.sb("x", [P, TILES, D]), s.sb("gb", [P, 2, D]), s.sb("rows", [2, 6 * D])
        stats, mv, rstd = s.sb("stats", [P, TILES, 12]), s.sb("mv", [P, TILES, 2]), s.sb("rstd", [P, TILES])
        cond, cexp = s.sb("cond", [P, KD, 2]), s.sb("cond_exp", [P, KD, 2])
        with nc.Block() as block:

            @block.sync
            def _(sp):
                sp.dma_start(cond[:, :, :], dram["cond"]).then_inc(S["cond_in"], 16)
                sp.dma_start(rows[0:1, :], dram["b_ada"][0:1]).then_inc(S["bias_in"], 16)
                for n in range(N_ADA + SLOTS):
                    if n >= SLOTS:
                        b, r = s.steps.at("ada", n - SLOTS)
                        sp.wait_ge(s.full[b], r + 1)
                    if n < N_ADA:
                        sp.dma_start(c.ring[:, slot(n), :], dram["w_ada"][0, n]).then_inc(piece_full[slot(n)], 16)
                    else:
                        fill_slot(c, sp, 0, n - N_ADA)

            @block.scalar
            def _(act):
                act.dma_start(c.ident[:, :], dram["ident"]).then_inc(S["gb_in"], 16)
                for t in range(TILES):
                    act.dma_start(x[:, t, :], dram["x_in"][t]).then_inc(S["x_in"], 16)
                for i in range(2):
                    act.dma_start(gb[:, i, :], dram["ln_in"][i].partition_broadcast(P)).then_inc(S["gb_in"], 16)
                act.wait_ge(S["cond_in"], 16)
                nc.scalar.activation(cexp[:, :, :], cond[:, :, :], ACT.Exp, scale=-1.0).then_inc(S["exp_ready"], 1)
                for t in range(TILES):
                    act.wait_ge(S["var_ready"], t + 1)
                    nc.scalar.activation(rstd[:, t:t + 1], mv[:, t, 1:2], ACT.Sqrt).then_inc(S["std_ready"], 1)
                    ada_copy(c, s, act, rows, t)
                for n in range(TILES, N_ADA):
                    ada_copy(c, s, act, rows, n)
                for t in range(TILES):
                    act.wait_ge(S["normed"], t + 1)
                    act.dma_start(c.x_dram[t], x[:, t, :]).then_inc(S["stored"], 16)
                store_gates(c, s, act, rows, c.gate_dram[0], S["gates_stored"])
                act.wait_ge(S["stored"], 16 * TILES)

            @block.vector
            def _(dve):
                link = in_order(dve, S["vdone"])
                nc.vector.memset(c.ones[:, :], 1.0)
                dve.wait_ge(S["exp_ready"], 1)
                link(nc.vector.tensor_scalar(cexp[:, :, :], cexp[:, :, :], 1.0, None, ALU.add))
                link(nc.vector.reciprocal(cexp[:, :, :], cexp[:, :, :]))
                nc.vector.tensor_tensor(c.silu[:, :, :], cond[:, :, :], cexp[:, :, :], ALU.mult).then_inc(S["cond_ready"], 1)
                dve.wait_ge(S["x_in"], 16 * TILES)
                dve.wait_ge(S["gb_in"], 16 * 3)
                for t in range(TILES):
                    norm_steps(nc, dve, link, x[:, t, :], stats[:, t, :], mv[:, t, :], rstd[:, t:t + 1], S["var_ready"],
                               S["std_ready"], t + 1, gb[:, 0, :], gb[:, 1, :], x[:, t, :]).then_inc(S["normed"], 1)
                ada_columns(c, s, dve)

            @block.tensor
            def _(pe):
                pe.wait_ge(S["cond_ready"], 1)
                pe.wait_ge(S["bias_in"], 16)
                for n in range(N_ADA):
                    ada_product(c, s, pe, rows, piece_full[slot(n)], filled(n), slot(n), n)
                pe.wait_ge(S["gb_in"], 16 * 3)
                ada_transposes(c, s, pe, rows)
        clear(nc, s.sems)


class Stage:

    def __init__(self, c, ctx, name, turns, semaphores, banks=8):
        self.nc, self.ctx, self.name = c.nc, ctx, name
        self.steps = Turns(turns, banks)
        self.bank = [ctx.enter_context(c.nc.psum_tensor(f"{name}_bank{i}", [P, 512], F32)) for i in range(banks)]
        self.sems = []
        self.full = [self.sem(f"full{i}") for i in range(banks)]
        self.free = [self.sem(f"free{i}") for i in range(banks)]
        self.named = {n: self.sem(n) for n in semaphores}

    def sem(self, name):
        self.sems.append(self.ctx.enter_context(self.nc.semaphore(f"{self.name}_{name}")))
        return self.sems[-1]

    def sb(self, name, shape, dt=F32):
        return self.ctx.enter_context(self.nc.sbuf_tensor(f"{self.name}_{name}", shape, dt))


def in_order(eng, done):
    count = [0]

    def link(ins):
        count[0] += 1
        ins.then_inc(done, 1)
        eng.wait_ge(done, count[0])

    return link


def project(c, l, pT):
    nc, dram = c.nc, c.dram
    turns = [("xT", t, h) for t in range(TILES) for h in range(2)] + [("proj", b) for b in range(N_IN)]
    with ExitStack() as ctx:
        s = Stage(c, ctx, "project", turns, ["w_high", "w_low", "h_high", "h_low"])
        at, bank, full, free, S = s.steps.at, s.bank, s.full, s.free, s.named
        x_in = [s.sem(f"x_in{t}") for t in range(TILES)]
        x, hT, hs = s.sb("x", [P, TILES, D]), s.sb("hT", [P, KD, TOK]), s.sb("hs", [P, 2, KD, TOK], F32R)
        ws = s.sb("ws", [P, 2, 2, PIECE], F32R)
        with nc.Block() as block:

            @block.sync
            def _(sp):
                refill(c, s, sp, l, AT_IN, N_PIN)

            @block.scalar
            def _(act):
                for t in range(TILES):
                    act.dma_start(x[:, t, :], c.x_dram[t]).then_inc(x_in[t], 16)
                for m in range(2):
                    split_high(c, s, act, AT_IN, m, ws)
                split_rows_high(c, s, act, hT, hs, lambda t: [at("xT", t, h) for h in range(2)])
                for m in range(N_PIN):
                    b, r = at("proj", 2 * m)
                    act.wait_ge(full[b], r + 1)
                    nc.scalar.copy(pT[:, 2 * m, :], bank[b][:, 0:TOK]).then_inc(free[b], 1)
                    if m + 2 < N_PIN:
                        split_high(c, s, act, AT_IN, m + 2, ws, at("proj", 2 * m + 1))

            @block.vector
            def _(dve):
                for m in range(2):
                    split_low(c, s, dve, AT_IN, m, ws)
                modulate(c, s, dve, 0, hT)
                split_rows_low(c, s, dve, hT, hs)
                for m in range(N_PIN):
                    b, r = at("proj", 2 * m + 1)
                    dve.wait_ge(full[b], r + 1)
                    nc.vector.tensor_copy(pT[:, 2 * m + 1, :], bank[b][:, 0:TOK]).then_inc(free[b], 1)
                    if m + 2 < N_PIN:
                        split_low(c, s, dve, AT_IN, m + 2, ws)

            @block.tensor
            def _(pe):
                transpose_x(c, s, pe, x, x_in)
                pe.wait_ge(S["h_low"], TILES)
                for n in range(N_IN):
                    weight_blocks_times_h(c, s, pe, n, at("proj", n), ws, hs)
        clear(nc, s.sems)


PASSES = ((0, 0), (0, 1), (1, 0))


def split_high(c, s, act, first, m, ws, used=None):
    n = first + m
    act.wait_ge(c.ring_full[slot(n)], filled(n))
    if used is not None:
        b, r = used
        act.wait_ge(s.full[b], r + 1)
    c.nc.scalar.copy(ws[:, m % 2, 0, :], c.ring[:, slot(n), :]).then_inc(s.named["w_high"], 1)


def split_low(c, s, dve, first, m, ws):
    dve.wait_ge(s.named["w_high"], m + 1)
    c.nc.vector.tensor_tensor(ws[:, m % 2, 1, :], c.ring[:, slot(first + m), :], ws[:, m % 2, 0, :].bitcast(F32),
                              ALU.subtract).then_inc(s.named["w_low"], 1)


def refill(c, s, sp, l, first, count):
    for m in range(count):
        sp.wait_ge(s.named["w_low"], m + 1)
        fill_slot(c, sp, l, first + m + SLOTS)


def split_rows_high(c, s, act, source, hs, ready):
    for t in range(TILES):
        for b, r in ready(t):
            act.wait_ge(s.free[b], r + 1)
        cols = slice(t * P, (t + 1) * P)
        c.nc.scalar.copy(hs[:, 0, :, cols], source[:, :, cols]).then_inc(s.named["h_high"], 1)


def split_rows_low(c, s, dve, source, hs):
    for t in range(TILES):
        dve.wait_ge(s.named["h_high"], t + 1)
        cols = slice(t * P, (t + 1) * P)
        c.nc.vector.tensor_tensor(hs[:, 1, :, cols], source[:, :, cols], hs[:, 0, :, cols].bitcast(F32),
                                  ALU.subtract).then_inc(s.named["h_low"], 1)


def weight_blocks_times_h(c, s, pe, n, turn, ws, hs):
    b, r = turn
    pe.wait_ge(s.named["w_low"], n // 2 + 1)
    pe.wait_ge(s.free[b], r)
    w = ws[:, (n // 2) % 2].rearrange("p s (h k n) -> p s h k n", h=2, k=KD)
    for k in range(KD):
        for i, (a, v) in enumerate(PASSES):
            ins = c.nc.tensor.matmul(s.bank[b][:, 0:TOK], w[:, a, n % 2, k, :], hs[:, v, k, :],
                                     start=(k == 0 and i == 0), stop=(k == KD - 1 and i == 2))
    ins.then_inc(s.full[b], 1)


def transpose_x(c, s, pe, x, x_in):
    for t in range(TILES):
        pe.wait_ge(x_in[t], 16)
        for h in range(2):
            b, r = s.steps.at("xT", t, h)
            pe.wait_ge(s.free[b], r)
            for k in range(4):
                f = 4 * h + k
                ins = c.nc.tensor.transpose(s.bank[b][:, k * P:(k + 1) * P], x[:, t, f * P:(f + 1) * P], c.ident[:, :])
            ins.then_inc(s.full[b], 1)


def modulate(c, s, dve, q, hT):
    for t in range(TILES):
        for h in range(2):
            b, r = s.steps.at("xT", t, h)
            dve.wait_ge(s.full[b], r + 1)
            for k in range(4):
                f, seq = 4 * h + k, SEQ_OF_TILE[t]
                ins = c.nc.vector.tensor_scalar(hT[:, f, t * P:(t + 1) * P], s.bank[b][:, k * P:(k + 1) * P],
                                                c.mod_cols[:, 2 * q + 1, f, seq:seq + 1],
                                                c.mod_cols[:, 2 * q, f, seq:seq + 1], ALU.mult, ALU.add)
            ins.then_inc(s.free[b], 1)


def attention(c, l, pT, mixT):
    nc, dram = c.nc, c.dram
    turns = [("rot", b) for b in range(5)] + [("avT",)]
    for t in range(TILES):
        turns += [("score", t, h) for h in range(HEADS)]
        for b in range(4):
            turns += [("probT", t, b, g) for g in range(2)] + [("att", t, b)]
    CONV = ((0, P), (P, TOK))
    with ExitStack() as ctx:
        s = Stage(c, ctx, "att", turns, ["tables_in", "k_out", "k_stored", "vdone", "pdone", "adone", "maxed", "expd",
                                         "sums", "scaled", "att_done", "conv_cols", "sink_exp"])
        at, bank, full, free, S = s.steps.at, s.bank, s.full, s.free, s.named
        cosT, sinT, rotate = s.sb("cosT", [P, 2 * P]), s.sb("sinT", [P, 2 * P]), s.sb("rotate", [P, P])
        mask, sink = s.sb("mask", [P, 2, 3 * P]), s.sb("sink", [P, HEADS])
        conv_w = s.sb("conv_w", [P, 2, 3])
        cacheT, vkey = s.sb("cacheT", [P, P]), s.sb("vkey", [P, 1 + TILES, P])
        turned = s.sb("turned", [P, 5, 2 * P])
        kctx = s.sb("kctx", [P, P])
        prob = s.sb("prob", [P, 2, HEADS, 3 * P])
        probT = s.sb("probT", [P, 4, 3, P])
        row = s.sb("row", [P, TILES, 5, HEADS])
        z, z1 = s.sb("conv_z", [P, 2, TOK]), s.sb("conv_z1", [P, 2, TOK])
        probT_turn = {}
        for t in range(TILES):
            for b in range(4):
                for g in range(2):
                    probT_turn[t, b, g] = len(probT_turn)
        with nc.Block() as block:

            @block.sync
            def _(sp):
                for dst, src in ((cosT, dram["cosT"]), (sinT, dram["sinT"]), (rotate, dram["rotate"])):
                    sp.dma_start(dst[:, :], src).then_inc(S["tables_in"], 16)
                sp.dma_start(mask[:, :, :], dram["att_mask"]).then_inc(S["tables_in"], 16)
                sp.dma_start(sink[:, :], layer_row(dram["sink"], l)).then_inc(S["tables_in"], 16)
                sp.dma_start(conv_w[:, :, :], layer_row(dram["conv_w"], l)).then_inc(S["tables_in"], 16)
                sp.dma_start(cacheT[:, :], layer_row(dram["cache_kT"], l)).then_inc(S["tables_in"], 16)
                sp.dma_start(vkey[:, 0, :], layer_row(dram["cache_v"], l)).then_inc(S["tables_in"], 16)
                sp.dma_start(layer_row(dram["new_k"], l), pT[:, KB, 0:P]).then_inc(S["k_stored"], 16)
                sp.dma_start(layer_row(dram["new_v"], l), pT[:, VB, 0:P]).then_inc(S["k_stored"], 16)
                sp.wait_ge(S["k_stored"], 32)

            @block.gpsimd
            def _(pool):
                link = in_order(pool, S["pdone"])
                pool.wait_ge(S["tables_in"], 16 * 8)
                link(nc.gpsimd.tensor_tensor(z[:, :, :], pT[:, CCB:CCB + 2, :], pT[:, CUB:CUB + 2, :], ALU.mult))
                for g in range(2):
                    link(nc.gpsimd.tensor_scalar(mixT[:, 6 + g, :], z[:, g, :], conv_w[:, g, 1:2], None, ALU.mult))
                for g in range(2):
                    for w, src, dst in ((0, 0, 1), (2, 1, 0)):
                        link(nc.gpsimd.tensor_scalar(z1[:, g, :], z[:, g, :], conv_w[:, g, w:w + 1], None, ALU.mult))
                        for lo, hi in CONV:
                            n = hi - lo - 1
                            out = mixT[:, 6 + g, lo + dst:lo + dst + n]
                            ins = nc.gpsimd.tensor_tensor(out, out, z1[:, g, lo + src:lo + src + n], ALU.add)
                        link(ins)
                    link(nc.gpsimd.tensor_tensor(mixT[:, 6 + g, :], mixT[:, 6 + g, :], pT[:, CBB + g, :], ALU.mult))

            @block.scalar
            def _(act):
                b, r = at("avT")
                act.wait_ge(full[b], r + 1)
                nc.scalar.copy(vkey[:, 1:4, :], bank[b][:, 0:TOK].rearrange("p (t n) -> p t n", t=TILES)).then_inc(free[b], 1)
                for t in range(TILES):
                    nk = 1 if t == 0 else 3
                    act.wait_ge(S["maxed"], t + 1)
                    for h in range(HEADS):
                        nc.scalar.activation(prob[:, t % 2, h, 0:nk * P], prob[:, t % 2, h, 0:nk * P], ACT.Exp,
                                             bias=row[:, t, 1, h:h + 1], accum_out=row[:, t, 2, h:h + 1])
                    nc.scalar.activation(row[:, t, 3, :], row[:, t, 3, :], ACT.Exp).then_inc(S["expd"], 1)
                    for bb in range(4):
                        for g in range(2):
                            b, r = at("probT", t, bb, g)
                            m = probT_turn[t, bb, g]
                            act.wait_ge(full[b], r + 1)
                            if m >= 4:
                                ab, ar = at("att", *[k for k, v in probT_turn.items() if v == m - 4][0][:2])
                                act.wait_ge(full[ab], ar + 1)
                            nc.scalar.copy(probT[:, m % 4, 0:nk, :],
                                           bank[b][:, 0:nk * P].rearrange("p (k n) -> p k n", k=nk)).then_inc(free[b], 1)

            @block.vector
            def _(dve):
                link = in_order(dve, S["vdone"])
                dve.wait_ge(S["tables_in"], 16 * 8)
                dve.wait_ge(S["k_stored"], 32)
                nc.vector.tensor_copy(kctx[:, :], pT[:, KB, 0:P])
                for b5 in range(5):
                    b, r = at("rot", b5)
                    dve.wait_ge(full[b], r + 1)
                    nc.vector.tensor_tensor(turned[:, b5, :], bank[b][:, 0:2 * P], sinT[:, :], ALU.mult).then_inc(free[b], 1)
                    link(nc.vector.tensor_tensor(pT[:, b5, P:TOK], pT[:, b5, P:TOK], cosT[:, :], ALU.mult))
                    ins = nc.vector.tensor_tensor(pT[:, b5, P:TOK], pT[:, b5, P:TOK], turned[:, b5, :], ALU.add)
                ins.then_inc(S["scaled"], 1)
                for t in range(TILES):
                    nk = 1 if t == 0 else 3
                    if t >= 2:
                        b, r = at("att", t - 2, 3)
                        dve.wait_ge(full[b], r + 1)
                    for h in range(HEADS):
                        b, r = at("score", t, h)
                        dve.wait_ge(full[b], r + 1)
                        if t == 0:
                            ins = nc.vector.tensor_scalar(prob[:, 0, h, 0:P], bank[b][:, 0:P], HD ** -0.5, None, ALU.mult)
                        else:
                            ins = nc.vector.scalar_tensor_tensor(prob[:, t % 2, h, :], bank[b][:, 0:3 * P], HD ** -0.5,
                                                                 mask[:, t - 1, :], ALU.mult, ALU.add)
                        ins.then_inc(free[b], 1)
                    for h in range(HEADS):
                        b, r = at("score", t, h)
                        dve.wait_ge(free[b], r + 1)
                    link(nc.vector.tensor_reduce(row[:, t, 0, :], prob[:, t % 2, :, 0:nk * P], AX.X, ALU.max))
                    link(nc.vector.tensor_tensor(row[:, t, 0, :], row[:, t, 0, :], sink[:, :], ALU.max))
                    nc.vector.tensor_scalar(row[:, t, 1, :], row[:, t, 0, :], -1.0, None, ALU.mult)
                    nc.vector.tensor_tensor(row[:, t, 3, :], sink[:, :], row[:, t, 0, :], ALU.subtract).then_inc(S["maxed"], 1)
                    dve.wait_ge(S["expd"], t + 1)
                    link(nc.vector.tensor_tensor(row[:, t, 2, :], row[:, t, 2, :], row[:, t, 3, :], ALU.add))
                    link(nc.vector.reciprocal(row[:, t, 4, :], row[:, t, 2, :]))
                    for h in range(HEADS):
                        ins = nc.vector.tensor_scalar(prob[:, t % 2, h, 0:nk * P], prob[:, t % 2, h, 0:nk * P],
                                                      row[:, t, 4, h:h + 1], None, ALU.mult)
                    ins.then_inc(S["scaled"], 1)
                    for bb in range(4):
                        b, r = at("att", t, bb)
                        dve.wait_ge(full[b], r + 1)
                        nc.vector.tensor_copy(mixT[:, bb, t * P:(t + 1) * P], bank[b][:, 0:P]).then_inc(free[b], 1)

            @block.tensor
            def _(pe):
                pe.wait_ge(S["tables_in"], 16 * 8)
                for b5 in range(5):
                    b, r = at("rot", b5)
                    pe.wait_ge(free[b], r)
                    nc.tensor.matmul(bank[b][:, 0:2 * P], rotate[:, :], pT[:, b5, P:TOK], start=True, stop=True).then_inc(full[b], 1)
                b, r = at("avT")
                pe.wait_ge(free[b], r)
                for t in range(TILES):
                    ins = nc.tensor.transpose(bank[b][:, t * P:(t + 1) * P], pT[:, VB, t * P:(t + 1) * P], c.ident[:, :])
                ins.then_inc(full[b], 1)
                b, r = at("avT")
                pe.wait_ge(free[b], r + 1)
                pe.wait_ge(S["scaled"], 1)
                for t in range(TILES):
                    for h in range(HEADS):
                        b, r = at("score", t, h)
                        pe.wait_ge(free[b], r)
                        rows = slice(HD * (h // 4), HD * (h // 4) + HD)
                        q = pT[rows, h % 4, t * P:(t + 1) * P]
                        if t == 0:
                            ins = nc.tensor.matmul(bank[b][:, 0:P], q, kctx[rows, :], start=True, stop=True)
                        else:
                            nc.tensor.matmul(bank[b][:, 0:P], q, cacheT[rows, :], start=True, stop=True)
                            ins = nc.tensor.matmul(bank[b][:, P:3 * P], q, pT[rows, KB, P:TOK], start=True, stop=True)
                        ins.then_inc(full[b], 1)
                    pe.wait_ge(S["scaled"], t + 2)
                    values = [1] if t == 0 else [0, 2, 3]
                    for bb in range(4):
                        for g in range(2):
                            b, r = at("probT", t, bb, g)
                            pe.wait_ge(free[b], r)
                            for k in range(len(values)):
                                ins = nc.tensor.transpose(bank[b][:, k * P:(k + 1) * P],
                                                          prob[:, t % 2, bb + 4 * g, k * P:(k + 1) * P], c.ident[:, :])
                            ins.then_inc(full[b], 1)
                        ab, ar = at("att", t, bb)
                        pe.wait_ge(free[ab], ar)
                        for g in range(2):
                            b, r = at("probT", t, bb, g)
                            pe.wait_ge(free[b], r + 1)
                            m = probT_turn[t, bb, g]
                            for k, v in enumerate(values):
                                ins = nc.tensor.matmul(bank[ab][HD * g:HD * g + HD, 0:P], vkey[:, v, HD * g:HD * g + HD],
                                                       probT[:, m % 4, k, :], start=(k == 0), stop=(k == len(values) - 1))
                        ins.then_inc(full[ab], 1)
        clear(nc, s.sems)


DECAY = float(np.exp(-0.5))


def rwkv(c, l, pT, mixT):
    nc, dram = c.nc, c.dram
    turns = [("decay", d, g) for d in range(2) for g in range(2)]
    turns += [("rate", d, g) for d in range(2) for g in range(2)]
    turns += [("gate", g) for g in range(2)] + [("kk2", g) for g in range(2)] + [("vT", g) for g in range(2)]
    GH = [(g, hh) for g in range(2) for hh in range(2)]
    GT = [(g, t) for g in range(2) for t in range(TILES)]
    chunks = {}
    for d in range(2):
        for s_, n0, n1 in ((0, 0, 2), (1, 2, 6)):
            chunks[d, s_] = list(range(n0, n1)) if d == 0 else list(range(n1 - 1, n0 - 1, -1))
    scans = [(s_, step) for step in range(4) for s_ in range(2) if (s_ == 1 or step == 1)]
    for d in range(2):
        for g, t in GT:
            turns += [("tokens", d, g, t)] + [("gram", d, g, t, hh) for hh in range(2)]
        turns += [("inv0", d, g, hh) for g, hh in GH]
        for lev in range(1, N_LEVELS):
            turns += [("invY", d, lev, g, hh) for g, hh in GH]
            for g, hh in GH:
                turns += ([("invX", d, lev, g, hh)] if lev < N_LEVELS - 1 else []) + [("invXT", d, lev, g, hh)]
        turns += [(n, d, g, t) for n in ("GW", "H", "EF", "QZ") for g, t in GT]
        turns += [("scan", d, s_, step, g) for s_, step in scans for g in range(2)]
    turns += [(n, g) for n in ("bonus", "mean", "var") for g in range(2)]

    with ExitStack() as ctx:
        s = Stage(c, ctx, "rwkv", turns, ["params_in", "zeroed", "states_in", "squashed", "sigmoids", "kk2_in", "kk_root",
                                          "vdone", "exps_asked", "exps", "chunk_ops", "levelled", "seeded",
                                          "states", "state_out", "sums_in", "centred", "var_root", "adone"])
        at, bank, full, free, S = s.steps.at, s.bank, s.full, s.free, s.named
        cols, one_ka = s.sb("cols", [P, N_COLS]), s.sb("one_ka", [P, 2])
        w_up, g_up = s.sb("w_up", [P, 2 * P]), s.sb("g_up", [HD, 2 * P])
        headones, resets = s.sb("headones", [P, P]), s.sb("resets", [P, 2 * TOK])
        gram_mask, level_mask = s.sb("gram_mask", [P, 2, 4 * P]), s.sb("level_mask", [P, 2, N_LEVELS, P])
        v_tok = s.sb("v_tok", [P, TILES, 2 * P])
        gate, kk, kdsum, y = (s.sb(n, [P, 2, TOK]) for n in ("gate", "kk", "kdsum", "y"))
        Lsum, kd = s.sb("Lsum", [P, 2, TOK]), s.sb("kd", [P, 2, TOK])
        rate1 = s.sb("rate1", [P, 2, TOK])
        AR = s.sb("AR", [P, 2, 2, TOK])
        Bf, Kf = s.sb("Bf", [P, 2, TOK]), s.sb("Kf", [P, 2, TOK])
        decayC = s.sb("decayC", [P, 2, 6])
        A_tok = s.sb("A_tok", [P, 2, TILES, P])
        BK_tok = s.sb("BK_tok", [P, 2, TILES, 2, 2, P])
        M = s.sb("M", [P, 2, 2, TILES, 4, P])
        Ak = s.sb("Ak", [P, 2, 2, TILES, P])
        Dm, DT, Ym = (s.sb(n, [P, 2, 2, TILES, P]) for n in ("Dm", "DT", "Ym"))
        GW, H = s.sb("GW", [P, 2, TILES, 2 * P]), s.sb("H", [P, 2, TILES, P])
        s_init = s.sb("s_init", [P, 2, 2, P])
        t_exc, t_inc, t_inv = pT[:, 0:2, :], pT[:, 2:4, :], pT[:, 4:6, :]
        sig = [pT[:, 14:16, :], pT[:, 16:18, :]]
        rate = [pT[:, 18:20, :], rate1[:, :, :]]
        r_, k_, v_ = pT[:, RB:RB + 2, :], pT[:, RKB:RKB + 2, :], pT[:, RVB:RVB + 2, :]
        ET = s.sb("ET", [P, 2, TILES, 2, P])
        F = Ym[:, :, :, :, :].rearrange("p g h t n -> p (g h t) n")
        QT = Ak[:, :, 0, :, :]
        state = Dm[:, :, :, :, :].rearrange("p g h t n -> p (g h t) n")

        def F_at(g, t, ch):
            return F[:, (g * TILES + t) * 2 + ch, :]

        def state_at(g, s_, step):
            return state[:, g * 6 + (step - 1 if s_ == 0 else 1 + step), :]

        def tile_cols(t):
            return slice(t * P, (t + 1) * P)

        with nc.Block() as block:

            @block.sync
            def _(sp):
                sp.wait_ge(S["zeroed"], 1)
                for d in range(2):
                    for h in range(4):
                        rows = slice(HD * (h % 2), HD * (h % 2) + HD)
                        sp.dma_start(s_init[rows, d, h // 2, rows],
                                     dram["state_T"][bass.ds(l, 1), d, h].rearrange("a p n -> (a p) n")).then_inc(S["states_in"], 16)
                for d in range(2):
                    sp.wait_ge(S["state_out"], 2 * (d + 1))
                    for h in range(4):
                        rows = slice(HD * (h % 2), HD * (h % 2) + HD)
                        sp.dma_start(dram["new_state_T"][bass.ds(l, 1), d, h].rearrange("a p n -> (a p) n"),
                                     state_at(h // 2, 0, 2)[rows, rows]).then_inc(S["states"], 16)
                    sp.wait_ge(S["states"], 64 * (d + 1))

            @block.gpsimd
            def _(pool):
                nc.gpsimd.memset(s_init[:, :, :, :], 0.0).then_inc(S["zeroed"], 1)
                nc.gpsimd.memset(BK_tok[:, :, :, :, :, :], 0.0).then_inc(S["zeroed"], 1)

            @block.scalar
            def _(act):
                for dst, src in ((cols, "cols"), (w_up, "w_up"), (g_up, "g_up")):
                    act.dma_start(dst[:, :], layer_row(dram[src], l)).then_inc(S["params_in"], 16)
                act.dma_start(headones[:, :], dram["headones"]).then_inc(S["params_in"], 16)
                act.dma_start(resets[:, :], dram["resets"]).then_inc(S["params_in"], 16)
                act.dma_start(gram_mask[:, :, :], dram["gram_mask"]).then_inc(S["params_in"], 16)
                act.dma_start(level_mask[:, :, :, :], dram["level_mask"]).then_inc(S["params_in"], 16)
                act.wait_ge(S["params_in"], 16 * 7)
                nc.scalar.activation(pT[0:HD, WAB, :], pT[0:HD, WAB, :], ACT.Tanh).then_inc(S["squashed"], 1)
                nc.scalar.activation(pT[0:HD, GB, :], pT[0:HD, GB, :], ACT.Sigmoid).then_inc(S["squashed"], 1)
                for name, dst, col in (("decay", sig, C_W0), ("rate", rate, C_A0)):
                    for d in range(2):
                        for g in range(2):
                            b, r = at(name, d, g)
                            act.wait_ge(full[b], r + 1)
                            nc.scalar.activation(dst[d][:, g, :], bank[b][:, 0:TOK], ACT.Sigmoid,
                                                 bias=cols[:, col + 2 * d + g:col + 2 * d + g + 1]).then_inc(free[b], 1)
                for g in range(2):
                    b, r = at("gate", g)
                    act.wait_ge(full[b], r + 1)
                    nc.scalar.copy(gate[:, g, :], bank[b][:, 0:TOK]).then_inc(free[b], 1)
                for g in range(2):
                    b, r = at("kk2", g)
                    act.wait_ge(free[b], r + 1)
                nc.scalar.activation(t_exc, t_exc, ACT.Sqrt).then_inc(S["kk_root"], 1)
                for g in range(2):
                    b, r = at("vT", g)
                    act.wait_ge(full[b], r + 1)
                    nc.scalar.copy(v_tok[:, :, g * P:(g + 1) * P],
                                   bank[b][:, 0:TOK].rearrange("p (t n) -> p t n", t=TILES)).then_inc(free[b], 1)
                act.wait_ge(S["zeroed"], 2)
                for d in range(2):
                    act.wait_ge(S["exps_asked"], d + 1)
                    inc = Lsum[:, :, :] if d == 0 else t_inc
                    tot = Lsum[:, :, :].rearrange("p g (k n) -> p g k n", n=CHUNK)[:, :, :, CHUNK - 1]
                    nc.scalar.activation(t_exc, t_exc, ACT.Exp, scale=-DECAY)
                    nc.scalar.activation(t_inv, inc, ACT.Exp, scale=DECAY)
                    nc.scalar.activation(decayC[:, :, :], tot, ACT.Exp, scale=-DECAY).then_inc(S["adone"], 1)
                    act.wait_ge(S["adone"], d + 1)
                    nc.scalar.activation(t_inc, inc, ACT.Exp, scale=-DECAY).then_inc(S["exps"], 1)
                    if d == 1:
                        b, r = at("QZ", 0, 1, 2)
                        act.wait_ge(full[b], r + 1)
                    for g, t in GT:
                        b, r = at("tokens", d, g, t)
                        act.wait_ge(full[b], r + 1)
                        nc.scalar.copy(A_tok[:, g, t, :], bank[b][:, 0:P])
                        for ch in range(2):
                            rows = slice(CHUNK * ch, CHUNK * ch + CHUNK)
                            ins = nc.scalar.copy(BK_tok[rows, g, t, :, ch, :],
                                                 bank[b][rows, P:3 * P].rearrange("p (w n) -> p w n", w=2))
                        ins.then_inc(free[b], 1)
                    for lev in range(1, N_LEVELS):
                        for g, hh in GH:
                            b, r = at("invY", d, lev, g, hh)
                            act.wait_ge(full[b], r + 1)
                            nc.scalar.copy(Ym[:, g, hh, :, :], bank[b][:, 0:TOK].rearrange("p (t n) -> p t n", t=TILES)).then_inc(free[b], 1)
                    for g, t in GT:
                        b, r = at("GW", d, g, t)
                        act.wait_ge(full[b], r + 1)
                        nc.scalar.copy(GW[:, g, t, :], bank[b][:, 0:2 * P]).then_inc(free[b], 1)
                    for g, t in GT:
                        b, r = at("H", d, g, t)
                        act.wait_ge(full[b], r + 1)
                        nc.scalar.copy(H[:, g, t, :], bank[b][:, 0:P]).then_inc(free[b], 1)
                for g in range(2):
                    b, r = at("var", g)
                    act.wait_ge(free[b], r + 1)
                nc.scalar.activation(t_exc, t_exc, ACT.Sqrt).then_inc(S["var_root"], 1)

            @block.vector
            def _(dve):
                link = in_order(dve, S["vdone"])
                dve.wait_ge(S["params_in"], 16 * 7)
                link(nc.vector.tensor_scalar(one_ka[:, :], cols[:, C_KA:C_KA + 2], -1.0, 1.0, ALU.mult, ALU.add))
                for g in range(2):
                    ins = nc.vector.tensor_scalar(kk[:, g, :], k_[:, g, :], cols[:, C_KK + g:C_KK + g + 1], None, ALU.mult)
                link(ins)
                nc.vector.tensor_tensor(t_inc, kk[:, :, :], kk[:, :, :], ALU.mult).then_inc(S["kk2_in"], 1)
                for g in range(2):
                    b, r = at("kk2", g)
                    dve.wait_ge(full[b], r + 1)
                    nc.vector.tensor_scalar(t_exc[:, g, :], bank[b][:, 0:TOK], 1e-24, None, ALU.max).then_inc(free[b], 1)
                dve.wait_ge(S["kk_root"], 1)
                link(nc.vector.reciprocal(t_exc, t_exc))
                link(nc.vector.tensor_tensor(kk[:, :, :], kk[:, :, :], t_exc, ALU.mult))
                for d in range(2):
                    for name in ("decay", "rate"):
                        for g in range(2):
                            b, r = at(name, d, g)
                            dve.wait_ge(free[b], r + 1)
                    flat = lambda ap: ap.rearrange("p g n -> p (g n)")
                    link(nc.vector.tensor_tensor_scan(flat(Lsum[:, :, :]), resets[:, :], flat(sig[d]), 0.0, ALU.mult, ALU.add))
                    if d == 0:
                        nc.vector.tensor_tensor(t_exc, Lsum[:, :, :], sig[d], ALU.subtract).then_inc(S["exps_asked"], 1)
                    else:
                        by_chunk = flat(Lsum[:, :, :]).rearrange("p (k n) -> p k n", n=CHUNK)
                        tot = by_chunk[:, :, CHUNK - 1:CHUNK].to_broadcast([P, 2 * TOK // CHUNK, CHUNK])
                        link(nc.vector.tensor_tensor(flat(t_exc).rearrange("p (k n) -> p k n", n=CHUNK), tot, by_chunk, ALU.subtract))
                        nc.vector.tensor_tensor(t_inc, t_exc, sig[d], ALU.add).then_inc(S["exps_asked"], 1)
                    for g in range(2):
                        ins = nc.vector.tensor_scalar(kd[:, g, :], rate[d][:, g, :], cols[:, C_KA + g:C_KA + g + 1],
                                                      one_ka[:, g:g + 1], ALU.mult, ALU.add)
                    link(ins)
                    link(nc.vector.tensor_tensor(kd[:, :, :], kd[:, :, :], k_, ALU.mult))
                    if d == 0:
                        nc.vector.tensor_copy(kdsum[:, :, :], kd[:, :, :])
                    else:
                        nc.vector.tensor_tensor(kdsum[:, :, :], kdsum[:, :, :], kd[:, :, :], ALU.add)
                    link(nc.vector.tensor_tensor(rate[d], rate[d], kk[:, :, :], ALU.mult))
                    dve.wait_ge(S["exps"], d + 1)
                    nc.vector.scalar_tensor_tensor(AR[:, :, 0, :], kk[:, :, :], -1.0, t_exc, ALU.mult, ALU.mult)
                    nc.vector.tensor_tensor(AR[:, :, 1, :], r_, t_inc, ALU.mult)
                    nc.vector.tensor_tensor(Bf[:, :, :], rate[d], t_inv, ALU.mult)
                    nc.vector.tensor_tensor(Kf[:, :, :], kd[:, :, :], t_inv, ALU.mult).then_inc(S["chunk_ops"], 1)
                    for g, t in GT:
                        for hh in range(2):
                            b, r = at("gram", d, g, t, hh)
                            dve.wait_ge(full[b], r + 1)
                            nc.vector.tensor_tensor(M[:, g, hh, t, :, :].rearrange("p q n -> p (q n)"), bank[b][:, :],
                                                    gram_mask[:, d, :], ALU.mult).then_inc(free[b], 1)
                    for g, t in GT:
                        b, r = at("gram", d, g, t, 1)
                        dve.wait_ge(free[b], r + 1)

                    def level(lev, g, hh):
                        lm = level_mask[:, d, lev, :].unsqueeze(1).to_broadcast([P, TILES, P])
                        return nc.vector.tensor_tensor(Ak[:, g, hh, :, :], M[:, g, hh, :, 0, :], lm, ALU.mult).then_inc(S["levelled"], 1)

                    def levels_done(lev):
                        return 4 * (d * N_LEVELS + lev + 1)

                    eye = c.ident[:, :].unsqueeze(1).to_broadcast([P, TILES, P])
                    for g, hh in GH:
                        level(0, g, hh)
                    dve.wait_ge(S["levelled"], levels_done(0))
                    for g, hh in GH:
                        b, r = at("inv0", d, g, hh)
                        dve.wait_ge(full[b], r + 1)
                        nc.vector.tensor_tensor(DT[:, g, hh, :, :], Ak[:, g, hh, :, :], eye, ALU.add)
                        nc.vector.tensor_tensor(Dm[:, g, hh, :, :], bank[b][:, 0:TOK].rearrange("p (t n) -> p t n", t=TILES),
                                                eye, ALU.add).then_inc(free[b], 1)
                    for g, hh in GH:
                        b, r = at("inv0", d, g, hh)
                        dve.wait_ge(free[b], r + 1)
                        level(1, g, hh)
                    for lev in range(1, N_LEVELS):
                        for g, hh in GH:
                            for name, dst in (("invX", Dm), ("invXT", DT)):
                                if name == "invX" and lev == N_LEVELS - 1:
                                    continue
                                b, r = at(name, d, lev, g, hh)
                                dve.wait_ge(full[b], r + 1)
                                nc.vector.tensor_tensor(dst[:, g, hh, :, :], dst[:, g, hh, :, :],
                                                        bank[b][:, 0:TOK].rearrange("p (t n) -> p t n", t=TILES),
                                                        ALU.add).then_inc(free[b], 1)
                            if lev < N_LEVELS - 1:
                                level(lev + 1, g, hh)
                    for g, t in GT:
                        b, r = at("EF", d, g, t)
                        dve.wait_ge(full[b], r + 1)
                        ones2 = headones[:, :].unsqueeze(1).to_broadcast([P, 2, P])
                        eye2 = c.ident[:, :].unsqueeze(1).to_broadcast([P, 2, P])
                        link(nc.vector.tensor_tensor(ET[:, g, t, :, :], bank[b][:, 0:2 * P].rearrange("p (c n) -> p c n", c=2),
                                                     ones2, ALU.mult))
                        nc.vector.tensor_tensor(ET[:, g, t, :, :], ET[:, g, t, :, :], eye2, ALU.add)
                        for ch in range(2):
                            ins = nc.vector.scalar_tensor_tensor(F_at(g, t, ch), bank[b][:, (2 + ch) * P:(3 + ch) * P],
                                                                 decayC[:, g, 2 * t + ch:2 * t + ch + 1], headones[:, :],
                                                                 ALU.mult, ALU.mult)
                        ins.then_inc(free[b], 1)
                    for g, t in GT:
                        b, r = at("QZ", d, g, t)
                        dve.wait_ge(full[b], r + 1)
                        nc.vector.tensor_tensor(QT[:, g, t, :], bank[b][:, 0:P], AR[:, g, 1, tile_cols(t)], ALU.add)
                        if d == 0:
                            ins = nc.vector.tensor_copy(y[:, g, tile_cols(t)], bank[b][:, P:2 * P])
                        else:
                            ins = nc.vector.tensor_tensor(y[:, g, tile_cols(t)], y[:, g, tile_cols(t)], bank[b][:, P:2 * P], ALU.add)
                        ins.then_inc(free[b], 1)
                    for g in range(2):
                        t0, ch0 = divmod(chunks[d, 0][0], 2)
                        dve.wait_ge(free[at("EF", d, g, t0)[0]], at("EF", d, g, t0)[1] + 1)
                        nc.vector.tensor_copy(state_at(g, 0, 1), F_at(g, t0, ch0)).then_inc(S["seeded"], 1)
                    for g, t in GT:
                        b, r = at("QZ", d, g, t)
                        dve.wait_ge(free[b], r + 1)
                    for s_, step in scans:
                        chunk = chunks[d, s_][step]
                        t, ch = divmod(chunk, 2)
                        for g in range(2):
                            b, r = at("scan", d, s_, step, g)
                            dve.wait_ge(full[b], r + 1)
                            ycols = slice(chunk * CHUNK, (chunk + 1) * CHUNK)
                            ins = None
                            if step < len(chunks[d, s_]) - 1 or s_ == 0:
                                ins = nc.vector.scalar_tensor_tensor(state_at(g, s_, step + 1), bank[b][:, CHUNK:CHUNK + P],
                                                                     decayC[:, g, chunk:chunk + 1], F_at(g, t, ch), ALU.mult, ALU.add)
                            if s_ == 0:
                                ins.then_inc(S["state_out"], 1)
                            nc.vector.tensor_tensor(y[:, g, ycols], y[:, g, ycols], bank[b][:, 0:CHUNK], ALU.add).then_inc(free[b], 1)
                    for g in range(2):
                        b, r = at("scan", d, 1, 3, g)
                        dve.wait_ge(free[b], r + 1)
                    if d == 0:
                        dve.wait_ge(S["states"], 64)
                for g in range(2):
                    ins = nc.vector.scalar_tensor_tensor(t_inc[:, g, :], kdsum[:, g, :], cols[:, C_RK + g:C_RK + g + 1],
                                                         r_[:, g, :], ALU.mult, ALU.mult)
                ins.then_inc(S["sums_in"], 1)
                for g in range(2):
                    b, r = at("bonus", g)
                    dve.wait_ge(full[b], r + 1)
                    nc.vector.tensor_tensor(t_inv[:, g, :], bank[b][:, 0:TOK], v_[:, g, :], ALU.mult).then_inc(free[b], 1)
                for g in range(2):
                    b, r = at("mean", g)
                    dve.wait_ge(full[b], r + 1)
                    nc.vector.scalar_tensor_tensor(y[:, g, :], bank[b][:, 0:TOK], -1.0 / HD, y[:, g, :], ALU.mult, ALU.add).then_inc(free[b], 1)
                for g in range(2):
                    b, r = at("mean", g)
                    dve.wait_ge(free[b], r + 1)
                nc.vector.tensor_tensor(t_inc, y[:, :, :], y[:, :, :], ALU.mult).then_inc(S["centred"], 1)
                for g in range(2):
                    b, r = at("var", g)
                    dve.wait_ge(full[b], r + 1)
                    ins = nc.vector.tensor_scalar(t_exc[:, g, :], bank[b][:, 0:TOK], 1.0 / HD, LNX_EPS, ALU.mult, ALU.add)
                    ins.then_inc(free[b], 1)
                dve.wait_ge(S["var_root"], 1)
                link(nc.vector.reciprocal(t_exc, t_exc))
                link(nc.vector.tensor_tensor(y[:, :, :], y[:, :, :], t_exc, ALU.mult))
                for g in range(2):
                    ins = nc.vector.tensor_scalar(y[:, g, :], y[:, g, :], cols[:, C_LG + g:C_LG + g + 1],
                                                  cols[:, C_LB + g:C_LB + g + 1], ALU.mult, ALU.add)
                link(ins)
                link(nc.vector.tensor_tensor(y[:, :, :], y[:, :, :], t_inv, ALU.add))
                for g in range(2):
                    b, r = at("gate", g)
                    dve.wait_ge(free[b], r + 1)
                nc.vector.tensor_tensor(mixT[:, 4:6, :], y[:, :, :], gate[:, :, :], ALU.mult)

            @block.tensor
            def _(pe):
                mm, tr = nc.tensor.matmul, nc.tensor.transpose
                pe.wait_ge(S["params_in"], 16 * 7)
                pe.wait_ge(S["squashed"], 2)
                for name, base in (("decay", 0), ("rate", 2 * RANK)):
                    for d in range(2):
                        rows = slice(base + RANK * d, base + RANK * d + RANK)
                        for g in range(2):
                            b, r = at(name, d, g)
                            pe.wait_ge(free[b], r)
                            mm(bank[b][:, 0:TOK], w_up[rows, g * P:(g + 1) * P], pT[rows, WAB, :], start=True, stop=True).then_inc(full[b], 1)
                for g in range(2):
                    b, r = at("gate", g)
                    pe.wait_ge(free[b], r)
                    mm(bank[b][:, 0:TOK], g_up[:, g * P:(g + 1) * P], pT[0:HD, GB, :], start=True, stop=True).then_inc(full[b], 1)
                pe.wait_ge(S["kk2_in"], 1)
                for g in range(2):
                    b, r = at("kk2", g)
                    pe.wait_ge(free[b], r)
                    mm(bank[b][:, 0:TOK], headones[:, :], t_inc[:, g, :], start=True, stop=True).then_inc(full[b], 1)
                for g in range(2):
                    b, r = at("vT", g)
                    pe.wait_ge(free[b], r)
                    for t in range(TILES):
                        ins = tr(bank[b][:, tile_cols(t)], v_[:, g, tile_cols(t)], c.ident[:, :])
                    ins.then_inc(full[b], 1)
                for g in range(2):
                    pe.wait_ge(free[at("vT", g)[0]], at("vT", g)[1] + 1)
                for d in range(2):
                    pe.wait_ge(S["chunk_ops"], d + 1)
                    for g, t in GT:
                        b, r = at("tokens", d, g, t)
                        pe.wait_ge(free[b], r)
                        for i, src in enumerate((AR[:, g, 0, tile_cols(t)], Bf[:, g, tile_cols(t)], Kf[:, g, tile_cols(t)])):
                            ins = tr(bank[b][:, tile_cols(i)], src, c.ident[:, :])
                        ins.then_inc(full[b], 1)
                        for hh in range(2):
                            b, r = at("gram", d, g, t, hh)
                            pe.wait_ge(free[b], r)
                            rows = slice(HD * hh, HD * hh + HD)
                            for i, src in enumerate((Bf, Kf)):
                                ins = mm(bank[b][:, 2 * i * P:2 * (i + 1) * P].rearrange("p (w n) -> p w n", w=2),
                                         src[rows, g, tile_cols(t)], AR[rows, g, :, tile_cols(t)], start=True, stop=True)
                            ins.then_inc(full[b], 1)
                    lv = lambda lev, g, hh: 4 * (d * N_LEVELS + lev) + 2 * g + hh + 1
                    for g, hh in GH:
                        b, r = at("inv0", d, g, hh)
                        pe.wait_ge(S["levelled"], lv(0, g, hh))
                        pe.wait_ge(free[b], r)
                        for t in range(TILES):
                            ins = tr(bank[b][:, tile_cols(t)], Ak[:, g, hh, t, :], c.ident[:, :])
                        ins.then_inc(full[b], 1)
                    for lev in range(1, N_LEVELS):
                        for g, hh in GH:
                            b, r = at("invY", d, lev, g, hh)
                            pe.wait_ge(S["levelled"], lv(lev, g, hh))
                            pe.wait_ge(free[b], r)
                            for t in range(TILES):
                                ins = mm(bank[b][:, tile_cols(t)], Ak[:, g, hh, t, :], Dm[:, g, hh, t, :], start=True, stop=True)
                            ins.then_inc(full[b], 1)
                        for g, hh in GH:
                            yb, yr = at("invY", d, lev, g, hh)
                            pe.wait_ge(free[yb], yr + 1)
                            for name in ("invX", "invXT"):
                                if name == "invX" and lev == N_LEVELS - 1:
                                    continue
                                b, r = at(name, d, lev, g, hh)
                                pe.wait_ge(free[b], r)
                                for t in range(TILES):
                                    Yt, Dt = Ym[:, g, hh, t, :], DT[:, g, hh, t, :]
                                    ins = mm(bank[b][:, tile_cols(t)], *((Dt, Yt) if name == "invX" else (Yt, Dt)), start=True, stop=True)
                                ins.then_inc(full[b], 1)
                    for g, hh in GH:
                        b, r = at("invXT", d, N_LEVELS - 1, g, hh)
                        pe.wait_ge(free[b], r + 1)
                    for g, t in GT:
                        b, r = at("tokens", d, g, t)
                        pe.wait_ge(free[b], r + 1)
                        b, r = at("GW", d, g, t)
                        pe.wait_ge(free[b], r)
                        for hh in range(2):
                            h0 = HD * hh
                            mm(bank[b][:, h0:h0 + HD], DT[:, g, hh, t, :], A_tok[:, g, t, h0:h0 + HD], start=True, stop=True)
                            ins = mm(bank[b][:, P + h0:P + h0 + HD], M[:, g, hh, t, 2, :], v_tok[:, t, g * P + h0:g * P + h0 + HD],
                                     start=True, stop=True)
                        ins.then_inc(full[b], 1)
                    for g, t in GT:
                        b, r = at("GW", d, g, t)
                        pe.wait_ge(free[b], r + 1)
                        b, r = at("H", d, g, t)
                        pe.wait_ge(free[b], r)
                        for hh in range(2):
                            h0 = HD * hh
                            ins = mm(bank[b][:, h0:h0 + HD], DT[:, g, hh, t, :], GW[:, g, t, P + h0:P + h0 + HD], start=True, stop=True)
                        ins.then_inc(full[b], 1)
                    for g, t in GT:
                        b, r = at("H", d, g, t)
                        pe.wait_ge(free[b], r + 1)
                        b, r = at("EF", d, g, t)
                        pe.wait_ge(free[b], r)
                        mm(bank[b][:, 0:2 * P], GW[:, g, t, 0:P], BK_tok[:, g, t, 0, :, :].rearrange("p c n -> p (c n)"), start=True, stop=True)
                        for ch in range(2):
                            out = bank[b][:, (2 + ch) * P:(3 + ch) * P]
                            mm(out, BK_tok[:, g, t, 0, ch, :], H[:, g, t, :], start=True, stop=False)
                            ins = mm(out, BK_tok[:, g, t, 1, ch, :], v_tok[:, t, g * P:(g + 1) * P], start=False, stop=True)
                        ins.then_inc(full[b], 1)
                    for g, t in GT:
                        b, r = at("QZ", d, g, t)
                        pe.wait_ge(free[b], r)
                        for hh in range(2):
                            rows = slice(HD * hh, HD * hh + HD)
                            mm(bank[b][rows, 0:P], GW[:, g, t, rows], M[:, g, hh, t, 1, :], start=True, stop=True)
                        for hh in range(2):
                            rows = slice(HD * hh, HD * hh + HD)
                            mm(bank[b][rows, P:2 * P], H[:, g, t, rows], M[:, g, hh, t, 1, :], start=True, stop=False)
                            ins = mm(bank[b][rows, P:2 * P], v_tok[:, t, g * P + HD * hh:g * P + HD * hh + HD],
                                     M[:, g, hh, t, 3, :], start=False, stop=True)
                        ins.then_inc(full[b], 1)
                    pe.wait_ge(S["states_in"], 16 * 8)
                    pe.wait_ge(S["seeded"], 2 * (d + 1))
                    for g, t in GT:
                        b, r = at("QZ", d, g, t)
                        pe.wait_ge(free[b], r + 1)
                    for s_, step in scans:
                        chunk = chunks[d, s_][step]
                        t, ch = divmod(chunk, 2)
                        for g in range(2):
                            if step > 0 and (s_, step) != (0, 1):
                                pb, pr = at("scan", d, s_, step - 1, g)
                                pe.wait_ge(free[pb], pr + 1)
                            S_in = s_init[:, d, g, :] if step == 0 else state_at(g, s_, step)
                            b, r = at("scan", d, s_, step, g)
                            pe.wait_ge(free[b], r)
                            ins = mm(bank[b][:, 0:CHUNK], S_in, QT[:, g, t, ch * CHUNK:(ch + 1) * CHUNK], start=True, stop=True)
                            if step < len(chunks[d, s_]) - 1 or s_ == 0:
                                ins = mm(bank[b][:, CHUNK:CHUNK + P], ET[:, g, t, ch, :], S_in, start=True, stop=True)
                            ins.then_inc(full[b], 1)
                pe.wait_ge(S["sums_in"], 1)
                for name, src in (("bonus", t_inc), ("mean", y), ("var", t_inc)):
                    if name == "var":
                        pe.wait_ge(S["centred"], 1)
                    for g in range(2):
                        b, r = at(name, g)
                        pe.wait_ge(free[b], r)
                        mm(bank[b][:, 0:TOK], headones[:, :], src[:, g, :], start=True, stop=True).then_inc(full[b], 1)
        clear(nc, s.sems)


def output(c, l, mixT):
    nc, dram = c.nc, c.dram
    turns = [("out", n, t) for n in range(N_POUT) for t in range(TILES)]
    NW = PIECE // KD
    with ExitStack() as ctx:
        s = Stage(c, ctx, "output", turns, ["w_high", "w_low", "h_high", "h_low", "x_in", "vdone", "var_ready", "std_ready", "normed", "stored"])
        at, bank, full, free, S = s.steps.at, s.bank, s.full, s.free, s.named
        x, part, gates, gb = s.sb("x", [P, TILES, D]), s.sb("part", [P, TILES, D]), s.sb("gates", [P, 2, D]), s.sb("gb", [P, 2, D])
        stats, mv, rstd = s.sb("stats", [P, TILES, 12]), s.sb("mv", [P, TILES, 2]), s.sb("rstd", [P, TILES])
        hs, ws = s.sb("hs", [P, 2, KD, TOK], F32R), s.sb("ws", [P, 2, 2, PIECE], F32R)
        with nc.Block() as block:

            @block.sync
            def _(sp):
                refill(c, s, sp, l, AT_OUT, N_POUT)

            @block.scalar
            def _(act):
                load_for_norm(c, l, act, S["x_in"], (x, gates, gb), 0, "ln1")
                split_high(c, s, act, AT_OUT, 0, ws)
                split_rows_high(c, s, act, mixT, hs, lambda t: [])
                split_high(c, s, act, AT_OUT, 1, ws)
                for m in range(2, N_POUT):
                    split_high(c, s, act, AT_OUT, m, ws, at("out", m - 2, TILES - 1))
                for t in range(TILES):
                    act.wait_ge(S["var_ready"], t + 1)
                    nc.scalar.activation(rstd[:, t:t + 1], mv[:, t, 1:2], ACT.Sqrt).then_inc(S["std_ready"], 1)
                for t in range(TILES):
                    act.wait_ge(S["normed"], t + 1)
                    act.dma_start(c.x_dram[t], x[:, t, :]).then_inc(S["stored"], 16)
                act.wait_ge(S["stored"], 16 * TILES)

            @block.vector
            def _(dve):
                link = in_order(dve, S["vdone"])
                split_low(c, s, dve, AT_OUT, 0, ws)
                split_rows_low(c, s, dve, mixT, hs)
                split_low(c, s, dve, AT_OUT, 1, ws)
                dve.wait_ge(S["x_in"], 16 * LOADS_FOR_NORM)
                for n in range(N_POUT):
                    if n >= 1 and n + 1 < N_POUT:
                        split_low(c, s, dve, AT_OUT, n + 1, ws)
                    for t in range(TILES):
                        b, r = at("out", n, t)
                        cols = slice(n * NW, (n + 1) * NW)
                        dve.wait_ge(full[b], r + 1)
                        nc.vector.tensor_tensor(part[:, t, cols], bank[b][:, 0:NW], gates[:, SEQ_OF_TILE[t], cols], ALU.mult).then_inc(free[b], 1)
                for n in range(N_POUT - 3, N_POUT):
                    for t in range(TILES):
                        b, r = at("out", n, t)
                        dve.wait_ge(free[b], r + 1)
                for t in range(TILES):
                    link(nc.vector.scalar_tensor_tensor(x[:, t, :], x[:, t, :], ALPHA, part[:, t, :], ALU.mult, ALU.add))
                    norm_steps(nc, dve, link, x[:, t, :], stats[:, t, :], mv[:, t, :], rstd[:, t:t + 1], S["var_ready"],
                               S["std_ready"], t + 1, gb[:, 0, :], gb[:, 1, :], x[:, t, :]).then_inc(S["normed"], 1)

            @block.tensor
            def _(pe):
                for n in range(N_POUT):
                    pe.wait_ge(S["w_low"], n + 1)
                    w = ws[:, n % 2].rearrange("p s (k n) -> p s k n", k=KD)
                    for t in range(TILES):
                        b, r = at("out", n, t)
                        pe.wait_ge(free[b], r)
                        if n == 0:
                            pe.wait_ge(S["h_low"], t + 1)
                        for k in range(KD):
                            for i, (v, a) in enumerate(PASSES):
                                ins = nc.tensor.matmul(bank[b][:, 0:NW], hs[:, v, k, t * P:(t + 1) * P], w[:, a, k, :],
                                                       start=(k == 0 and i == 0), stop=(k == KD - 1 and i == 2))
                        ins.then_inc(full[b], 1)
        clear(nc, s.sems)


LOADS_FOR_NORM = TILES + 4
NORM_IN = LOADS_FOR_NORM * D


def norm_inputs(buffer):
    view = lambda at, n: buffer[:, at * D:(at + n) * D].rearrange("p (t n) -> p t n", t=n)
    return view(0, TILES), view(TILES, 2), view(TILES + 2, 2)


def load_for_norm(c, l, eng, loaded, views, which, name):
    x, gates, gb = views
    for t in range(TILES):
        eng.dma_start(x[:, t, :], c.x_dram[t]).then_inc(loaded, 16)
    for i in range(2):
        gate = c.gate_dram[bass.ds(l, 1), which, i]
        eng.dma_start(gates[:, i, :], gate.rearrange("a n -> (a n)").partition_broadcast(P)).then_inc(loaded, 16)
    for i in range(2):
        eng.dma_start(gb[:, i, :], layer_row(c.dram[name], l)[i].partition_broadcast(P)).then_inc(loaded, 16)


SHORT = 4
LONG_ROWS = SHORT * TOPK
CAND = LONG_ROWS + (TOPK - SHORT) * SHORT


def routing(c, l, xs, route):
    nc, dram = c.nc, c.dram
    HP = 2 * PH
    turns = [("xT", t, h) for t in range(TILES) for h in range(2)] + [("q", n) for n in range(HP)]
    turns += [("sc", t, n) for t in range(TILES) for n in range(HP // 4)]
    PART = (10, 20, N_ADA)
    for t in range(TILES):
        turns += [("ada", n) for n in range(PART[t - 1] if t else 0, PART[t])] + [("route", t)]
    turns += [("cols",)]
    with ExitStack() as ctx:
        s = Stage(c, ctx, "route", turns, ["w_high", "w_low", "h_high", "h_low", "counted", "multiplied", "bias_in", "gates_stored", "keys_in", "vdone", "normed", "exp_asked", "exps", "routed", "split"])
        at, bank, full, free, S = s.steps.at, s.bank, s.full, s.free, s.named
        x_in = [s.sem(f"x_in{t}") for t in range(TILES)]
        rows_mod = s.sb("rows_mod", [2, 6 * D])
        hT, ws = s.sb("hT", [P, KD, TOK]), s.sb("ws", [P, 2, 2, PIECE], F32R)
        qT, keys, sc = s.sb("qT", [P, HP, TOK]), s.sb("keys", [P, HP, NK]), s.sb("sc", [P, HP, TILES, NK])
        top, idx, idxf = s.sb("top", [P, HP, TOPK]), s.sb("idx", [P, HP, TOPK], U32), s.sb("idxf", [P, HP, TOPK])
        spares, used = hT[:, :, :].rearrange("p k n -> p (k n)"), [0]

        def spare(n):
            used[0] += n
            return spares[:, used[0] - n:used[0]]

        cand = spare(PH * CAND).rearrange("p (h n) -> p h n", h=PH)
        best, pos = s.sb("best", [P, PH, TOPK]), s.sb("pos", [P, PH, TOPK], U32)
        shifted = s.sb("shifted", [P, 2, PH * TOPK], U32)
        place = spare(2 * PH * TOPK).rearrange("p (w k) -> p w k", w=2)
        posf, start = spare(PH * TOPK), spare(PH * TOPK)
        iota16 = s.sb("iota16", [P, TOPK])
        pick = s.sb("pick", [P, 2, PH * TOPK, TOPK])
        x = pick[:, :, :, :].rearrange("p w k a -> p (w k a)")[:, 0:TILES * D].rearrange("p (t n) -> p t n", t=TILES)
        chosen = spare(3 * PH * TOPK).rearrange("p (w k) -> p w k", w=3)
        rows = s.sb("rows", [P, 2, PH])
        rest, gT = spare(TOK), spare(TOK)

        def picks(w):
            return pick[:, w, :, :].rearrange("p (h k) a -> p h k a", h=PH)

        def tables(w):
            found = idxf[:, :, :].rearrange("p (h two) k -> p h two k", two=2)[:, :, w, :]
            return found.unsqueeze(2).to_broadcast([P, PH, TOPK, TOPK])

        with nc.Block() as block:

            @block.gpsimd
            def _(pool):
                for t in range(TILES):
                    pool.wait_ge(S["counted"], t + 1)
                    nc.gpsimd.tensor_tensor(picks(0), picks(0), tables(0), ALU.mult).then_inc(S["multiplied"], 1)

            @block.sync
            def _(sp):
                refill(c, s, sp, l, AT_Q, N_PQ)
                for n in range(AT_ADA + SLOTS, AT_EXP + SLOTS):
                    b, r = at("ada", n - SLOTS - AT_ADA)
                    sp.wait_ge(full[b], r + 1)
                    fill_slot(c, sp, l, n)

            @block.scalar
            def _(act):
                for t in range(TILES):
                    act.dma_start(x[:, t, :], c.x_dram[t]).then_inc(x_in[t], 16)
                act.dma_start(rows_mod[0:1, :], dram["b_ada"][NEXT:NEXT + 1]).then_inc(S["bias_in"], 16)
                act.dma_start(keys[:, :, :], layer_row(dram["subkeys_T"], l)).then_inc(S["keys_in"], 16)
                act.dma_start(iota16[:, :], dram["iota16"]).then_inc(S["keys_in"], 16)
                for m in range(2):
                    split_high(c, s, act, AT_Q, m, ws)
                split_rows_high(c, s, act, hT, xs, lambda t: [at("xT", t, h) for h in range(2)])
                for n in range(HP):
                    b, r = at("q", n)
                    act.wait_ge(full[b], r + 1)
                    nc.scalar.copy(qT[:, n, :], bank[b][:, 0:TOK]).then_inc(free[b], 1)
                    if n % 2 == 1 and n // 2 + 2 < N_PQ:
                        split_high(c, s, act, AT_Q, n // 2 + 2, ws, at("q", n))
                for t in range(TILES):
                    for n in range(HP // 4):
                        b, r = at("sc", t, n)
                        act.wait_ge(full[b], r + 1)
                        nc.scalar.copy(sc[:, 4 * n:4 * n + 4, t, :], bank[b][:, :].rearrange("p (h n) -> p h n", h=4)).then_inc(free[b], 1)
                for t in range(TILES):
                    for n in range(PART[t - 1] if t else 0, PART[t]):
                        ada_copy(c, s, act, rows_mod, n)
                    act.wait_ge(S["exp_asked"], t + 1)
                    nc.scalar.activation(chosen[:, 2, :], chosen[:, 2, :], ACT.Exp).then_inc(S["exps"], 1)
                    b, r = at("route", t)
                    act.wait_ge(full[b], r + 1)
                    cols = slice(t * P, (t + 1) * P)
                    nc.scalar.copy(route[:, 0:2, cols], bank[b][:, 0:2 * P].rearrange("p (w n) -> p w n", w=2))
                    nc.scalar.copy(gT[:, cols], bank[b][:, 2 * P:3 * P]).then_inc(free[b], 1)
                store_gates(c, s, act, rows_mod, c.gate_dram[bass.ds(l + 1, 1)].rearrange("a i s n -> (a i) s n"), S["gates_stored"])

            @block.vector
            def _(dve):
                link = in_order(dve, S["vdone"])
                V = nc.vector
                for m in range(2):
                    split_low(c, s, dve, AT_Q, m, ws)
                modulate(c, s, dve, 1, hT)
                split_rows_low(c, s, dve, hT, xs)
                for m in range(2, N_PQ):
                    split_low(c, s, dve, AT_Q, m, ws)
                dve.wait_ge(S["keys_in"], 32)
                dve.wait_ge(S["h_low"], TILES)
                for t in range(TILES):
                    for n in range(HP // 4):
                        b, r = at("sc", t, n)
                        dve.wait_ge(free[b], r + 1)
                    for r8 in range(2):
                        part = slice(8 * r8, 8 * r8 + 8)
                        for n in range(HP):
                            ins = V.max(top[:, n, part], sc[:, n, t, :])
                        link(ins)
                        for n in range(HP):
                            ins = V.max_index(idx[:, n, part], top[:, n, part], sc[:, n, t, :])
                        if r8 == 0:
                            for n in range(HP):
                                ins = V.match_replace(sc[:, n, t, :], top[:, n, part], sc[:, n, t, :], NEG)
                        link(ins)
                    V.tensor_copy(idxf[:, :, :], idx[:, :, :])
                    tops = top[:, :, :].rearrange("p (h two) k -> p h two k", two=2)
                    half0, half1, long = tops[:, :, 0, :], tops[:, :, 1, :], [P, PH, SHORT, TOPK]
                    V.tensor_tensor(cand[:, :, 0:LONG_ROWS].rearrange("p h (a b) -> p h a b", a=SHORT),
                                    half0[:, :, 0:SHORT].unsqueeze(3).to_broadcast(long),
                                    half1.unsqueeze(2).to_broadcast(long), ALU.add)
                    short = [P, PH, TOPK - SHORT, SHORT]
                    ins = V.tensor_tensor(cand[:, :, LONG_ROWS:CAND].rearrange("p h (a b) -> p h a b", b=SHORT),
                                          half0[:, :, SHORT:TOPK].unsqueeze(3).to_broadcast(short),
                                          half1[:, :, 0:SHORT].unsqueeze(2).to_broadcast(short), ALU.add)
                    link(ins)
                    for r8 in range(2):
                        part = slice(8 * r8, 8 * r8 + 8)
                        for h in range(PH):
                            ins = V.max(best[:, h, part], cand[:, h, :])
                        link(ins)
                        for h in range(PH):
                            ins = V.max_index(pos[:, h, part], best[:, h, part], cand[:, h, :])
                        if r8 == 0:
                            for h in range(PH):
                                ins = V.match_replace(cand[:, h, :], best[:, h, part], cand[:, h, :], NEG)
                        link(ins)
                    flat = pos[:, :, :].rearrange("p h k -> p (h k)")
                    V.tensor_copy(posf[:, :], flat)
                    V.tensor_scalar(shifted[:, 0, :], flat, 4, None, ALU.logical_shift_right)
                    link(V.tensor_scalar(shifted[:, 1, :], flat, 2, None, ALU.logical_shift_right))
                    link(V.tensor_copy(place[:, :, :], shifted[:, :, :]))
                    link(V.scalar_tensor_tensor(place[:, 0, :], place[:, 1, :], float(LONG_ROWS // SHORT - SHORT), place[:, 0, :],
                                                ALU.subtract, ALU.max))
                    link(V.tensor_scalar(start[:, :], place[:, 0, :], float(SHORT), float(LONG_ROWS - SHORT * SHORT), ALU.mult, ALU.add))
                    link(V.scalar_tensor_tensor(start[:, :], place[:, 0, :], float(TOPK), start[:, :], ALU.mult, ALU.min))
                    if t > 0:
                        b, r = at("route", t - 1)
                        dve.wait_ge(full[b], r + 1)
                    link(V.tensor_tensor(place[:, 1, :], posf[:, :], start[:, :], ALU.subtract))
                    numbers = iota16[:, :].unsqueeze(1).to_broadcast([P, PH * TOPK, TOPK])
                    for w in range(2):
                        ins = V.tensor_tensor(pick[:, w, :, :], place[:, w, :].unsqueeze(2).to_broadcast([P, PH * TOPK, TOPK]),
                                              numbers, ALU.is_equal)
                        if w == 0:
                            ins.then_inc(S["counted"], 1)
                    link(ins)
                    link(V.tensor_tensor(picks(1), picks(1), tables(1), ALU.mult))
                    V.tensor_reduce(chosen[:, 1, :], pick[:, 1, :, :], AX.X, ALU.add)
                    dve.wait_ge(S["multiplied"], t + 1)
                    V.tensor_reduce(chosen[:, 0, :], pick[:, 0, :, :], AX.X, ALU.add)
                    c3 = chosen[:, 2, :].rearrange("p (h k) -> p h k", h=PH)
                    V.tensor_tensor(c3, best[:, :, :], best[:, :, 0:1].to_broadcast([P, PH, TOPK]),
                                    ALU.subtract).then_inc(S["exp_asked"], 1)
                    dve.wait_ge(S["exps"], t + 1)
                    link(V.tensor_reduce(rows[:, 0, :], c3, AX.X, ALU.add))
                    link(V.reciprocal(rows[:, 1, :], rows[:, 0, :]))
                    V.tensor_tensor(c3, c3, rows[:, 1, :].unsqueeze(2).to_broadcast([P, PH, TOPK]), ALU.mult).then_inc(S["routed"], 1)
                for t in range(TILES):
                    b, r = at("route", t)
                    dve.wait_ge(free[b], r + 1)
                link(V.tensor_copy(route[:, 2, :], gT[:, :]))
                link(V.tensor_tensor(rest[:, :], gT[:, :], route[:, 2, :], ALU.subtract))
                link(V.tensor_copy(route[:, 3, :], rest[:, :]))
                V.tensor_tensor(route[:, 4, :], rest[:, :], route[:, 3, :], ALU.subtract)
                ada_columns(c, s, dve)

            @block.tensor
            def _(pe):
                transpose_x(c, s, pe, x, x_in)
                pe.wait_ge(S["h_low"], TILES)
                for n in range(HP):
                    weight_blocks_times_h(c, s, pe, n, at("q", n), ws, xs)
                pe.wait_ge(S["keys_in"], 32)
                for n in range(HP):
                    b, r = at("q", n)
                    pe.wait_ge(free[b], r + 1)
                for t in range(TILES):
                    for n in range(HP // 4):
                        b, r = at("sc", t, n)
                        pe.wait_ge(free[b], r)
                        for i in range(4):
                            ins = nc.tensor.matmul(bank[b][:, i * P:(i + 1) * P], qT[:, 4 * n + i, t * P:(t + 1) * P],
                                                   keys[:, 4 * n + i, :], start=True, stop=True)
                        ins.then_inc(full[b], 1)
                pe.wait_ge(S["bias_in"], 16)
                for t in range(TILES):
                    for n in range(PART[t - 1] if t else 0, PART[t]):
                        m = AT_ADA + n
                        ada_product(c, s, pe, rows_mod, c.ring_full[slot(m)], filled(m), slot(m), n)
                    b, r = at("route", t)
                    pe.wait_ge(S["routed"], t + 1)
                    pe.wait_ge(free[b], r)
                    for w in range(3):
                        ins = nc.tensor.transpose(bank[b][:, w * P:(w + 1) * P], chosen[:, w, :], c.ident[:, :])
                    ins.then_inc(full[b], 1)
                ada_transposes(c, s, pe, rows_mod)
        clear(nc, s.sems)


def experts(c, l, xs, route, acc, W, late):
    nc, dram = c.nc, c.dram
    STEPS = NK
    BT = TOK // JG
    UN = 4
    with ExitStack() as ctx:
        sem = lambda name: ctx.enter_context(nc.semaphore("exp_" + name))
        sb = lambda name, shape, dt=F32: ctx.enter_context(nc.sbuf_tensor("exp_" + name, shape, dt))
        Us, Vs = sb("Us", [P, 2, 2, D], F32R), sb("Vs", [P, 2, D], F32R)
        gel, wa = sb("gelu", [P, TOK]), sb("wa", [P, TOK])
        was = sb("was", [P, 2, 2, TOK], F32R)
        Ai, Bj = sb("Ai", [P, 2, BT, NK], BF16), sb("Bj", [P, 2, 4, BT, JG], BF16)
        iota = sb("iota", [P, NK + JG], BF16)
        act_bank = ctx.enter_context(nc.psum_tensor("exp_act", [P, 512], F32))
        w_bank = ctx.enter_context(nc.psum_tensor("exp_w", [P, 512], F32))
        iota_in, zeroed = sem("iota_in"), sem("zeroed")
        u_hi, u_lo, v_hi, v_lo = sem("u_hi"), sem("u_lo"), sem("v_hi"), sem("v_lo")
        act_done, acc_done, w_done = sem("act_done"), sem("acc_done"), sem("w_done")
        gelu_done, wa_done, wa_hi, wa_lo = sem("gelu_done"), sem("wa_done"), sem("wa_hi"), sem("wa_lo")
        ai_ready, bj_hot, bj_ready, w_stored = sem("ai_ready"), sem("bj_hot"), sem("bj_ready"), sem("w_stored")
        sems = [iota_in, zeroed, u_hi, u_lo, v_hi, v_lo, act_done, acc_done, w_done, gelu_done, wa_done, wa_hi, wa_lo,
                ai_ready, bj_hot, bj_ready, w_stored]
        U_PIECE, V_PIECE = (0, 2), (1, 3)

        def at_slot(q):
            return slot(AT_EXP + q)

        def have(q, it):
            return filled(AT_EXP + q) + 16 * it

        def part_of(q, u):
            return c.ring[:, at_slot(q), (u % 2) * D:(u % 2 + 1) * D]

        PER = JG // UN
        CHUNKS = STEPS // JG

        def main_loop(eng, body):
            for chunk in range(CHUNKS):
                with eng.Fori(0, PER - (chunk == CHUNKS - 1)) as it8:
                    for u in range(UN):
                        body(it8 + chunk * PER, it8, chunk, u, it8 * UN + (chunk * JG + u), False)
            for u in range(UN):
                body(STEPS // UN - 1, PER - 1, CHUNKS - 1, u, STEPS - UN + u, u == UN - 1)

        with nc.Block() as block:

            @block.sync
            def _(sp):
                sp.dma_start(iota[:, :], dram["iota"]).then_inc(iota_in, 16)
                with sp.Fori(1, STEPS // UN) as it:
                    for q in range(4):
                        steps_split = it * UN - UN + 2 * (q // 2 + 1)
                        if q % 2 == 0:
                            sp.wait_ge(u_lo, steps_split)
                        else:
                            sp.wait_ge(v_lo, steps_split * 2 + 1)
                        src = dram["uv"[q % 2]][bass.ds(l, 1), bass.ds(it * 2 + q // 2, 1)]
                        sp.dma_start(c.ring[:, at_slot(q), :], src.rearrange("a b p n -> (a b p) n")).then_inc(c.ring_full[at_slot(q)], 16)

            @block.gpsimd
            def _(pool):
                nc.gpsimd.memset(was[:, 1, :, :].bitcast(F32), 0.0).then_inc(zeroed, 1)
                nc.gpsimd.memset(Vs[:, :, :].bitcast(F32), 0.0).then_inc(zeroed, 1)

                def scale_one_hot(m, it8, u):
                    tok = it8 * (UN * BT) + u * BT
                    pool.wait_ge(bj_hot, m + 1)
                    for i in range(3):
                        ins = nc.gpsimd.tensor_tensor(Bj[:, u % 2, 1 + i, :, :], Bj[:, u % 2, 0, :, :],
                                                      route[:, 2 + i, bass.ds(tok, BT)].unsqueeze(2).to_broadcast([P, BT, JG]), ALU.mult)
                    ins.then_inc(bj_ready, 1)

                pool.sem_inc(v_lo, 1)
                with pool.Fori(0, JG // UN) as it8:
                    for u in range(UN):
                        scale_one_hot(it8 * UN + u, it8, u)

                def step(it, it8, chunk, u, j, last):
                    if chunk < CHUNKS - 1:
                        scale_one_hot(j + JG, it8, u)
                    q = V_PIECE[u // 2]
                    for h in range(2):
                        cols = slice(512 * h, 512 * h + 512)
                        pool.wait_ge(v_hi, 2 * j + (h + 1))
                        nc.gpsimd.tensor_tensor(Vs[:, 1, cols], part_of(q, u)[:, cols], Vs[:, 0, cols].bitcast(F32),
                                                ALU.subtract).then_inc(v_lo, 1)

                main_loop(pool, step)

            @block.scalar
            def _(act):
                def step(it, it8, chunk, u, j, last):
                    if isinstance(j, int) and j == STEPS - UN:
                        load_for_norm(c, l, act, c.late_in, late, 1, "ln2")
                    act.wait_ge(act_done, j + 3)
                    nc.scalar.activation(gel[:, :], act_bank[:, 0:TOK], ACT.Gelu_apprx_tanh).then_inc(gelu_done, 1)
                    act.wait_ge(wa_done, j + 1)
                    act.wait_ge(acc_done, 2 * j + 1)
                    nc.scalar.copy(was[:, u % 2, 0, :], wa[:, :]).then_inc(wa_hi, 1)
                    q = V_PIECE[u // 2]
                    act.wait_ge(c.ring_full[at_slot(q)], have(q, it))
                    for h in range(2):
                        cols = slice(512 * h, 512 * h + 512)
                        act.wait_ge(acc_done, 2 * j + (h + 2))
                        nc.scalar.copy(Vs[:, 0, cols], part_of(q, u)[:, cols]).then_inc(v_hi, 1)

                act.sem_inc(gelu_done, 1)
                with act.Fori(0, JG // UN) as it8:
                    for u in range(UN):
                        act.wait_ge(w_done, it8 * UN + (u + 3))
                        nc.scalar.copy(W[:, 0, bass.ds(it8 * (UN * BT) + u * BT, BT), :],
                                       w_bank[:, 0:BT * JG].rearrange("p (t n) -> p t n", t=BT)).then_inc(w_stored, 1)
                main_loop(act, step)

            @block.vector
            def _(dve):
                V = nc.vector

                def build_one_hot(m, it8, u, base):
                    tok = it8 * (UN * BT) + u * BT
                    numbers = iota[:, bass.ds(base, JG)].unsqueeze(1).to_broadcast([P, BT, JG])
                    dve.wait_ge(w_done, m + 1)
                    V.tensor_tensor(Bj[:, u % 2, 0, :, :], numbers,
                                    route[:, 1, bass.ds(tok, BT)].unsqueeze(2).to_broadcast([P, BT, JG]),
                                    ALU.is_equal).then_inc(bj_hot, 1)
                    for n in range(BT):
                        ins = V.tensor_scalar(Ai[:, u % 2, n, :], iota[:, 0:NK], route[:, 0, bass.ds(tok + n, 1)], None, ALU.is_equal)
                    ins.then_inc(ai_ready, 1)

                def store_w(m, it8, u, buf):
                    tok = it8 * (UN * BT) + u * BT
                    dve.wait_ge(w_done, m + 3)
                    V.tensor_copy(W[:, buf, bass.ds(tok, BT), :],
                                  w_bank[:, 0:BT * JG].rearrange("p (t n) -> p t n", t=BT)).then_inc(w_stored, 1)

                dve.sem_inc(wa_lo, 1)
                dve.sem_inc(w_stored, 1)
                dve.wait_ge(iota_in, 16)
                with dve.Fori(0, JG // UN) as it8:
                    for u in range(UN):
                        build_one_hot(it8 * UN + u, it8, u, 0)

                def split_u(it, u, j):
                    q = U_PIECE[u // 2]
                    dve.wait_ge(c.ring_full[at_slot(q)], have(q, it))
                    dve.wait_ge(act_done, j + 1)
                    V.tensor_copy(Us[:, u % 2, 0, :], part_of(q, u)).then_inc(u_hi, 1)
                    dve.wait_ge(u_hi, j + 1)
                    V.tensor_tensor(Us[:, u % 2, 1, :], part_of(q, u), Us[:, u % 2, 0, :].bitcast(F32),
                                    ALU.subtract).then_inc(u_lo, 1)

                def step(it, it8, chunk, u, j, last):
                    if chunk < CHUNKS - 1:
                        build_one_hot(j + JG, it8, u, (chunk + 1) * JG)
                    elif not last:
                        split_u(it + (u + 1) // UN, (u + 1) % UN, j + 1)
                    dve.wait_ge(gelu_done, j + 2)
                    dve.wait_ge(wa_lo, j + 1)
                    dve.wait_ge(w_stored, (chunk + 1) * JG + 1)
                    V.tensor_tensor(wa[:, :], gel[:, :], W[:, chunk % 2, :, bass.ds(it8 * UN + u, 1)].rearrange("p t a -> p (t a)"),
                                    ALU.mult).then_inc(wa_done, 1)
                    dve.wait_ge(wa_hi, j + 1)
                    V.tensor_tensor(was[:, u % 2, 1, :], wa[:, :], was[:, u % 2, 0, :].bitcast(F32), ALU.subtract).then_inc(wa_lo, 1)
                    if chunk < CHUNKS - 1:
                        split_u(it + (u + 1) // UN, (u + 1) % UN, j + 1)
                        store_w(j + JG, it8, u, 1 - chunk % 2)

                split_u(0, 0, 0)
                main_loop(dve, step)

            @block.tensor
            def _(pe):
                mm = nc.tensor.matmul

                def build_w(m, u):
                    pe.wait_ge(ai_ready, m + 1)
                    pe.wait_ge(bj_ready, m + 1)
                    pe.wait_ge(w_stored, m + 1)
                    for n in range(BT):
                        for i in range(3):
                            ins = mm(w_bank[:, n * JG:(n + 1) * JG], Ai[:, u % 2, n, :], Bj[:, u % 2, 1 + i, n, :],
                                     start=(i == 0), stop=(i == 2))
                    ins.then_inc(w_done, 1)

                def add_v(buf, first=False, last=False):
                    for h in range(2):
                        cols = slice(512 * h, 512 * h + 512)
                        for t in range(TILES):
                            tok = slice(t * P, (t + 1) * P)
                            for n, (a, v) in enumerate(((0, 0), (0, 1), (1, 0))):
                                ins = mm(acc[2 * t + h][:, :], was[:, buf, a, tok], Vs[:, v, cols],
                                         start=False, stop=last and n == 2)
                        ins.then_inc(acc_done, 1)

                pe.wait_ge(zeroed, 2)
                credits = [act_done, act_done, w_done, w_done, acc_done, None]
                for i, credit in enumerate(credits):
                    ins = mm(acc[i][:, :], was[:, 1, 0, 0:P], Vs[:, 0, 0:512], start=True, stop=False)
                    if credit is not None:
                        ins.then_inc(credit, 1)
                with pe.Fori(0, JG // UN) as it8:
                    for u in range(UN):
                        build_w(it8 * UN + u, u)

                def step(it, it8, chunk, u, j, last):
                    pe.wait_ge(u_lo, j + 1)
                    pe.wait_ge(gelu_done, j + 1)
                    for k in range(KD):
                        for n, (a, v) in enumerate(((0, 0), (0, 1), (1, 0))):
                            ins = mm(act_bank[:, 0:TOK], Us[:, u % 2, a, k * P:(k + 1) * P], xs[:, v, k, :],
                                     start=(k == 0 and n == 0), stop=(k == KD - 1 and n == 2))
                    ins.then_inc(act_done, 1)
                    pe.wait_ge(wa_lo, j + 1)
                    pe.wait_ge(v_lo, 2 * j + 1)
                    add_v((u + 1) % 2)
                    if chunk < CHUNKS - 1:
                        build_w(j + JG, u)

                main_loop(pe, step)
                pe.wait_ge(wa_lo, STEPS + 1)
                pe.wait_ge(v_lo, 2 * STEPS + 1)
                add_v(1, last=True)
        clear(nc, sems + c.ring_full)


def finish(c, l, acc, late):
    nc, dram = c.nc, c.dram
    with ExitStack() as ctx:
        sem = lambda name: ctx.enter_context(nc.semaphore("fin_" + name))
        sb = lambda name, shape, dt=F32: ctx.enter_context(nc.sbuf_tensor("fin_" + name, shape, dt))
        (x, gates, gb), x_in = late, c.late_in
        part = sb("part", [P, TILES, D])
        stats, mv, rstd = sb("stats", [P, TILES, 12]), sb("mv", [P, TILES, 2]), sb("rstd", [P, TILES])
        vdone, var_ready, std_ready, normed, stored = map(sem, ("vdone", "var_ready", "std_ready", "normed", "stored"))
        with nc.Block() as block:

            @block.scalar
            def _(act):
                for t in range(TILES):
                    act.wait_ge(var_ready, t + 1)
                    nc.scalar.activation(rstd[:, t:t + 1], mv[:, t, 1:2], ACT.Sqrt).then_inc(std_ready, 1)

            @block.sync
            def _(sp):
                for n in range(SLOTS):
                    fill_slot(c, sp, NEXT, n)
                for t in range(TILES):
                    sp.wait_ge(normed, t + 1)
                    sp.dma_start(c.x_dram[t], x[:, t, :]).then_inc(stored, 16)
                    sp.dma_start(dram["y"][t], x[:, t, :]).then_inc(stored, 16)
                sp.wait_ge(stored, 32 * TILES)

            @block.vector
            def _(dve):
                link = in_order(dve, vdone)
                dve.wait_ge(x_in, 16 * LOADS_FOR_NORM)
                for t in range(TILES):
                    for h in range(2):
                        cols = slice(512 * h, 512 * h + 512)
                        ins = nc.vector.tensor_tensor(part[:, t, cols], acc[2 * t + h][:, :], gates[:, SEQ_OF_TILE[t], cols], ALU.mult)
                    link(ins)
                    link(nc.vector.scalar_tensor_tensor(x[:, t, :], x[:, t, :], ALPHA, part[:, t, :], ALU.mult, ALU.add))
                    norm_steps(nc, dve, link, x[:, t, :], stats[:, t, :], mv[:, t, :], rstd[:, t:t + 1], var_ready,
                               std_ready, t + 1, gb[:, 0, :], gb[:, 1, :], x[:, t, :]).then_inc(normed, 1)
        clear(nc, [x_in, vdone, var_ready, std_ready, normed, stored])


def build(nc, dram):
    with ExitStack() as ctx:
        c = make_core(nc, ctx, dram)
        begin(c)
        with nc.Fori(0, DEPTH) as l:
            with ExitStack() as mid:
                pT = mid.enter_context(nc.sbuf_tensor("pT", [P, N_IN, TOK], F32))
                mixT = mid.enter_context(nc.sbuf_tensor("mixT", [P, KD, TOK], F32))
                project(c, l, pT)
                attention(c, l, pT, mixT)
                rwkv(c, l, pT, mixT)
                output(c, l, mixT)
            with ExitStack() as mid:
                xs = mid.enter_context(nc.sbuf_tensor("xs", [P, 2, KD, TOK], F32R))
                route = mid.enter_context(nc.sbuf_tensor("route", [P, 5, TOK], BF16))
                routing(c, l, xs, route)
                acc = [mid.enter_context(nc.psum_tensor(f"acc{i}", [P, 512], F32)) for i in range(6)]
                W = mid.enter_context(nc.sbuf_tensor("W", [P, 2, TOK, JG], F32))
                late = norm_inputs(W[:, 0].rearrange("p t n -> p (t n)"))
                experts(c, l, xs, route, acc, W, late)
                finish(c, l, acc, late)


def shape_constants():
    f = np.float32
    half = HD // 4
    freqs = (f(10000.0) ** (-np.arange(half, dtype=f) / f(half))).astype(f)
    t = np.arange(2 * P)
    cosT, sinT = np.zeros((HD, 2 * P), f), np.zeros((HD, 2 * P), f)
    rot = np.zeros((P, P), f)
    for axis, pos in enumerate((t // HD, t % HD)):
        ang = pos.astype(f)[None, :] * freqs[:, None]
        for part in range(2):
            lo = axis * 2 * half + part * half
            cosT[lo:lo + half], sinT[lo:lo + half] = np.cos(ang), np.sin(ang)
    for head in range(2):
        for axis in range(2):
            for i in range(half):
                a = head * HD + axis * 2 * half + i
                rot[a + half, a], rot[a, a + half] = -1.0, 1.0
    q, k = np.arange(P)[:, None], np.arange(2 * P)[None, :]
    mask = np.zeros((P, 2, 3 * P), f)
    for n in range(2):
        mask[:, n, P:] = np.where(np.abs(k - (q + n * P)) <= 128, 0.0, NEG)
    s_, t_ = np.arange(P)[:, None], np.arange(P)[None, :]
    same = (s_ // CHUNK) == (t_ // CHUNK)
    gram, level = np.zeros((P, 2, 4, P), f), np.zeros((P, 2, N_LEVELS, P), f)
    for d in range(2):
        before = (s_ < t_) if d == 0 else (s_ > t_)
        strict, incl = same & before, same & (before | (s_ == t_))
        gram[:, d, 0], gram[:, d, 1], gram[:, d, 2], gram[:, d, 3] = strict, incl, strict, incl
        for lev in range(N_LEVELS):
            level[:, d, lev] = before & ((s_ >> (lev + 1)) == (t_ >> (lev + 1))) & ((s_ >> lev) != (t_ >> lev))
    resets = np.ones((P, 2 * TOK), f)
    resets[:, ::CHUNK] = 0.0
    return {
        "ident": np.eye(P, dtype=f), "cosT": np.tile(cosT, (2, 1)), "sinT": np.tile(sinT, (2, 1)), "rotate": rot,
        "att_mask": mask, "gram_mask": gram.reshape(P, 2, 4 * P), "level_mask": level,
        "headones": (s_ // HD == t_ // HD).astype(f), "resets": resets,
        "iota16": np.tile(np.arange(TOPK, dtype=f), (P, 1)),
    }


def lay_out(i):
    L = DEPTH
    cat, tile = np.concatenate, np.ascontiguousarray

    def blocks(w, n):
        N = w.shape[2]
        per = PIECE // KD // n
        return tile(w.reshape(L, KD, P, N // n // per, per, n).transpose(0, 3, 2, 4, 1, 5)).reshape(L, -1, P, PIECE)

    def halves(a):
        a = a.reshape(L, -1, 2, P)
        return a.transpose(0, 3, 1, 2).reshape(L, P, -1)

    order = np.concatenate([np.r_[b * HD:(b + 1) * HD, (4 + b) * HD:(5 + b) * HD] for b in range(4)])
    w_in = cat([i["w_in"][:, :, order], i["w_in"][:, :, 512:]], axis=2)
    starts = [0, 128, 256, 384, 512, 640, 768, 896, 1024, 1152, 1280, 1408, 1536, 1664, 1728, 1856, 1984, 2112, 2240, 2368]
    w_in = cat([w_in[:, :, a:a + P] for a in starts], axis=2)
    w_out = cat([i["w_out"][:, order, :], i["w_out"][:, 512:, :]], axis=1)
    out = {
        "x_in": cat([i["x_prompt"].reshape(1, P, D), i["x_sample"].reshape(2, P, D)]),
        "ln_in": np.stack([i["ln_in_g"], i["ln_in_b"]]),
        "cond": tile(np.stack([i["c_ctx"], i["c"][0]]).reshape(2, KD, P).transpose(2, 1, 0)),
        "b_ada": i["b_ada"],
        "w_ada": blocks(i["w_ada"], PIECE // KD), "w_in": blocks(w_in, P), "w_out": blocks(w_out, PIECE // KD),
        "wq": blocks(i["peer_wq"], P),
        "u": tile(i["peer_u"].reshape(L, P, NK // 2, 2, KD, P).transpose(0, 2, 5, 3, 4, 1)).reshape(L, NK // 2, P, PIECE),
        "v": tile(i["peer_v"].reshape(L, P, NK // 2, 2 * D).transpose(0, 2, 1, 3)),
        "cache_kT": tile(i["cache_k"][0].reshape(L, P, P).transpose(0, 2, 1)),
        "cache_v": i["cache_v"][0].reshape(L, P, P),
        "sink": np.repeat(i["att_sink"][:, None, :], P, axis=1),
        "conv_w": tile(i["conv_w"].reshape(L, 3, 2, P).transpose(0, 3, 2, 1)),
        "cols": cat([halves(i[n]) for n in ("rw_w0", "rw_a0", "rw_kk", "rw_ka", "rw_rk", "rw_lnx_g", "rw_lnx_b")]
                    + [np.zeros((L, P, N_COLS - 18), np.float32)], axis=2),
        "w_up": cat([i["rw_w_up"].reshape(L, 2 * RANK, 256), i["rw_a_up"].reshape(L, 2 * RANK, 256)], axis=1),
        "g_up": i["rw_g_up"],
        "state_T": tile(i["state_rwkv"][0].transpose(0, 1, 2, 4, 3)),
        "ln1": np.stack([i["ln1_g"], i["ln1_b"]], axis=1), "ln2": np.stack([i["ln2_g"], i["ln2_b"]], axis=1),
        "subkeys_T": tile(i["peer_subkeys"].reshape(L, 2 * PH, NK, P).transpose(0, 3, 1, 2)),
    }
    out.update(shape_constants())
    return {k: tile(v) for k, v in out.items()}


OUTS = {"y": [TILES, P, D], "new_k": [DEPTH, P, P], "new_v": [DEPTH, P, P], "new_state_T": [DEPTH, 2, 4, HD, HD]}


def kernel(**inputs):
    import concourse.bacc as bacc
    from concourse.bass_utils import run_bass_kernel_spmd as run
    import ml_dtypes

    arrays = lay_out({k: np.asarray(v) for k, v in inputs.items()})
    arrays["iota"] = np.tile(np.arange(NK + JG, dtype=np.float32), (P, 1)).astype(ml_dtypes.bfloat16)
    nc = bacc.Bacc("TRN2", target_bir_lowering=False, num_devices=1)
    dram = {k: nc.dram_tensor("in_" + k, v.shape, mybir.dt.from_np(v.dtype), kind="ExternalInput").ap() for k, v in arrays.items()}
    dram.update({k: nc.dram_tensor("out_" + k, v, F32, kind="ExternalOutput").ap() for k, v in OUTS.items()})
    build(nc, dram)
    r = run(nc, [{"in_" + k: v for k, v in arrays.items()}], core_ids=[0]).results[0]
    y, nk, nv = r["out_y"], r["out_new_k"], r["out_new_v"]
    return (y[0:1], y[1:3].reshape(1, 2 * P, D),
            nk.transpose(0, 2, 1).reshape(1, DEPTH, P, 2, HD), nv.transpose(0, 2, 1).reshape(1, DEPTH, P, 2, HD),
            r["out_new_state_T"].transpose(0, 1, 2, 4, 3)[None])
```

```python
import numpy as np
import concourse.bass as bass
from concourse import mybir
from concourse.alu_op_type import AluOpType as ALU
from contextlib import ExitStack

ACT = mybir.ActivationFunctionType
AX = mybir.AxisListType
F32, F32R, BF16, U32 = mybir.dt.float32, mybir.dt.float32r, mybir.dt.bfloat16, mybir.dt.uint32

P = 128
D = 1024
KD = D // P
DEPTH = 2
TILES = 3
TOK = TILES * P
SEQ_OF_TILE = (0, 1, 1)
HD = 64
RANK = 32
CHUNK = 64
N_LEVELS = 6
HEADS = 8
N_IN = 20
QB, KB, VB, RB, RKB, RVB, WAB, GB, CBB, CCB, CUB = 0, 4, 5, 6, 8, 10, 12, 13, 14, 16, 18
NEG = -1e30
LN_EPS, LNX_EPS = 1e-5, 64e-5
ALPHA = (2 * DEPTH) ** 0.25
TOPK = 16
NK = 128
PH = 8
JG = 32
JSTEP = TOK * 1 // JG

SLOTS = 4
PIECE = 2048
N_ADA, N_PIN, N_POUT, N_PQ, N_PEXP = 24, 10, 4, 8, 128
AT_IN = 0
AT_OUT = AT_IN + N_PIN
AT_Q = AT_OUT + N_POUT
AT_ADA = AT_Q + N_PQ
N_GATE2 = D // (PIECE // KD)
N_EARLY = N_ADA - N_GATE2
AT_EXP = AT_ADA + N_EARLY
NW_ADA = PIECE // KD
NEXT = DEPTH - 1
assert DEPTH == 2
C_W0, C_A0, C_KK, C_KA, C_RK, C_LG, C_LB, C_CW, N_COLS = 0, 4, 8, 10, 12, 14, 16, 18, 24


def slot(n):
    return n % SLOTS


def filled(n):
    return 16 * (n // SLOTS + 1)


class Turns:

    def __init__(self, names, banks):
        self.n = {name: i for i, name in enumerate(names)}
        self.banks = banks

    def at(self, *name):
        i = self.n[name]
        return i % self.banks, i // self.banks


def layer_row(ap, l):
    row = ap[bass.ds(l, 1)]
    names = " ".join(f"x{i}" for i in range(len(ap.shape) - 1))
    first, rest = names.split(" ", 1) if " " in names else (names, "")
    return row.rearrange(f"a {names} -> (a {first}) {rest}")


def norm_steps(nc, dve, link, x, stats, mv, rstd, var_ready, std_ready, count, g, b, out):
    for h in range(2):
        ins = nc.vector.bn_stats(stats[:, 6 * h:6 * h + 6], x[:, 512 * h:512 * h + 512])
    link(ins)
    link(nc.vector.bn_aggr(mv, stats))
    nc.vector.tensor_scalar(mv[:, 1:2], mv[:, 1:2], LN_EPS, None, ALU.add).then_inc(var_ready, 1)
    dve.wait_ge(std_ready, count)
    link(nc.vector.reciprocal(rstd, rstd))
    link(nc.vector.tensor_scalar(out, x, mv[:, 0:1], rstd, ALU.subtract, ALU.mult))
    link(nc.vector.tensor_tensor(out, out, g, ALU.mult))
    return nc.vector.tensor_tensor(out, out, b, ALU.add)


def clear(nc, sems):
    for s in sems:
        nc.sync.sem_clear(s)
    nc.all_engine_barrier()


class Core:
    pass


def make_core(nc, ctx, dram):
    c = Core()
    c.nc, c.dram = nc, dram
    sb = lambda name, shape, dt=F32: ctx.enter_context(nc.sbuf_tensor(name, shape, dt))
    sem = lambda name: ctx.enter_context(nc.semaphore(name))
    c.ring = sb("ring", [P, SLOTS, PIECE])
    c.ident = sb("ident", [P, P])
    c.hT = sb("hT", [P, KD, TOK])
    c.mod_cols = sb("mod_cols", [P, 4, KD, 2])
    c.ring_full = [sem(f"ring_full{i}") for i in range(SLOTS)]
    c.att_tables_in, c.rwkv_tables_in = sem("att_tables_in"), sem("rwkv_tables_in")
    c.late_in = sem("late_in")
    c.x_dram = nc.dram_tensor("x_between_blocks", [TILES, P, D], F32, kind="Internal").ap()
    c.gate_dram = nc.dram_tensor("gate_rows", [DEPTH + 1, 2, 2, D], F32, kind="Internal").ap()
    c.silu, c.ones = sb("cond_silu", [P, KD, 2]), sb("ones", [1, 2])
    return c


def piece_source(c, l, n):
    for first, name in ((AT_EXP, "u"), (AT_ADA, "w_ada"), (AT_Q, "wq"), (AT_OUT, "w_out"), (AT_IN, "w_in")):
        if n >= first:
            break
    m = n - first
    if name == "w_ada":
        return c.dram[name][NEXT, m]
    if name == "u":
        name, m = ("u", "v")[m % 2], m // 2
    return c.dram[name][bass.ds(l, 1), m].rearrange("a p n -> (a p) n")


def fill_slot(c, sp, l, n):
    sp.dma_start(c.ring[:, slot(n), :], piece_source(c, l, n)).then_inc(c.ring_full[slot(n)], 16)



def ada_product(c, s, pe, rows, piece_full, count, ring_slot, n, first=0):
    b, r = s.steps.at("ada", n)
    pe.wait_ge(piece_full, count)
    pe.wait_ge(s.free[b], r)
    out, w = s.bank[b][0:2, 0:NW_ADA], c.ring[:, ring_slot, :].rearrange("p (k n) -> p k n", k=KD)
    c.nc.tensor.matmul(out, c.ones[:, :], rows[0:1, (n - first) * NW_ADA:(n - first + 1) * NW_ADA],
                       start=True, stop=False)
    for k in range(KD):
        ins = c.nc.tensor.matmul(out, c.silu[:, k, :], w[:, k, :], start=False, stop=(k == KD - 1))
    ins.then_inc(s.full[b], 1)


def ada_copy(c, s, act, rows, n, first=0):
    b, r = s.steps.at("ada", n)
    act.wait_ge(s.full[b], r + 1)
    c.nc.scalar.copy(rows[:, (n - first) * NW_ADA:(n - first + 1) * NW_ADA], s.bank[b][0:2, 0:NW_ADA]).then_inc(s.free[b], 1)


def ada_transposes(c, s, pe, rows):
    b, r = s.steps.at("cols")
    for n in range(N_EARLY):
        bb, rr = s.steps.at("ada", n)
        pe.wait_ge(s.free[bb], rr + 1)
    pe.wait_ge(s.free[b], r)
    for i, q in enumerate((0, 1, 3, 4)):
        for k in range(KD):
            ins = c.nc.tensor.transpose(s.bank[b][:, 2 * (i * KD + k):2 * (i * KD + k) + 2],
                                        rows[:, q * D + k * P:q * D + (k + 1) * P], c.ident[0:2, 0:2])
    ins.then_inc(s.full[b], 1)


def ada_columns(c, s, dve):
    b, r = s.steps.at("cols")
    dve.wait_ge(s.full[b], r + 1)
    cols = s.bank[b][:, 0:64].rearrange("p (q k s) -> p q k s", q=4, k=KD)
    c.nc.vector.tensor_copy(c.mod_cols[:, 0::2], cols[:, 0::2])
    c.nc.vector.tensor_scalar(c.mod_cols[:, 1::2], cols[:, 1::2], 1.0, None, ALU.add).then_inc(s.free[b], 1)


def store_gate(c, s, act, rows, which, place, stored):
    for n in range(N_GATE2):
        b, r = s.steps.at("ada", (8, N_EARLY)[which] + n)
        act.wait_ge(s.free[b], r + 1)
    act.dma_start(place, rows).then_inc(stored, 16)


def gate_place(c, l, which):
    return c.gate_dram[bass.ds(l, 1), which].rearrange("a s n -> (a s) n")


def begin(c):
    nc, dram = c.nc, c.dram
    with ExitStack() as ctx:
        turns = [("ada", n) for n in range(N_ADA)] + [("cols",)]
        for t in range(TILES):
            turns += feature_turns(t)
        s = Stage(c, ctx, "begin", turns,
                  ["x_in", "gb_in", "cond_in", "bias_in", "var_ready", "std_ready", "normed", "stored", "vdone",
                   "exp_ready", "cond_ready", "gates_stored"])
        S = s.named
        piece_full = [s.sem(f"piece_full{i}") for i in range(SLOTS)]
        x, gb, rows = s.sb("x", [P, TILES, D]), s.sb("gb", [P, 2, D]), s.sb("rows", [2, 6 * D])
        stats, mv, rstd = s.sb("stats", [P, TILES, 12]), s.sb("mv", [P, TILES, 2]), s.sb("rstd", [P, TILES])
        cond, cexp = s.sb("cond", [P, KD, 2]), s.sb("cond_exp", [P, KD, 2])
        with nc.Block() as block:

            @block.sync
            def _(sp):
                sp.dma_start(cond[:, :, :], dram["cond"]).then_inc(S["cond_in"], 16)
                sp.dma_start(rows[0:1, :], dram["b_ada"][0:1]).then_inc(S["bias_in"], 16)
                for n in range(N_ADA + SLOTS):
                    if n >= SLOTS:
                        b, r = s.steps.at("ada", n - SLOTS)
                        sp.wait_ge(s.full[b], r + 1)
                    if n < N_ADA:
                        sp.dma_start(c.ring[:, slot(n), :], dram["w_ada"][0, n]).then_inc(piece_full[slot(n)], 16)
                    else:
                        fill_slot(c, sp, 0, n - N_ADA)

            @block.scalar
            def _(act):
                act.dma_start(c.ident[:, :], dram["ident"]).then_inc(S["gb_in"], 16)
                for t in range(TILES):
                    act.dma_start(x[:, t, :], dram["x_in"][t]).then_inc(S["x_in"], 16)
                for i in range(2):
                    act.dma_start(gb[:, i, :], dram["ln_in"][i].partition_broadcast(P)).then_inc(S["gb_in"], 16)
                act.wait_ge(S["cond_in"], 16)
                nc.scalar.activation(cexp[:, :, :], cond[:, :, :], ACT.Exp, scale=-1.0).then_inc(S["exp_ready"], 1)
                for t in range(TILES):
                    act.wait_ge(S["var_ready"], t + 1)
                    nc.scalar.activation(rstd[:, t:t + 1], mv[:, t, 1:2], ACT.Sqrt).then_inc(S["std_ready"], 1)
                    ada_copy(c, s, act, rows, t)
                for n in range(TILES, N_ADA):
                    ada_copy(c, s, act, rows, n)
                for t in range(TILES):
                    act.wait_ge(S["normed"], t + 1)
                    act.dma_start(c.x_dram[t], x[:, t, :]).then_inc(S["stored"], 16)
                for which, q in enumerate((2, 5)):
                    store_gate(c, s, act, rows[:, q * D:(q + 1) * D], which, c.gate_dram[0, which], S["gates_stored"])
                b, r = s.steps.at("cols")
                act.wait_ge(s.free[b], r + 1)
                for t in range(TILES):
                    modulate(c, s, act, 0, t, 1)
                act.wait_ge(S["gates_stored"], 32)
                act.wait_ge(S["stored"], 16 * TILES)

            @block.vector
            def _(dve):
                link = in_order(dve, S["vdone"])
                nc.vector.memset(c.ones[:, :], 1.0)
                dve.wait_ge(S["exp_ready"], 1)
                link(nc.vector.tensor_scalar(cexp[:, :, :], cexp[:, :, :], 1.0, None, ALU.add))
                link(nc.vector.reciprocal(cexp[:, :, :], cexp[:, :, :]))
                nc.vector.tensor_tensor(c.silu[:, :, :], cond[:, :, :], cexp[:, :, :], ALU.mult).then_inc(S["cond_ready"], 1)
                dve.wait_ge(S["x_in"], 16 * TILES)
                dve.wait_ge(S["gb_in"], 16 * 3)
                for t in range(TILES):
                    norm_steps(nc, dve, link, x[:, t, :], stats[:, t, :], mv[:, t, :], rstd[:, t:t + 1], S["var_ready"],
                               S["std_ready"], t + 1, gb[:, 0, :], gb[:, 1, :], x[:, t, :]).then_inc(S["normed"], 1)
                ada_columns(c, s, dve)
                b, r = s.steps.at("cols")
                dve.wait_ge(s.free[b], r + 1)
                for t in range(TILES):
                    modulate(c, s, dve, 0, t, 0)

            @block.tensor
            def _(pe):
                pe.wait_ge(S["cond_ready"], 1)
                pe.wait_ge(S["bias_in"], 16)
                for n in range(N_ADA):
                    ada_product(c, s, pe, rows, piece_full[slot(n)], filled(n), slot(n), n)
                pe.wait_ge(S["gb_in"], 16 * 3)
                ada_transposes(c, s, pe, rows)
                pe.wait_ge(S["normed"], TILES)
                for t in range(TILES):
                    transpose_x(c, s, pe, x, t)
        clear(nc, s.sems)


class Stage:

    def __init__(self, c, ctx, name, turns, semaphores, banks=8):
        self.nc, self.ctx, self.name = c.nc, ctx, name
        self.steps = Turns(turns, banks)
        self.bank = [ctx.enter_context(c.nc.psum_tensor(f"{name}_bank{i}", [P, 512], F32)) for i in range(banks)]
        self.sems = []
        self.full = [self.sem(f"full{i}") for i in range(banks)]
        self.free = [self.sem(f"free{i}") for i in range(banks)]
        self.named = {n: self.sem(n) for n in semaphores}

    def sem(self, name):
        self.sems.append(self.ctx.enter_context(self.nc.semaphore(f"{self.name}_{name}")))
        return self.sems[-1]

    def sb(self, name, shape, dt=F32):
        return self.ctx.enter_context(self.nc.sbuf_tensor(f"{self.name}_{name}", shape, dt))


def in_order(eng, done):
    count = [0]

    def link(ins):
        count[0] += 1
        ins.then_inc(done, 1)
        eng.wait_ge(done, count[0])

    return link


def project(c, l, pT, att, rw):
    nc, dram = c.nc, c.dram
    turns = [("proj", b) for b in range(N_IN)]
    with ExitStack() as ctx:
        s = Stage(c, ctx, "project", turns, ["w_high", "w_low", "h_high", "h_low"])
        at, bank, full, free, S = s.steps.at, s.bank, s.full, s.free, s.named
        hs = s.sb("hs", [P, 2, KD, TOK], F32R)
        ws = s.sb("ws", [P, 2, 2, PIECE], F32R)
        with nc.Block() as block:

            @block.sync
            def _(sp):
                load_attention_tables(c, sp, l, att)
                load_rwkv_tables(c, sp, l, rw)
                refill(c, s, sp, l, AT_IN, N_PIN)

            @block.scalar
            def _(act):
                split_high(c, s, act, AT_IN, 0, ws)
                split_rows_high(c, s, act, c.hT, hs)
                split_high(c, s, act, AT_IN, 1, ws)
                for m in range(N_PIN):
                    b, r = at("proj", 2 * m)
                    act.wait_ge(full[b], r + 1)
                    nc.scalar.copy(pT[:, 2 * m, :], bank[b][:, 0:TOK]).then_inc(free[b], 1)
                    if m + 2 < N_PIN:
                        split_high(c, s, act, AT_IN, m + 2, ws, at("proj", 2 * m + 1))

            @block.vector
            def _(dve):
                split_low(c, s, dve, AT_IN, 0, ws)
                split_rows_low(c, s, dve, c.hT, hs)
                split_low(c, s, dve, AT_IN, 1, ws)
                for m in range(N_PIN):
                    b, r = at("proj", 2 * m + 1)
                    dve.wait_ge(full[b], r + 1)
                    nc.vector.tensor_copy(pT[:, 2 * m + 1, :], bank[b][:, 0:TOK]).then_inc(free[b], 1)
                    if m + 2 < N_PIN:
                        split_low(c, s, dve, AT_IN, m + 2, ws)

            @block.tensor
            def _(pe):
                pe.wait_ge(S["h_low"], TILES)
                for n in range(N_IN):
                    weight_blocks_times_h(c, s, pe, n, at("proj", n), ws, hs)
        clear(nc, s.sems)


PASSES = ((0, 0), (0, 1), (1, 0))


def split_high(c, s, act, first, m, ws, used=None):
    n = first + m
    act.wait_ge(c.ring_full[slot(n)], filled(n))
    if used is not None:
        b, r = used
        act.wait_ge(s.full[b], r + 1)
    c.nc.scalar.copy(ws[:, m % ws.shape[1], 0, :], c.ring[:, slot(n), :]).then_inc(s.named["w_high"], 1)


def split_low(c, s, dve, first, m, ws):
    dve.wait_ge(s.named["w_high"], m + 1)
    b = m % ws.shape[1]
    c.nc.vector.tensor_tensor(ws[:, b, 1, :], c.ring[:, slot(first + m), :], ws[:, b, 0, :].bitcast(F32),
                              ALU.subtract).then_inc(s.named["w_low"], 1)


def refill(c, s, sp, l, first, count):
    for m in range(count):
        sp.wait_ge(s.named["w_low"], m + 1)
        fill_slot(c, sp, l, first + m + SLOTS)


def split_rows_high(c, s, act, source, hs, tiles=range(TILES)):
    for t in tiles:
        cols = slice(t * P, (t + 1) * P)
        c.nc.scalar.copy(hs[:, 0, :, cols], source[:, :, cols]).then_inc(s.named["h_high"], 1)


def split_rows_low(c, s, dve, source, hs, tiles=range(TILES)):
    for t in tiles:
        dve.wait_ge(s.named["h_high"], t + 1)
        cols = slice(t * P, (t + 1) * P)
        c.nc.vector.tensor_tensor(hs[:, 1, :, cols], source[:, :, cols], hs[:, 0, :, cols].bitcast(F32),
                                  ALU.subtract).then_inc(s.named["h_low"], 1)


def weight_blocks_times_h(c, s, pe, n, turn, ws, hs):
    b, r = turn
    pe.wait_ge(s.named["w_low"], n // 2 + 1)
    pe.wait_ge(s.free[b], r)
    w = ws[:, (n // 2) % 2].rearrange("p s (h k n) -> p s h k n", h=2, k=KD)
    for k in range(KD):
        for i, (a, v) in enumerate(PASSES):
            ins = c.nc.tensor.matmul(s.bank[b][:, 0:TOK], w[:, a, n % 2, k, :], hs[:, v, k, :],
                                     start=(k == 0 and i == 0), stop=(k == KD - 1 and i == 2))
    ins.then_inc(s.full[b], 1)


def feature_turns(t):
    return [("xT", t, h) for h in range(2)]


def transpose_x(c, s, pe, x, t):
    for h in range(2):
        b, r = s.steps.at("xT", t, h)
        pe.wait_ge(s.free[b], r)
        for k in range(4):
            f = 4 * h + k
            ins = c.nc.tensor.transpose(s.bank[b][:, k * P:(k + 1) * P], x[:, t, f * P:(f + 1) * P], c.ident[:, :])
        ins.then_inc(s.full[b], 1)


def modulate(c, s, eng, q, t, h, scalar=None):
    scalar = h == 1 if scalar is None else scalar
    b, r = s.steps.at("xT", t, h)
    eng.wait_ge(s.full[b], r + 1)
    for k in range(4):
        f, seq = 4 * h + k, SEQ_OF_TILE[t]
        out, block = c.hT[:, f, t * P:(t + 1) * P], s.bank[b][:, k * P:(k + 1) * P]
        shift, scale = (c.mod_cols[:, 2 * q + i, f, seq:seq + 1] for i in range(2))
        if not scalar:
            ins = c.nc.vector.tensor_scalar(out, block, scale, shift, ALU.mult, ALU.add)
        else:
            ins = c.nc.scalar.activation(out, block, ACT.Identity, bias=shift, scale=scale)
    ins.then_inc(s.free[b], 1)


class Tables:
    pass


def attention_tables(c, ctx):
    sb = lambda name, shape: ctx.enter_context(c.nc.sbuf_tensor("att_" + name, shape, F32))
    a = Tables()
    a.cosT, a.sinT, a.rotate = sb("cosT", [P, 2 * P]), sb("sinT", [P, 2 * P]), sb("rotate", [P, P])
    a.mask, a.sink, a.conv_w = sb("mask", [P, 2, 3 * P]), sb("sink", [P, HEADS]), sb("conv_w", [P, 2, 3])
    a.cacheT, a.vkey = sb("cacheT", [P, P]), sb("vkey", [P, 1 + TILES, P])
    return a


def load_attention_tables(c, eng, l, a):
    whole = lambda tensor: tensor[tuple(slice(None) for _ in tensor.shape)]
    for tensor, name in ((a.cosT, "cosT"), (a.sinT, "sinT"), (a.rotate, "rotate"), (a.mask, "att_mask")):
        eng.dma_start(whole(tensor), c.dram[name]).then_inc(c.att_tables_in, 16)
    for tensor, name in ((a.sink, "sink"), (a.conv_w, "conv_w"), (a.cacheT, "cache_kT")):
        eng.dma_start(whole(tensor), layer_row(c.dram[name], l)).then_inc(c.att_tables_in, 16)
    eng.dma_start(a.vkey[:, 0, :], layer_row(c.dram["cache_v"], l)).then_inc(c.att_tables_in, 16)


def attention(c, l, pT, mixT, tables):
    nc, dram = c.nc, c.dram
    turns = [("rot", b) for b in range(5)] + [("avT",)]
    order = [("scores", 0)] + [part for t in range(1, TILES) for part in (("scores", t), ("values", t - 1))]
    order += [("values", TILES - 1)]
    for what, t in order:
        if what == "scores":
            turns += [("score", t, h) for h in range(HEADS)]
        else:
            for b in range(5):
                turns += ([("probT", t, b, g) for g in range(2)] if b < 4 else []) + ([("att", t, b - 1)] if b > 0 else [])
    CONV = ((0, P), (P, TOK))
    with ExitStack() as ctx:
        s = Stage(c, ctx, "att", turns, ["k_out", "k_stored", "vdone", "pdone", "adone", "maxed", "expd",
                                         "sums", "scaled", "att_done", "conv_cols", "sink_exp"])
        at, bank, full, free, S = s.steps.at, s.bank, s.full, s.free, s.named
        cosT, sinT, rotate, mask, sink = tables.cosT, tables.sinT, tables.rotate, tables.mask, tables.sink
        conv_w, cacheT, vkey, tables_in = tables.conv_w, tables.cacheT, tables.vkey, c.att_tables_in
        turned = s.sb("turned", [P, 5, 2 * P])
        kctx = s.sb("kctx", [P, P])
        prob = s.sb("prob", [P, 2, HEADS, 3 * P])
        probT = s.sb("probT", [P, 4, 3, P])
        row = s.sb("row", [P, TILES, 5, HEADS])
        z, z1 = s.sb("conv_z", [P, 2, TOK]), s.sb("conv_z1", [P, 2, TOK])
        probT_turn = {}
        for t in range(TILES):
            for b in range(4):
                for g in range(2):
                    probT_turn[t, b, g] = len(probT_turn)
        with nc.Block() as block:

            @block.sync
            def _(sp):
                sp.dma_start(layer_row(dram["new_k"], l), pT[:, KB, 0:P]).then_inc(S["k_stored"], 16)
                sp.dma_start(layer_row(dram["new_v"], l), pT[:, VB, 0:P]).then_inc(S["k_stored"], 16)
                sp.wait_ge(S["k_stored"], 32)

            @block.gpsimd
            def _(pool):
                link = in_order(pool, S["pdone"])
                pool.wait_ge(tables_in, 16 * 8)
                link(nc.gpsimd.tensor_tensor(z[:, :, :], pT[:, CCB:CCB + 2, :], pT[:, CUB:CUB + 2, :], ALU.mult))
                for g in range(2):
                    link(nc.gpsimd.tensor_scalar(mixT[:, 6 + g, :], z[:, g, :], conv_w[:, g, 1:2], None, ALU.mult))
                for g in range(2):
                    for w, src, dst in ((0, 0, 1), (2, 1, 0)):
                        link(nc.gpsimd.tensor_scalar(z1[:, g, :], z[:, g, :], conv_w[:, g, w:w + 1], None, ALU.mult))
                        for lo, hi in CONV:
                            n = hi - lo - 1
                            out = mixT[:, 6 + g, lo + dst:lo + dst + n]
                            ins = nc.gpsimd.tensor_tensor(out, out, z1[:, g, lo + src:lo + src + n], ALU.add)
                        link(ins)
                    link(nc.gpsimd.tensor_tensor(mixT[:, 6 + g, :], mixT[:, 6 + g, :], pT[:, CBB + g, :], ALU.mult))

            @block.scalar
            def _(act):
                b, r = at("avT")
                act.wait_ge(full[b], r + 1)
                nc.scalar.copy(vkey[:, 1:4, :], bank[b][:, 0:TOK].rearrange("p (t n) -> p t n", t=TILES)).then_inc(free[b], 1)
                for what, t in order:
                    nk = 1 if t == 0 else 3
                    if what == "scores":
                        act.wait_ge(S["maxed"], t + 1)
                        for h in range(HEADS):
                            nc.scalar.activation(prob[:, t % 2, h, 0:nk * P], prob[:, t % 2, h, 0:nk * P], ACT.Exp,
                                                 bias=row[:, t, 1, h:h + 1], accum_out=row[:, t, 2, h:h + 1])
                        nc.scalar.activation(row[:, t, 3, :], row[:, t, 3, :], ACT.Exp).then_inc(S["expd"], 1)
                        continue
                    for bb in range(4):
                        for g in range(2):
                            b, r = at("probT", t, bb, g)
                            m = probT_turn[t, bb, g]
                            act.wait_ge(full[b], r + 1)
                            if m >= 4:
                                ab, ar = at("att", *[k for k, v in probT_turn.items() if v == m - 4][0][:2])
                                act.wait_ge(full[ab], ar + 1)
                            nc.scalar.copy(probT[:, m % 4, 0:nk, :],
                                           bank[b][:, 0:nk * P].rearrange("p (k n) -> p k n", k=nk)).then_inc(free[b], 1)

            @block.vector
            def _(dve):
                link = in_order(dve, S["vdone"])
                dve.wait_ge(tables_in, 16 * 8)
                dve.wait_ge(S["k_stored"], 32)
                nc.vector.tensor_copy(kctx[:, :], pT[:, KB, 0:P])
                for b5 in range(5):
                    b, r = at("rot", b5)
                    dve.wait_ge(full[b], r + 1)
                    nc.vector.tensor_tensor(turned[:, b5, :], bank[b][:, 0:2 * P], sinT[:, :], ALU.mult).then_inc(free[b], 1)
                    link(nc.vector.tensor_tensor(pT[:, b5, P:TOK], pT[:, b5, P:TOK], cosT[:, :], ALU.mult))
                    ins = nc.vector.tensor_tensor(pT[:, b5, P:TOK], pT[:, b5, P:TOK], turned[:, b5, :], ALU.add)
                ins.then_inc(S["scaled"], 1)
                for what, t in order:
                    nk = 1 if t == 0 else 3
                    if what == "scores":
                        if t >= 2:
                            b, r = at("att", t - 2, 3)
                            dve.wait_ge(full[b], r + 1)
                        for h in range(HEADS):
                            b, r = at("score", t, h)
                            dve.wait_ge(full[b], r + 1)
                            if t == 0:
                                ins = nc.vector.tensor_scalar(prob[:, 0, h, 0:P], bank[b][:, 0:P], HD ** -0.5, None, ALU.mult)
                            else:
                                ins = nc.vector.scalar_tensor_tensor(prob[:, t % 2, h, :], bank[b][:, 0:3 * P], HD ** -0.5,
                                                                     mask[:, t - 1, :], ALU.mult, ALU.add)
                            ins.then_inc(free[b], 1)
                        for h in range(HEADS):
                            b, r = at("score", t, h)
                            dve.wait_ge(free[b], r + 1)
                        link(nc.vector.tensor_reduce(row[:, t, 0, :], prob[:, t % 2, :, 0:nk * P], AX.X, ALU.max))
                        link(nc.vector.tensor_tensor(row[:, t, 0, :], row[:, t, 0, :], sink[:, :], ALU.max))
                        nc.vector.tensor_scalar(row[:, t, 1, :], row[:, t, 0, :], -1.0, None, ALU.mult)
                        nc.vector.tensor_tensor(row[:, t, 3, :], sink[:, :], row[:, t, 0, :], ALU.subtract).then_inc(S["maxed"], 1)
                        continue
                    dve.wait_ge(S["expd"], t + 1)
                    link(nc.vector.tensor_tensor(row[:, t, 2, :], row[:, t, 2, :], row[:, t, 3, :], ALU.add))
                    link(nc.vector.reciprocal(row[:, t, 4, :], row[:, t, 2, :]))
                    for h in (0, 4, 1, 5, 2, 6, 3, 7):
                        ins = nc.vector.tensor_scalar(prob[:, t % 2, h, 0:nk * P], prob[:, t % 2, h, 0:nk * P],
                                                      row[:, t, 4, h:h + 1], None, ALU.mult)
                        ins.then_inc(S["scaled"], 1)
                    for bb in range(4):
                        b, r = at("att", t, bb)
                        dve.wait_ge(full[b], r + 1)
                        nc.vector.tensor_copy(mixT[:, bb, t * P:(t + 1) * P], bank[b][:, 0:P]).then_inc(free[b], 1)

            @block.tensor
            def _(pe):
                pe.wait_ge(tables_in, 16 * 8)
                for b5 in range(5):
                    b, r = at("rot", b5)
                    pe.wait_ge(free[b], r)
                    nc.tensor.matmul(bank[b][:, 0:2 * P], rotate[:, :], pT[:, b5, P:TOK], start=True, stop=True).then_inc(full[b], 1)
                b, r = at("avT")
                pe.wait_ge(free[b], r)
                for t in range(TILES):
                    ins = nc.tensor.transpose(bank[b][:, t * P:(t + 1) * P], pT[:, VB, t * P:(t + 1) * P], c.ident[:, :])
                ins.then_inc(full[b], 1)
                b, r = at("avT")
                pe.wait_ge(free[b], r + 1)
                pe.wait_ge(S["scaled"], 1)
                for what, t in order:
                    if what == "scores":
                        for h in range(HEADS):
                            b, r = at("score", t, h)
                            pe.wait_ge(free[b], r)
                            rows = slice(HD * (h // 4), HD * (h // 4) + HD)
                            q = pT[rows, h % 4, t * P:(t + 1) * P]
                            if t == 0:
                                ins = nc.tensor.matmul(bank[b][:, 0:P], q, kctx[rows, :], start=True, stop=True)
                            else:
                                nc.tensor.matmul(bank[b][:, 0:P], q, cacheT[rows, :], start=True, stop=True)
                                ins = nc.tensor.matmul(bank[b][:, P:3 * P], q, pT[rows, KB, P:TOK], start=True, stop=True)
                            ins.then_inc(full[b], 1)
                        continue
                    values = [1] if t == 0 else [0, 2, 3]

                    def transpose_probabilities(bb):
                        for g in range(2):
                            b, r = at("probT", t, bb, g)
                            pe.wait_ge(S["scaled"], 1 + HEADS * t + 2 * bb + g + 1)
                            pe.wait_ge(free[b], r)
                            for k in range(len(values)):
                                ins = nc.tensor.transpose(bank[b][:, k * P:(k + 1) * P],
                                                          prob[:, t % 2, bb + 4 * g, k * P:(k + 1) * P], c.ident[:, :])
                            ins.then_inc(full[b], 1)

                    transpose_probabilities(0)
                    for bb in range(4):
                        if bb < 3:
                            transpose_probabilities(bb + 1)
                        ab, ar = at("att", t, bb)
                        pe.wait_ge(free[ab], ar)
                        for g in range(2):
                            b, r = at("probT", t, bb, g)
                            pe.wait_ge(free[b], r + 1)
                            m = probT_turn[t, bb, g]
                            for k, v in enumerate(values):
                                ins = nc.tensor.matmul(bank[ab][HD * g:HD * g + HD, 0:P], vkey[:, v, HD * g:HD * g + HD],
                                                       probT[:, m % 4, k, :], start=(k == 0), stop=(k == len(values) - 1))
                        ins.then_inc(full[ab], 1)
        clear(nc, s.sems + [tables_in])


DECAY = float(np.exp(-0.5))


def rwkv_tables(c, ctx):
    sb = lambda name, shape: ctx.enter_context(c.nc.sbuf_tensor("rwkv_" + name, shape, F32))
    a = Tables()
    a.cols, a.w_up, a.g_up = sb("cols", [P, N_COLS]), sb("w_up", [P, 2 * P]), sb("g_up", [HD, 2 * P])
    a.headones, a.resets = sb("headones", [P, P]), sb("resets", [P, 2 * TOK])
    a.gram_mask, a.level_mask = sb("gram_mask", [P, 2, 4 * P]), sb("level_mask", [P, 2, N_LEVELS, P])
    return a


def load_rwkv_tables(c, eng, l, a):
    for tensor, name in ((a.cols, "cols"), (a.w_up, "w_up"), (a.g_up, "g_up")):
        eng.dma_start(tensor[:, :], layer_row(c.dram[name], l)).then_inc(c.rwkv_tables_in, 16)
    eng.dma_start(a.headones[:, :], c.dram["headones"]).then_inc(c.rwkv_tables_in, 16)
    eng.dma_start(a.resets[:, :], c.dram["resets"]).then_inc(c.rwkv_tables_in, 16)
    eng.dma_start(a.gram_mask[:, :, :], c.dram["gram_mask"]).then_inc(c.rwkv_tables_in, 16)
    eng.dma_start(a.level_mask[:, :, :, :], c.dram["level_mask"]).then_inc(c.rwkv_tables_in, 16)


def rwkv(c, l, pT, mixT, tables):
    nc, dram = c.nc, c.dram
    turns = [("kk2", g) for g in range(2)]
    turns += [(name, d, g) for d in range(2) for name in ("decay", "rate") for g in range(2)]
    turns += [("gate", g) for g in range(2)] + [("vT", g) for g in range(2)]
    GH = [(g, hh) for g in range(2) for hh in range(2)]
    GT = [(g, t) for g in range(2) for t in range(TILES)]
    chunks = {}
    for d in range(2):
        for s_, n0, n1 in ((0, 0, 2), (1, 2, 6)):
            chunks[d, s_] = list(range(n0, n1)) if d == 0 else list(range(n1 - 1, n0 - 1, -1))
    scans = [(s_, step) for step in range(4) for s_ in range(2) if (s_ == 1 or step == 1)]
    gram_turns = lambda d, g, t: [("tokens", d, g, t)] + [("gram", d, g, t, hh) for hh in range(2)]
    for g, t in GT:
        turns += gram_turns(0, g, t)
    for d in range(2):
        turns += [("inv0", d, g, hh) for g, hh in GH]
        for lev in range(1, N_LEVELS):
            turns += [("invY", d, lev, g, hh) for g, hh in GH]
            for g, hh in GH:
                turns += ([("invX", d, lev, g, hh)] if lev < N_LEVELS - 1 else []) + [("invXT", d, lev, g, hh)]
        turns += [(n, d, g, t) for n in ("GW", "H", "EF", "QZ") for g, t in GT]
        for n, (s_, step) in enumerate(scans):
            turns += [("scan", d, s_, step, g) for g in range(2)]
            if d == 0:
                turns += gram_turns(1, *GT[n])
        if d == 0:
            turns += gram_turns(1, *GT[len(scans)])
    turns += [(n, g) for n in ("bonus", "mean", "var") for g in range(2)]

    with ExitStack() as ctx:
        s = Stage(c, ctx, "rwkv", turns, ["zeroed", "states_in", "squashed", "sigmoids", "kk2_in", "kk_root",
                                          "vdone", "exps_asked", "exps", "chunk_ops", "levelled", "seeded",
                                          "states", "state_out", "sums_in", "centred", "var_root", "adone"])
        at, bank, full, free, S = s.steps.at, s.bank, s.full, s.free, s.named
        cols, w_up, g_up, headones = tables.cols, tables.w_up, tables.g_up, tables.headones
        resets, gram_mask, level_mask = tables.resets, tables.gram_mask, tables.level_mask
        one_ka = s.sb("one_ka", [P, 2])
        v_tok = s.sb("v_tok", [P, TILES, 2 * P])
        gate, kk, kdsum, y = (s.sb(n, [P, 2, TOK]) for n in ("gate", "kk", "kdsum", "y"))
        Lsum, kd = s.sb("Lsum", [P, 2, TOK]), s.sb("kd", [P, 2, TOK])
        rate1 = s.sb("rate1", [P, 2, TOK])
        AR0 = c.hT[:, 0:4, :].rearrange("p (g w) n -> p g w n", g=2)
        decayC = s.sb("decayC", [P, 2, 2, 6])
        A_tok = s.sb("A_tok", [P, 2, TILES, P])
        BK_tok = s.sb("BK_tok", [P, 2, TILES, 2, 2, P])
        M = s.sb("M", [P, 2, 2, TILES, 4, P])
        Ak = s.sb("Ak", [P, 2, 2, TILES, P])
        Dm, DT, Ym = (s.sb(n, [P, 2, 2, TILES, P]) for n in ("Dm", "DT", "Ym"))
        GW, H = s.sb("GW", [P, 2, TILES, 2 * P]), s.sb("H", [P, 2, TILES, P])
        s_init = s.sb("s_init", [P, 2, 2, P])
        t_exc, t_inc, t_inv = pT[:, 0:2, :], pT[:, 2:4, :], pT[:, 4:6, :]
        sig = [pT[:, 14:16, :], pT[:, 16:18, :]]
        rate = [pT[:, 18:20, :], rate1[:, :, :]]
        AR = [AR0, pT[:, 0:4, :].rearrange("p (w g) n -> p g w n", w=2)]
        Bf, Kf = [c.hT[:, 4:6, :], rate[1]], [c.hT[:, 6:8, :], t_inv]
        r_, k_, v_ = pT[:, RB:RB + 2, :], pT[:, RKB:RKB + 2, :], pT[:, RVB:RVB + 2, :]
        ET = s.sb("ET", [P, 2, TILES, 2, P])
        F = Ym[:, :, :, :, :].rearrange("p g h t n -> p (g h t) n")
        QT = Ak[:, :, 0, :, :]
        state = Dm[:, :, :, :, :].rearrange("p g h t n -> p (g h t) n")

        def F_at(g, t, ch):
            return F[:, (g * TILES + t) * 2 + ch, :]

        def state_at(g, s_, step):
            return state[:, g * 6 + (step - 1 if s_ == 0 else 1 + step), :]

        def tile_cols(t):
            return slice(t * P, (t + 1) * P)

        with nc.Block() as block:

            @block.sync
            def _(sp):
                sp.wait_ge(S["zeroed"], 1)
                for d in range(2):
                    for h in range(4):
                        rows = slice(HD * (h % 2), HD * (h % 2) + HD)
                        sp.dma_start(s_init[rows, d, h // 2, rows],
                                     dram["state_T"][bass.ds(l, 1), d, h].rearrange("a p n -> (a p) n")).then_inc(S["states_in"], 16)
                for d in range(2):
                    sp.wait_ge(S["state_out"], 2 * (d + 1))
                    for h in range(4):
                        rows = slice(HD * (h % 2), HD * (h % 2) + HD)
                        sp.dma_start(dram["new_state_T"][bass.ds(l, 1), d, h].rearrange("a p n -> (a p) n"),
                                     state_at(h // 2, 0, 2)[rows, rows]).then_inc(S["states"], 16)
                    sp.wait_ge(S["states"], 64 * (d + 1))

            @block.gpsimd
            def _(pool):
                nc.gpsimd.memset(s_init[:, :, :, :], 0.0).then_inc(S["zeroed"], 1)
                nc.gpsimd.memset(BK_tok[:, :, :, :, :, :], 0.0).then_inc(S["zeroed"], 1)

            @block.scalar
            def _(act):
                act.wait_ge(c.rwkv_tables_in, 16 * 7)
                nc.scalar.activation(pT[0:HD, WAB, :], pT[0:HD, WAB, :], ACT.Tanh).then_inc(S["squashed"], 1)
                nc.scalar.activation(pT[0:HD, GB, :], pT[0:HD, GB, :], ACT.Sigmoid).then_inc(S["squashed"], 1)
                for g in range(2):
                    b, r = at("kk2", g)
                    act.wait_ge(free[b], r + 1)
                nc.scalar.activation(t_exc, t_exc, ACT.Sqrt).then_inc(S["kk_root"], 1)
                for d in range(2):
                    for name, dst, col in (("decay", sig, C_W0), ("rate", rate, C_A0)):
                        for g in range(2):
                            b, r = at(name, d, g)
                            act.wait_ge(full[b], r + 1)
                            nc.scalar.activation(dst[d][:, g, :], bank[b][:, 0:TOK], ACT.Sigmoid,
                                                 bias=cols[:, col + 2 * d + g:col + 2 * d + g + 1]).then_inc(free[b], 1)
                for g in range(2):
                    b, r = at("gate", g)
                    act.wait_ge(full[b], r + 1)
                    nc.scalar.copy(gate[:, g, :], bank[b][:, 0:TOK]).then_inc(free[b], 1)
                for g in range(2):
                    b, r = at("vT", g)
                    act.wait_ge(full[b], r + 1)
                    nc.scalar.copy(v_tok[:, :, g * P:(g + 1) * P],
                                   bank[b][:, 0:TOK].rearrange("p (t n) -> p t n", t=TILES)).then_inc(free[b], 1)
                act.wait_ge(S["zeroed"], 2)

                def exps(d):
                    act.wait_ge(S["exps_asked"], d + 1)
                    inc = Lsum[:, :, :] if d == 0 else t_inc
                    tot = Lsum[:, :, :].rearrange("p g (k n) -> p g k n", n=CHUNK)[:, :, :, CHUNK - 1]
                    nc.scalar.activation(t_exc, t_exc, ACT.Exp, scale=-DECAY)
                    nc.scalar.activation(t_inv, inc, ACT.Exp, scale=DECAY)
                    nc.scalar.activation(decayC[:, d], tot, ACT.Exp, scale=-DECAY).then_inc(S["adone"], 1)
                    act.wait_ge(S["adone"], d + 1)
                    nc.scalar.activation(t_inc, inc, ACT.Exp, scale=-DECAY).then_inc(S["exps"], 1)

                def tokens(d, g, t):
                    b, r = at("tokens", d, g, t)
                    act.wait_ge(full[b], r + 1)
                    nc.scalar.copy(A_tok[:, g, t, :], bank[b][:, 0:P])
                    for ch in range(2):
                        rows = slice(CHUNK * ch, CHUNK * ch + CHUNK)
                        ins = nc.scalar.copy(BK_tok[rows, g, t, :, ch, :],
                                             bank[b][rows, P:3 * P].rearrange("p (w n) -> p w n", w=2))
                    ins.then_inc(free[b], 1)

                exps(0)
                for n, (g, t) in enumerate(GT):
                    tokens(0, g, t)
                    if n == 2:
                        exps(1)
                for d in range(2):
                    if d == 1:
                        b, r = at("QZ", 0, 1, 2)
                        act.wait_ge(full[b], r + 1)
                        for g, t in GT:
                            tokens(1, g, t)
                    for lev in range(1, N_LEVELS):
                        for g, hh in GH:
                            b, r = at("invY", d, lev, g, hh)
                            act.wait_ge(full[b], r + 1)
                            nc.scalar.copy(Ym[:, g, hh, :, :], bank[b][:, 0:TOK].rearrange("p (t n) -> p t n", t=TILES)).then_inc(free[b], 1)
                    for g, t in GT:
                        b, r = at("GW", d, g, t)
                        act.wait_ge(full[b], r + 1)
                        nc.scalar.copy(GW[:, g, t, :], bank[b][:, 0:2 * P]).then_inc(free[b], 1)
                    for g, t in GT:
                        b, r = at("H", d, g, t)
                        act.wait_ge(full[b], r + 1)
                        nc.scalar.copy(H[:, g, t, :], bank[b][:, 0:P]).then_inc(free[b], 1)
                for g in range(2):
                    b, r = at("var", g)
                    act.wait_ge(free[b], r + 1)
                nc.scalar.activation(t_exc, t_exc, ACT.Sqrt).then_inc(S["var_root"], 1)

            @block.vector
            def _(dve):
                link = in_order(dve, S["vdone"])
                dve.wait_ge(c.rwkv_tables_in, 16 * 7)
                link(nc.vector.tensor_scalar(one_ka[:, :], cols[:, C_KA:C_KA + 2], -1.0, 1.0, ALU.mult, ALU.add))
                for g in range(2):
                    ins = nc.vector.tensor_scalar(kk[:, g, :], k_[:, g, :], cols[:, C_KK + g:C_KK + g + 1], None, ALU.mult)
                link(ins)
                nc.vector.tensor_tensor(t_inc, kk[:, :, :], kk[:, :, :], ALU.mult).then_inc(S["kk2_in"], 1)
                for g in range(2):
                    b, r = at("kk2", g)
                    dve.wait_ge(full[b], r + 1)
                    nc.vector.tensor_scalar(t_exc[:, g, :], bank[b][:, 0:TOK], 1e-24, None, ALU.max).then_inc(free[b], 1)
                dve.wait_ge(S["kk_root"], 1)
                link(nc.vector.reciprocal(t_exc, t_exc))
                link(nc.vector.tensor_tensor(kk[:, :, :], kk[:, :, :], t_exc, ALU.mult))
                flat = lambda ap: ap.rearrange("p g n -> p (g n)")

                def running_sums(d):
                    for name in ("decay", "rate"):
                        for g in range(2):
                            b, r = at(name, d, g)
                            dve.wait_ge(free[b], r + 1)
                    link(nc.vector.tensor_tensor_scan(flat(Lsum[:, :, :]), resets[:, :], flat(sig[d]), 0.0, ALU.mult, ALU.add))
                    if d == 0:
                        nc.vector.tensor_tensor(t_exc, Lsum[:, :, :], sig[d], ALU.subtract).then_inc(S["exps_asked"], 1)
                    else:
                        by_chunk = flat(Lsum[:, :, :]).rearrange("p (k n) -> p k n", n=CHUNK)
                        tot = by_chunk[:, :, CHUNK - 1:CHUNK].to_broadcast([P, 2 * TOK // CHUNK, CHUNK])
                        link(nc.vector.tensor_tensor(flat(t_exc).rearrange("p (k n) -> p k n", n=CHUNK), tot, by_chunk, ALU.subtract))
                        nc.vector.tensor_tensor(t_inc, t_exc, sig[d], ALU.add).then_inc(S["exps_asked"], 1)

                def keys(d):
                    for g in range(2):
                        ins = nc.vector.tensor_scalar(kd[:, g, :], rate[d][:, g, :], cols[:, C_KA + g:C_KA + g + 1],
                                                      one_ka[:, g:g + 1], ALU.mult, ALU.add)
                    link(ins)
                    link(nc.vector.tensor_tensor(kd[:, :, :], kd[:, :, :], k_, ALU.mult))
                    if d == 0:
                        nc.vector.tensor_copy(kdsum[:, :, :], kd[:, :, :])
                    else:
                        nc.vector.tensor_tensor(kdsum[:, :, :], kdsum[:, :, :], kd[:, :, :], ALU.add)
                    link(nc.vector.tensor_tensor(rate[d], rate[d], kk[:, :, :], ALU.mult))

                def operands(d):
                    dve.wait_ge(S["exps"], d + 1)
                    nc.vector.scalar_tensor_tensor(AR[d][:, :, 0, :], kk[:, :, :], -1.0, t_exc, ALU.mult, ALU.mult)
                    nc.vector.tensor_tensor(AR[d][:, :, 1, :], r_, t_inc, ALU.mult)
                    nc.vector.tensor_tensor(Bf[d], rate[d], t_inv, ALU.mult).then_inc(S["chunk_ops"], 1)
                    dve.wait_ge(S["chunk_ops"], 2 * d + 1)
                    nc.vector.tensor_tensor(Kf[d], kd[:, :, :], t_inv, ALU.mult).then_inc(S["chunk_ops"], 1)

                def grams(d, g, t):
                    for hh in range(2):
                        b, r = at("gram", d, g, t, hh)
                        dve.wait_ge(full[b], r + 1)
                        nc.vector.tensor_tensor(M[:, g, hh, t, :, :].rearrange("p q n -> p (q n)"), bank[b][:, :],
                                                gram_mask[:, d, :], ALU.mult).then_inc(free[b], 1)

                running_sums(0)
                keys(0)
                operands(0)
                for n, (g, t) in enumerate(GT):
                    grams(0, g, t)
                    if n == 0:
                        dve.wait_ge(S["chunk_ops"], 2)
                        running_sums(1)
                    if n == 2:
                        keys(1)
                    if n == 4:
                        operands(1)
                for d in range(2):
                    for g, t in GT:
                        b, r = at("gram", d, g, t, 1)
                        dve.wait_ge(free[b], r + 1)
                    if d == 1:
                        dve.wait_ge(S["states"], 64)

                    def level(lev, g, hh):
                        lm = level_mask[:, d, lev, :].unsqueeze(1).to_broadcast([P, TILES, P])
                        return nc.vector.tensor_tensor(Ak[:, g, hh, :, :], M[:, g, hh, :, 0, :], lm, ALU.mult).then_inc(S["levelled"], 1)

                    def levels_done(lev):
                        return 4 * (d * N_LEVELS + lev + 1)

                    eye = c.ident[:, :].unsqueeze(1).to_broadcast([P, TILES, P])
                    for g, hh in GH:
                        level(0, g, hh)
                    dve.wait_ge(S["levelled"], levels_done(0))
                    for g, hh in GH:
                        b, r = at("inv0", d, g, hh)
                        dve.wait_ge(full[b], r + 1)
                        nc.vector.tensor_tensor(DT[:, g, hh, :, :], Ak[:, g, hh, :, :], eye, ALU.add)
                        nc.vector.tensor_tensor(Dm[:, g, hh, :, :], bank[b][:, 0:TOK].rearrange("p (t n) -> p t n", t=TILES),
                                                eye, ALU.add).then_inc(free[b], 1)
                    for g, hh in GH:
                        b, r = at("inv0", d, g, hh)
                        dve.wait_ge(free[b], r + 1)
                        level(1, g, hh)
                    for lev in range(1, N_LEVELS):
                        for g, hh in GH:
                            for name, dst in (("invX", Dm), ("invXT", DT)):
                                if name == "invX" and lev == N_LEVELS - 1:
                                    continue
                                b, r = at(name, d, lev, g, hh)
                                dve.wait_ge(full[b], r + 1)
                                nc.vector.tensor_tensor(dst[:, g, hh, :, :], dst[:, g, hh, :, :],
                                                        bank[b][:, 0:TOK].rearrange("p (t n) -> p t n", t=TILES),
                                                        ALU.add).then_inc(free[b], 1)
                            if lev < N_LEVELS - 1:
                                level(lev + 1, g, hh)
                    for g, t in GT:
                        b, r = at("EF", d, g, t)
                        dve.wait_ge(full[b], r + 1)
                        ones2 = headones[:, :].unsqueeze(1).to_broadcast([P, 2, P])
                        eye2 = c.ident[:, :].unsqueeze(1).to_broadcast([P, 2, P])
                        link(nc.vector.tensor_tensor(ET[:, g, t, :, :], bank[b][:, 0:2 * P].rearrange("p (c n) -> p c n", c=2),
                                                     ones2, ALU.mult))
                        nc.vector.tensor_tensor(ET[:, g, t, :, :], ET[:, g, t, :, :], eye2, ALU.add)
                        for ch in range(2):
                            ins = nc.vector.scalar_tensor_tensor(F_at(g, t, ch), bank[b][:, (2 + ch) * P:(3 + ch) * P],
                                                                 decayC[:, d, g, 2 * t + ch:2 * t + ch + 1], headones[:, :],
                                                                 ALU.mult, ALU.mult)
                        ins.then_inc(free[b], 1)
                    for g, t in GT:
                        b, r = at("QZ", d, g, t)
                        dve.wait_ge(full[b], r + 1)
                        nc.vector.tensor_tensor(QT[:, g, t, :], bank[b][:, 0:P], AR[d][:, g, 1, tile_cols(t)], ALU.add)
                        if d == 0:
                            ins = nc.vector.tensor_copy(y[:, g, tile_cols(t)], bank[b][:, P:2 * P])
                        else:
                            ins = nc.vector.tensor_tensor(y[:, g, tile_cols(t)], y[:, g, tile_cols(t)], bank[b][:, P:2 * P], ALU.add)
                        ins.then_inc(free[b], 1)
                    for g in range(2):
                        t0, ch0 = divmod(chunks[d, 0][0], 2)
                        dve.wait_ge(free[at("EF", d, g, t0)[0]], at("EF", d, g, t0)[1] + 1)
                        nc.vector.tensor_copy(state_at(g, 0, 1), F_at(g, t0, ch0)).then_inc(S["seeded"], 1)
                    for g, t in GT:
                        b, r = at("QZ", d, g, t)
                        dve.wait_ge(free[b], r + 1)
                    for n, (s_, step) in enumerate(scans):
                        chunk = chunks[d, s_][step]
                        t, ch = divmod(chunk, 2)
                        for g in range(2):
                            b, r = at("scan", d, s_, step, g)
                            dve.wait_ge(full[b], r + 1)
                            ycols = slice(chunk * CHUNK, (chunk + 1) * CHUNK)
                            ins = None
                            if step < len(chunks[d, s_]) - 1 or s_ == 0:
                                ins = nc.vector.scalar_tensor_tensor(state_at(g, s_, step + 1), bank[b][:, CHUNK:CHUNK + P],
                                                                     decayC[:, d, g, chunk:chunk + 1], F_at(g, t, ch), ALU.mult, ALU.add)
                            if s_ == 0:
                                ins.then_inc(S["state_out"], 1)
                            nc.vector.tensor_tensor(y[:, g, ycols], y[:, g, ycols], bank[b][:, 0:CHUNK], ALU.add).then_inc(free[b], 1)
                        if d == 0:
                            grams(1, *GT[n])
                    if d == 0:
                        grams(1, *GT[len(scans)])
                    for g in range(2):
                        b, r = at("scan", d, 1, 3, g)
                        dve.wait_ge(free[b], r + 1)
                for g in range(2):
                    ins = nc.vector.scalar_tensor_tensor(t_inc[:, g, :], kdsum[:, g, :], cols[:, C_RK + g:C_RK + g + 1],
                                                         r_[:, g, :], ALU.mult, ALU.mult)
                ins.then_inc(S["sums_in"], 1)
                for g in range(2):
                    b, r = at("bonus", g)
                    dve.wait_ge(full[b], r + 1)
                    nc.vector.tensor_tensor(t_inv[:, g, :], bank[b][:, 0:TOK], v_[:, g, :], ALU.mult).then_inc(free[b], 1)
                for g in range(2):
                    b, r = at("mean", g)
                    dve.wait_ge(full[b], r + 1)
                    nc.vector.scalar_tensor_tensor(y[:, g, :], bank[b][:, 0:TOK], -1.0 / HD, y[:, g, :], ALU.mult, ALU.add).then_inc(free[b], 1)
                for g in range(2):
                    b, r = at("mean", g)
                    dve.wait_ge(free[b], r + 1)
                nc.vector.tensor_tensor(t_inc, y[:, :, :], y[:, :, :], ALU.mult).then_inc(S["centred"], 1)
                for g in range(2):
                    b, r = at("var", g)
                    dve.wait_ge(full[b], r + 1)
                    ins = nc.vector.tensor_scalar(t_exc[:, g, :], bank[b][:, 0:TOK], 1.0 / HD, LNX_EPS, ALU.mult, ALU.add)
                    ins.then_inc(free[b], 1)
                dve.wait_ge(S["var_root"], 1)
                link(nc.vector.reciprocal(t_exc, t_exc))
                link(nc.vector.tensor_tensor(y[:, :, :], y[:, :, :], t_exc, ALU.mult))
                for g in range(2):
                    ins = nc.vector.tensor_scalar(y[:, g, :], y[:, g, :], cols[:, C_LG + g:C_LG + g + 1],
                                                  cols[:, C_LB + g:C_LB + g + 1], ALU.mult, ALU.add)
                link(ins)
                link(nc.vector.tensor_tensor(y[:, :, :], y[:, :, :], t_inv, ALU.add))
                for g in range(2):
                    b, r = at("gate", g)
                    dve.wait_ge(free[b], r + 1)
                nc.vector.tensor_tensor(mixT[:, 4:6, :], y[:, :, :], gate[:, :, :], ALU.mult)

            @block.tensor
            def _(pe):
                mm, tr = nc.tensor.matmul, nc.tensor.transpose
                pe.wait_ge(c.rwkv_tables_in, 16 * 7)
                pe.wait_ge(S["kk2_in"], 1)
                for g in range(2):
                    b, r = at("kk2", g)
                    pe.wait_ge(free[b], r)
                    mm(bank[b][:, 0:TOK], headones[:, :], t_inc[:, g, :], start=True, stop=True).then_inc(full[b], 1)
                pe.wait_ge(S["squashed"], 2)
                for d in range(2):
                    for name, base in (("decay", 0), ("rate", 2 * RANK)):
                        rows = slice(base + RANK * d, base + RANK * d + RANK)
                        for g in range(2):
                            b, r = at(name, d, g)
                            pe.wait_ge(free[b], r)
                            mm(bank[b][:, 0:TOK], w_up[rows, g * P:(g + 1) * P], pT[rows, WAB, :], start=True, stop=True).then_inc(full[b], 1)
                for g in range(2):
                    b, r = at("gate", g)
                    pe.wait_ge(free[b], r)
                    mm(bank[b][:, 0:TOK], g_up[:, g * P:(g + 1) * P], pT[0:HD, GB, :], start=True, stop=True).then_inc(full[b], 1)
                for g in range(2):
                    b, r = at("vT", g)
                    pe.wait_ge(free[b], r)
                    for t in range(TILES):
                        ins = tr(bank[b][:, tile_cols(t)], v_[:, g, tile_cols(t)], c.ident[:, :])
                    ins.then_inc(full[b], 1)
                for g in range(2):
                    pe.wait_ge(free[at("vT", g)[0]], at("vT", g)[1] + 1)

                def grams(d, g, t):
                    b, r = at("tokens", d, g, t)
                    pe.wait_ge(free[b], r)
                    for i, src in enumerate((AR[d][:, g, 0, tile_cols(t)], Bf[d][:, g, tile_cols(t)], Kf[d][:, g, tile_cols(t)])):
                        ins = tr(bank[b][:, tile_cols(i)], src, c.ident[:, :])
                    ins.then_inc(full[b], 1)
                    for hh in range(2):
                        b, r = at("gram", d, g, t, hh)
                        pe.wait_ge(free[b], r)
                        rows = slice(HD * hh, HD * hh + HD)
                        for i, src in enumerate((Bf[d], Kf[d])):
                            ins = mm(bank[b][:, 2 * i * P:2 * (i + 1) * P].rearrange("p (w n) -> p w n", w=2),
                                     src[rows, g, tile_cols(t)], AR[d][rows, g, :, tile_cols(t)], start=True, stop=True)
                        ins.then_inc(full[b], 1)

                pe.wait_ge(S["chunk_ops"], 2)
                for g, t in GT:
                    grams(0, g, t)
                for d in range(2):
                    lv = lambda lev, g, hh: 4 * (d * N_LEVELS + lev) + 2 * g + hh + 1
                    for g, hh in GH:
                        b, r = at("inv0", d, g, hh)
                        pe.wait_ge(S["levelled"], lv(0, g, hh))
                        pe.wait_ge(free[b], r)
                        for t in range(TILES):
                            ins = tr(bank[b][:, tile_cols(t)], Ak[:, g, hh, t, :], c.ident[:, :])
                        ins.then_inc(full[b], 1)
                    for lev in range(1, N_LEVELS):
                        for g, hh in GH:
                            b, r = at("invY", d, lev, g, hh)
                            pe.wait_ge(S["levelled"], lv(lev, g, hh))
                            pe.wait_ge(free[b], r)
                            for t in range(TILES):
                                ins = mm(bank[b][:, tile_cols(t)], Ak[:, g, hh, t, :], Dm[:, g, hh, t, :], start=True, stop=True)
                            ins.then_inc(full[b], 1)
                        for g, hh in GH:
                            yb, yr = at("invY", d, lev, g, hh)
                            pe.wait_ge(free[yb], yr + 1)
                            for name in ("invX", "invXT"):
                                if name == "invX" and lev == N_LEVELS - 1:
                                    continue
                                b, r = at(name, d, lev, g, hh)
                                pe.wait_ge(free[b], r)
                                for t in range(TILES):
                                    Yt, Dt = Ym[:, g, hh, t, :], DT[:, g, hh, t, :]
                                    ins = mm(bank[b][:, tile_cols(t)], *((Dt, Yt) if name == "invX" else (Yt, Dt)), start=True, stop=True)
                                ins.then_inc(full[b], 1)
                    for g, hh in GH:
                        b, r = at("invXT", d, N_LEVELS - 1, g, hh)
                        pe.wait_ge(free[b], r + 1)
                    for g, t in GT:
                        b, r = at("tokens", d, g, t)
                        pe.wait_ge(free[b], r + 1)
                        b, r = at("GW", d, g, t)
                        pe.wait_ge(free[b], r)
                        for hh in range(2):
                            h0 = HD * hh
                            mm(bank[b][:, h0:h0 + HD], DT[:, g, hh, t, :], A_tok[:, g, t, h0:h0 + HD], start=True, stop=True)
                            ins = mm(bank[b][:, P + h0:P + h0 + HD], M[:, g, hh, t, 2, :], v_tok[:, t, g * P + h0:g * P + h0 + HD],
                                     start=True, stop=True)
                        ins.then_inc(full[b], 1)
                    for g, t in GT:
                        b, r = at("GW", d, g, t)
                        pe.wait_ge(free[b], r + 1)
                        b, r = at("H", d, g, t)
                        pe.wait_ge(free[b], r)
                        for hh in range(2):
                            h0 = HD * hh
                            ins = mm(bank[b][:, h0:h0 + HD], DT[:, g, hh, t, :], GW[:, g, t, P + h0:P + h0 + HD], start=True, stop=True)
                        ins.then_inc(full[b], 1)
                    for g, t in GT:
                        b, r = at("H", d, g, t)
                        pe.wait_ge(free[b], r + 1)
                        b, r = at("EF", d, g, t)
                        pe.wait_ge(free[b], r)
                        mm(bank[b][:, 0:2 * P], GW[:, g, t, 0:P], BK_tok[:, g, t, 0, :, :].rearrange("p c n -> p (c n)"), start=True, stop=True)
                        for ch in range(2):
                            out = bank[b][:, (2 + ch) * P:(3 + ch) * P]
                            mm(out, BK_tok[:, g, t, 0, ch, :], H[:, g, t, :], start=True, stop=False)
                            ins = mm(out, BK_tok[:, g, t, 1, ch, :], v_tok[:, t, g * P:(g + 1) * P], start=False, stop=True)
                        ins.then_inc(full[b], 1)
                    for g, t in GT:
                        b, r = at("QZ", d, g, t)
                        pe.wait_ge(free[b], r)
                        for hh in range(2):
                            rows = slice(HD * hh, HD * hh + HD)
                            mm(bank[b][rows, 0:P], GW[:, g, t, rows], M[:, g, hh, t, 1, :], start=True, stop=True)
                        for hh in range(2):
                            rows = slice(HD * hh, HD * hh + HD)
                            mm(bank[b][rows, P:2 * P], H[:, g, t, rows], M[:, g, hh, t, 1, :], start=True, stop=False)
                            ins = mm(bank[b][rows, P:2 * P], v_tok[:, t, g * P + HD * hh:g * P + HD * hh + HD],
                                     M[:, g, hh, t, 3, :], start=False, stop=True)
                        ins.then_inc(full[b], 1)
                    pe.wait_ge(S["states_in"], 16 * 8)
                    pe.wait_ge(S["seeded"], 2 * (d + 1))
                    for g, t in GT:
                        b, r = at("QZ", d, g, t)
                        pe.wait_ge(free[b], r + 1)
                    if d == 0:
                        pe.wait_ge(S["chunk_ops"], 4)
                    for n, (s_, step) in enumerate(scans):
                        chunk = chunks[d, s_][step]
                        t, ch = divmod(chunk, 2)
                        for g in range(2):
                            if step > 0 and (s_, step) != (0, 1):
                                pb, pr = at("scan", d, s_, step - 1, g)
                                pe.wait_ge(free[pb], pr + 1)
                            S_in = s_init[:, d, g, :] if step == 0 else state_at(g, s_, step)
                            b, r = at("scan", d, s_, step, g)
                            pe.wait_ge(free[b], r)
                            ins = mm(bank[b][:, 0:CHUNK], S_in, QT[:, g, t, ch * CHUNK:(ch + 1) * CHUNK], start=True, stop=True)
                            if step < len(chunks[d, s_]) - 1 or s_ == 0:
                                ins = mm(bank[b][:, CHUNK:CHUNK + P], ET[:, g, t, ch, :], S_in, start=True, stop=True)
                            ins.then_inc(full[b], 1)
                        if d == 0:
                            grams(1, *GT[n])
                    if d == 0:
                        grams(1, *GT[len(scans)])
                pe.wait_ge(S["sums_in"], 1)
                for name, src in (("bonus", t_inc), ("mean", y), ("var", t_inc)):
                    if name == "var":
                        pe.wait_ge(S["centred"], 1)
                    for g in range(2):
                        b, r = at(name, g)
                        pe.wait_ge(free[b], r)
                        mm(bank[b][:, 0:TOK], headones[:, :], src[:, g, :], start=True, stop=True).then_inc(full[b], 1)
        clear(nc, s.sems + [c.rwkv_tables_in])


def output(c, l, pT, mixT):
    nc, dram = c.nc, c.dram
    parts = [("out", 0, n) for n in range(N_POUT)] + [("out", 1, n) for n in range(N_POUT)] + feature_turns(0)
    parts += [("out", 2, n) for n in range(N_POUT - 1)] + feature_turns(1) + [("out", 2, N_POUT - 1)] + feature_turns(2)
    NW = PIECE // KD
    with ExitStack() as ctx:
        s = Stage(c, ctx, "output", parts, ["w_high", "w_low", "h_high", "h_low", "x_in", "vdone", "var_ready",
                                            "std_ready", "normed", "stored"])
        at, bank, full, free, S = s.steps.at, s.bank, s.full, s.free, s.named
        place = lambda block: pT[:, block:block + KD, :].rearrange("p k n -> p (k n)").rearrange("p (t n) -> p t n", t=TILES)
        x, part, gates, gb = place(0), place(KD), s.sb("gates", [P, 2, D]), s.sb("gb", [P, 2, D])
        stats, mv, rstd = s.sb("stats", [P, TILES, 12]), s.sb("mv", [P, TILES, 2]), s.sb("rstd", [P, TILES])
        hs, ws = s.sb("hs", [P, 2, KD, TOK], F32R), s.sb("ws", [P, N_POUT, 2, PIECE], F32R)
        with nc.Block() as block:

            @block.sync
            def _(sp):
                load_for_norm(c, l, sp, S["x_in"], (x, gates, gb), 0, "ln1")
                refill(c, s, sp, l, AT_OUT, N_POUT)
                for t in range(TILES):
                    sp.wait_ge(S["normed"], t + 1)
                    sp.dma_start(c.x_dram[t], x[:, t, :]).then_inc(S["stored"], 16)
                sp.wait_ge(S["stored"], 16 * TILES)

            @block.scalar
            def _(act):
                split_high(c, s, act, AT_OUT, 0, ws)
                split_rows_high(c, s, act, mixT, hs, [0])
                for m in range(1, N_POUT):
                    split_high(c, s, act, AT_OUT, m, ws)
                split_rows_high(c, s, act, mixT, hs, [1, 2])
                for t in range(TILES):
                    act.wait_ge(S["var_ready"], t + 1)
                    nc.scalar.activation(rstd[:, t:t + 1], mv[:, t, 1:2], ACT.Sqrt).then_inc(S["std_ready"], 1)
                    if t > 0:
                        modulate(c, s, act, 1, t - 1, 1)
                modulate(c, s, act, 1, TILES - 1, 1)

            @block.vector
            def _(dve):
                link = in_order(dve, S["vdone"])
                split_low(c, s, dve, AT_OUT, 0, ws)
                split_rows_low(c, s, dve, mixT, hs, [0])
                for m in range(1, N_POUT):
                    split_low(c, s, dve, AT_OUT, m, ws)
                split_rows_low(c, s, dve, mixT, hs, [1, 2])
                dve.wait_ge(S["x_in"], 16 * LOADS_FOR_NORM)
                for t in range(TILES):
                    for n in range(N_POUT):
                        if (t, n) == (TILES - 1, N_POUT - 1):
                            modulate(c, s, dve, 1, 1, 0)
                        b, r = at("out", t, n)
                        cols = slice(n * NW, (n + 1) * NW)
                        dve.wait_ge(full[b], r + 1)
                        nc.vector.tensor_tensor(part[:, t, cols], bank[b][:, 0:NW], gates[:, SEQ_OF_TILE[t], cols], ALU.mult).then_inc(free[b], 1)
                    for n in range(N_POUT):
                        b, r = at("out", t, n)
                        dve.wait_ge(free[b], r + 1)
                    link(nc.vector.scalar_tensor_tensor(x[:, t, :], x[:, t, :], ALPHA, part[:, t, :], ALU.mult, ALU.add))
                    norm_steps(nc, dve, link, x[:, t, :], stats[:, t, :], mv[:, t, :], rstd[:, t:t + 1], S["var_ready"],
                               S["std_ready"], t + 1, gb[:, 0, :], gb[:, 1, :], x[:, t, :]).then_inc(S["normed"], 1)
                    if t != 0:
                        modulate(c, s, dve, 1, 0 if t == 1 else 2, 0)

            @block.tensor
            def _(pe):
                def products(t, n):
                    b, r = at("out", t, n)
                    pe.wait_ge(free[b], r)
                    pe.wait_ge(S["h_low"], t + 1)
                    pe.wait_ge(S["w_low"], n + 1)
                    w = ws[:, n].rearrange("p s (k n) -> p s k n", k=KD)
                    for k in range(KD):
                        for i, (v, a) in enumerate(PASSES):
                            ins = nc.tensor.matmul(bank[b][:, 0:NW], hs[:, v, k, t * P:(t + 1) * P], w[:, a, k, :],
                                                   start=(k == 0 and i == 0), stop=(k == KD - 1 and i == 2))
                    ins.then_inc(full[b], 1)

                def features(t):
                    pe.wait_ge(S["normed"], t + 1)
                    transpose_x(c, s, pe, x, t)

                for t in range(2):
                    for n in range(N_POUT):
                        products(t, n)
                features(0)
                for n in range(N_POUT - 1):
                    products(2, n)
                features(1)
                products(2, N_POUT - 1)
                features(2)
        clear(nc, s.sems)


LOADS_FOR_NORM = TILES + 4
NORM_IN = LOADS_FOR_NORM * D


def norm_inputs(buffer):
    view = lambda at, n: buffer[:, at * D:(at + n) * D].rearrange("p (t n) -> p t n", t=n)
    return view(0, TILES), view(TILES, 2), view(TILES + 2, 2)


def load_for_norm(c, l, eng, loaded, views, which, name):
    x, gates, gb = views
    for t in range(TILES):
        eng.dma_start(x[:, t, :], c.x_dram[t]).then_inc(loaded, 16)
    for i in range(2):
        gate = c.gate_dram[bass.ds(l, 1), which, i]
        eng.dma_start(gates[:, i, :], gate.rearrange("a n -> (a n)").partition_broadcast(P)).then_inc(loaded, 16)
    for i in range(2):
        eng.dma_start(gb[:, i, :], layer_row(c.dram[name], l)[i].partition_broadcast(P)).then_inc(loaded, 16)


SHORT = 4
LONG_ROWS = SHORT * TOPK
CAND = LONG_ROWS + (TOPK - SHORT) * SHORT


def routing(c, l, xs, route):
    nc, dram = c.nc, c.dram
    HP = 2 * PH
    scoring = [("q", 0)] + [item for n in range(1, HP) for item in (("q", n), ("sc", n - 1))] + [("sc", HP - 1)]
    turns = list(scoring)
    work = []
    for n in range(N_EARLY):
        work.append(("ada", n))
        work += [("route", t) for t in range(TILES) if n + 1 == (9, 14, 20)[t]]
        work += [("exps", t) for t in range(TILES) if n + 1 == (5, 11, 16)[t]]
    turns += [item for item in work if item[0] != "exps"] + [("cols",)]
    with ExitStack() as ctx:
        s = Stage(c, ctx, "route", turns, ["w_high", "w_low", "h_high", "h_low", "counted", "indexed", "pdone", "bias_in", "gates_stored", "keys_in", "vdone", "normed", "exp_asked", "exps", "routed", "split"])
        at, bank, full, free, S = s.steps.at, s.bank, s.full, s.free, s.named
        hT, rows_mod = c.hT, s.sb("rows_mod", [2, 5 * D])
        ws = s.sb("ws", [P, 2, 2, PIECE], F32R)
        qT, keys, sc = s.sb("qT", [P, HP, TOK]), s.sb("keys", [P, HP, NK]), s.sb("sc", [P, HP, TILES, NK])
        top, idx = s.sb("top", [P, TILES, HP, TOPK]), s.sb("idx", [P, TILES, HP, TOPK], U32)
        spares, used = hT[:, :, :].rearrange("p k n -> p (k n)"), [0]

        def spare(n):
            used[0] += n
            return spares[:, used[0] - n:used[0]]

        cand = spare(PH * CAND).rearrange("p (h n) -> p h n", h=PH)
        best, pos = s.sb("best", [P, PH, TOPK]), s.sb("pos", [P, PH, TOPK], U32)
        shifted = s.sb("shifted", [P, 2, PH * TOPK], U32)
        place = spare(2 * PH * TOPK).rearrange("p (w k) -> p w k", w=2)
        posf, start = spare(PH * TOPK), spare(PH * TOPK)
        iota16 = s.sb("iota16", [P, TOPK])
        pick = qT[:, :, :].rearrange("p n t -> p (n t)")[:, 0:2 * PH * TOPK * TOPK]
        pick = pick.rearrange("p (w k a) -> p w k a", w=2, a=TOPK)
        chosen = spare(3 * PH * TOPK).rearrange("p (w k) -> p w k", w=3)
        rows = s.sb("rows", [P, 2, PH])
        rest, gT = spare(TOK), spare(TOK)
        idxf = [spare(HP * TOPK).rearrange("p (h k) -> p h k", h=HP) for _ in range(2)]

        def picks(w):
            return pick[:, w, :, :].rearrange("p (h k) a -> p h k a", h=PH)

        def tables(t, w):
            found = idxf[t % 2].rearrange("p (h two) k -> p h two k", two=2)[:, :, w, :]
            return found.unsqueeze(2).to_broadcast([P, PH, TOPK, TOPK])

        with nc.Block() as block:

            @block.gpsimd
            def _(pool):
                link = in_order(pool, S["pdone"])
                for t in range(TILES):
                    pool.wait_ge(S["counted"], t + 1)
                    link(nc.gpsimd.tensor_tensor(picks(0), picks(0), tables(t, 0), ALU.mult))
                    n = TOPK // 2
                    while n > 1:
                        link(nc.gpsimd.tensor_tensor(pick[:, 0, :, 0:n], pick[:, 0, :, 0:n], pick[:, 0, :, n:2 * n], ALU.add))
                        n //= 2
                    if t > 0:
                        b, r = at("route", t - 1)
                        pool.wait_ge(full[b], r + 1)
                    ins = nc.gpsimd.tensor_tensor(chosen[:, 0, :].unsqueeze(2), pick[:, 0, :, 0:1], pick[:, 0, :, 1:2], ALU.add)
                    ins.then_inc(S["indexed"], 1)

            @block.sync
            def _(sp):
                refill(c, s, sp, l, AT_Q, N_PQ)
                for n in range(AT_ADA + SLOTS, AT_EXP + SLOTS):
                    b, r = at("ada", n - SLOTS - AT_ADA)
                    sp.wait_ge(full[b], r + 1)
                    fill_slot(c, sp, l, n)

            @block.scalar
            def _(act):
                act.dma_start(rows_mod[0:1, :], dram["b_ada"][NEXT:NEXT + 1, 0:5 * D]).then_inc(S["bias_in"], 16)
                act.dma_start(keys[:, :, :], layer_row(dram["subkeys_T"], l)).then_inc(S["keys_in"], 16)
                act.dma_start(iota16[:, :], dram["iota16"]).then_inc(S["keys_in"], 16)
                split_high(c, s, act, AT_Q, 0, ws)
                split_rows_high(c, s, act, hT, xs)
                split_high(c, s, act, AT_Q, 1, ws)
                for what, n in scoring:
                    b, r = at(what, n)
                    act.wait_ge(full[b], r + 1)
                    if what == "sc":
                        nc.scalar.copy(sc[:, n, :, :], bank[b][:, 0:TOK].rearrange("p (t n) -> p t n", t=TILES)).then_inc(free[b], 1)
                        continue
                    nc.scalar.copy(qT[:, n, :], bank[b][:, 0:TOK]).then_inc(free[b], 1)
                    if n % 2 == 1 and n // 2 + 2 < N_PQ:
                        split_high(c, s, act, AT_Q, n // 2 + 2, ws, at("q", n))
                for what, n in work:
                    if what == "ada":
                        ada_copy(c, s, act, rows_mod, n)
                    elif what == "exps":
                        act.wait_ge(S["exp_asked"], n + 1)
                        nc.scalar.activation(chosen[:, 2, :], chosen[:, 2, :], ACT.Exp).then_inc(S["exps"], 1)
                    else:
                        b, r = at("route", n)
                        act.wait_ge(full[b], r + 1)
                        cols = slice(n * P, (n + 1) * P)
                        nc.scalar.copy(route[:, 0:2, cols], bank[b][:, 0:2 * P].rearrange("p (w n) -> p w n", w=2))
                        nc.scalar.copy(gT[:, cols], bank[b][:, 2 * P:3 * P]).then_inc(free[b], 1)
                store_gate(c, s, act, rows_mod[:, 2 * D:3 * D], 0, gate_place(c, l + 1, 0), S["gates_stored"])
                act.wait_ge(S["gates_stored"], 16)

            @block.vector
            def _(dve):
                link = in_order(dve, S["vdone"])
                V = nc.vector
                split_low(c, s, dve, AT_Q, 0, ws)
                split_rows_low(c, s, dve, hT, xs)
                split_low(c, s, dve, AT_Q, 1, ws)
                for m in range(N_PQ):
                    if m + 2 < N_PQ:
                        split_low(c, s, dve, AT_Q, m + 2, ws)
                    half_heads = (2 * m, 2 * m + 1)
                    for n in half_heads:
                        b, r = at("sc", n)
                        dve.wait_ge(free[b], r + 1)
                    each = [(n, t) for n in half_heads for t in range(TILES)]
                    for r8 in range(2):
                        part = slice(8 * r8, 8 * r8 + 8)
                        for n, t in each:
                            ins = V.max(top[:, t, n, part], sc[:, n, t, :])
                        link(ins)
                        for n, t in each:
                            ins = V.max_index(idx[:, t, n, part], top[:, t, n, part], sc[:, n, t, :])
                        if r8 == 0:
                            for n, t in each:
                                ins = V.match_replace(sc[:, n, t, :], top[:, t, n, part], sc[:, n, t, :], NEG)
                        link(ins)
                c3 = chosen[:, 2, :].rearrange("p (h k) -> p h k", h=PH)

                def softmax_rest(t):
                    dve.wait_ge(S["exps"], t + 1)
                    link(V.tensor_reduce(rows[:, 0, :], c3, AX.X, ALU.add))
                    link(V.reciprocal(rows[:, 1, :], rows[:, 0, :]))
                    V.tensor_tensor(c3, c3, rows[:, 1, :].unsqueeze(2).to_broadcast([P, PH, TOPK]), ALU.mult).then_inc(S["routed"], 1)

                dve.wait_ge(S["keys_in"], 32)
                dve.wait_ge(S["h_low"], TILES)
                for t in range(TILES):
                    if t > 1:
                        dve.wait_ge(S["indexed"], t - 1)
                    V.tensor_copy(idxf[t % 2], idx[:, t, :, :])
                    tops = top[:, t, :, :].rearrange("p (h two) k -> p h two k", two=2)
                    half0, half1, long = tops[:, :, 0, :], tops[:, :, 1, :], [P, PH, SHORT, TOPK]
                    V.tensor_tensor(cand[:, :, 0:LONG_ROWS].rearrange("p h (a b) -> p h a b", a=SHORT),
                                    half0[:, :, 0:SHORT].unsqueeze(3).to_broadcast(long),
                                    half1.unsqueeze(2).to_broadcast(long), ALU.add)
                    short = [P, PH, TOPK - SHORT, SHORT]
                    ins = V.tensor_tensor(cand[:, :, LONG_ROWS:CAND].rearrange("p h (a b) -> p h a b", b=SHORT),
                                          half0[:, :, SHORT:TOPK].unsqueeze(3).to_broadcast(short),
                                          half1[:, :, 0:SHORT].unsqueeze(2).to_broadcast(short), ALU.add)
                    link(ins)
                    for r8 in range(2):
                        part = slice(8 * r8, 8 * r8 + 8)
                        for h in range(PH):
                            ins = V.max(best[:, h, part], cand[:, h, :])
                        link(ins)
                        for h in range(PH):
                            ins = V.max_index(pos[:, h, part], best[:, h, part], cand[:, h, :])
                        if r8 == 0:
                            for h in range(PH):
                                ins = V.match_replace(cand[:, h, :], best[:, h, part], cand[:, h, :], NEG)
                        link(ins)
                        if r8 == 0 and t > 0:
                            softmax_rest(t - 1)
                    flat = pos[:, :, :].rearrange("p h k -> p (h k)")
                    V.tensor_copy(posf[:, :], flat)
                    V.tensor_scalar(shifted[:, 0, :], flat, 4, None, ALU.logical_shift_right)
                    link(V.tensor_scalar(shifted[:, 1, :], flat, 2, None, ALU.logical_shift_right))
                    link(V.tensor_copy(place[:, :, :], shifted[:, :, :]))
                    link(V.scalar_tensor_tensor(place[:, 0, :], place[:, 1, :], float(LONG_ROWS // SHORT - SHORT), place[:, 0, :],
                                                ALU.subtract, ALU.max))
                    link(V.tensor_scalar(start[:, :], place[:, 0, :], float(SHORT), float(LONG_ROWS - SHORT * SHORT), ALU.mult, ALU.add))
                    link(V.scalar_tensor_tensor(start[:, :], place[:, 0, :], float(TOPK), start[:, :], ALU.mult, ALU.min))
                    if t > 0:
                        b, r = at("route", t - 1)
                        dve.wait_ge(full[b], r + 1)
                    link(V.tensor_tensor(place[:, 1, :], posf[:, :], start[:, :], ALU.subtract))
                    numbers = iota16[:, :].unsqueeze(1).to_broadcast([P, PH * TOPK, TOPK])
                    if t > 0:
                        dve.wait_ge(S["indexed"], t)
                    for w in range(2):
                        ins = V.tensor_tensor(pick[:, w, :, :], place[:, w, :].unsqueeze(2).to_broadcast([P, PH * TOPK, TOPK]),
                                              numbers, ALU.is_equal)
                        if w == 0:
                            ins.then_inc(S["counted"], 1)
                    link(ins)
                    link(V.tensor_tensor(picks(1), picks(1), tables(t, 1), ALU.mult))
                    V.tensor_reduce(chosen[:, 1, :], pick[:, 1, :, :], AX.X, ALU.add)
                    V.tensor_tensor(c3, best[:, :, :], best[:, :, 0:1].to_broadcast([P, PH, TOPK]),
                                    ALU.subtract).then_inc(S["exp_asked"], 1)
                softmax_rest(TILES - 1)
                for t in range(TILES):
                    b, r = at("route", t)
                    dve.wait_ge(free[b], r + 1)
                link(V.tensor_copy(route[:, 2, :], gT[:, :]))
                link(V.tensor_tensor(rest[:, :], gT[:, :], route[:, 2, :], ALU.subtract))
                link(V.tensor_copy(route[:, 3, :], rest[:, :]))
                V.tensor_tensor(route[:, 4, :], rest[:, :], route[:, 3, :], ALU.subtract)
                ada_columns(c, s, dve)

            @block.tensor
            def _(pe):
                pe.wait_ge(S["h_low"], TILES)
                pe.wait_ge(S["keys_in"], 32)
                for what, n in scoring:
                    if what == "q":
                        weight_blocks_times_h(c, s, pe, n, at("q", n), ws, xs)
                        continue
                    b, r = at("q", n)
                    pe.wait_ge(free[b], r + 1)
                    b, r = at("sc", n)
                    pe.wait_ge(free[b], r)
                    for t in range(TILES):
                        ins = nc.tensor.matmul(bank[b][:, t * P:(t + 1) * P], qT[:, n, t * P:(t + 1) * P],
                                               keys[:, n, :], start=True, stop=True)
                    ins.then_inc(full[b], 1)
                pe.wait_ge(S["bias_in"], 16)
                for what, n in work:
                    if what == "ada":
                        m = AT_ADA + n
                        ada_product(c, s, pe, rows_mod, c.ring_full[slot(m)], filled(m), slot(m), n)
                    elif what == "route":
                        b, r = at("route", n)
                        pe.wait_ge(S["routed"], n + 1)
                        pe.wait_ge(S["indexed"], n + 1)
                        pe.wait_ge(free[b], r)
                        for w in range(3):
                            ins = nc.tensor.transpose(bank[b][:, w * P:(w + 1) * P], chosen[:, w, :], c.ident[:, :])
                        ins.then_inc(full[b], 1)
                ada_transposes(c, s, pe, rows_mod)
        clear(nc, s.sems)


def experts(c, l, xs, route, acc, W, late):
    nc, dram = c.nc, c.dram
    STEPS = NK
    BT = TOK // JG
    UN = 4
    with ExitStack() as ctx:
        sem = lambda name: ctx.enter_context(nc.semaphore("exp_" + name))
        sb = lambda name, shape, dt=F32: ctx.enter_context(nc.sbuf_tensor("exp_" + name, shape, dt))
        Us, Vs = sb("Us", [P, 2, 2, D], F32R), sb("Vs", [P, 2, D], F32R)
        spare = c.hT[:, :, :].rearrange("p k n -> p (k n)")
        gel, wa = spare[:, 0:TOK], spare[:, TOK:2 * TOK]
        Ai = spare[:, 2 * TOK:2 * TOK + BT * NK].bitcast(BF16).rearrange("p (b t n) -> p b t n", b=2, t=BT)
        was = sb("was", [P, 2, 2, TOK], F32R)
        Bj = sb("Bj", [P, 2, 4, BT, JG], BF16)
        iota = sb("iota", [P, NK + JG], BF16)
        act_bank = ctx.enter_context(nc.psum_tensor("exp_act", [P, 512], F32))
        w_bank = ctx.enter_context(nc.psum_tensor("exp_w", [P, 512], F32))
        iota_in, zeroed = sem("iota_in"), sem("zeroed")
        u_hi, u_lo, v_hi, v_lo = sem("u_hi"), sem("u_lo"), sem("v_hi"), sem("v_lo")
        act_done, acc_done, w_done = sem("act_done"), sem("acc_done"), sem("w_done")
        gelu_done, wa_done, wa_hi, wa_lo = sem("gelu_done"), sem("wa_done"), sem("wa_hi"), sem("wa_lo")
        ai_ready, bj_hot, bj_ready, w_stored = sem("ai_ready"), sem("bj_hot"), sem("bj_ready"), sem("w_stored")
        sems = [iota_in, zeroed, u_hi, u_lo, v_hi, v_lo, act_done, acc_done, w_done, gelu_done, wa_done, wa_hi, wa_lo,
                ai_ready, bj_hot, bj_ready, w_stored]
        U_PIECE, V_PIECE = (0, 2), (1, 3)

        def at_slot(q):
            return slot(AT_EXP + q)

        def have(q, it):
            return filled(AT_EXP + q) + 16 * it

        def part_of(q, u):
            return c.ring[:, at_slot(q), (u % 2) * D:(u % 2 + 1) * D]

        PER = JG // UN
        CHUNKS = STEPS // JG

        def main_loop(eng, body):
            for chunk in range(CHUNKS):
                with eng.Fori(0, PER - (chunk == CHUNKS - 1)) as it8:
                    for u in range(UN):
                        body(it8 + chunk * PER, it8, chunk, u, it8 * UN + (chunk * JG + u), False)
            for u in range(UN):
                body(STEPS // UN - 1, PER - 1, CHUNKS - 1, u, STEPS - UN + u, u == UN - 1)

        with nc.Block() as block:

            @block.sync
            def _(sp):
                sp.dma_start(iota[:, :], dram["iota"]).then_inc(iota_in, 16)
                with sp.Fori(1, STEPS // UN) as it:
                    for q in range(4):
                        steps_split = it * UN - UN + 2 * (q // 2 + 1)
                        if q % 2 == 0:
                            sp.wait_ge(u_lo, steps_split)
                        else:
                            sp.wait_ge(v_lo, steps_split * 2 + 1)
                        src = dram["uv"[q % 2]][bass.ds(l, 1), bass.ds(it * 2 + q // 2, 1)]
                        sp.dma_start(c.ring[:, at_slot(q), :], src.rearrange("a b p n -> (a b p) n")).then_inc(c.ring_full[at_slot(q)], 16)

            @block.gpsimd
            def _(pool):
                nc.gpsimd.memset(was[:, 1, :, :].bitcast(F32), 0.0).then_inc(zeroed, 1)
                nc.gpsimd.memset(Vs[:, :, :].bitcast(F32), 0.0).then_inc(zeroed, 1)

                def scale_one_hot(m, it8, u):
                    tok = it8 * (UN * BT) + u * BT
                    pool.wait_ge(bj_hot, m + 1)
                    for i in range(3):
                        ins = nc.gpsimd.tensor_tensor(Bj[:, u % 2, 1 + i, :, :], Bj[:, u % 2, 0, :, :],
                                                      route[:, 2 + i, bass.ds(tok, BT)].unsqueeze(2).to_broadcast([P, BT, JG]), ALU.mult)
                    ins.then_inc(bj_ready, 1)

                pool.sem_inc(v_lo, 1)
                with pool.Fori(0, JG // UN) as it8:
                    for u in range(UN):
                        scale_one_hot(it8 * UN + u, it8, u)

                def step(it, it8, chunk, u, j, last):
                    if chunk < CHUNKS - 1:
                        scale_one_hot(j + JG, it8, u)
                    q = V_PIECE[u // 2]
                    for h in range(2):
                        cols = slice(512 * h, 512 * h + 512)
                        pool.wait_ge(v_hi, 2 * j + (h + 1))
                        nc.gpsimd.tensor_tensor(Vs[:, 1, cols], part_of(q, u)[:, cols], Vs[:, 0, cols].bitcast(F32),
                                                ALU.subtract).then_inc(v_lo, 1)

                main_loop(pool, step)

            @block.scalar
            def _(act):
                def step(it, it8, chunk, u, j, last):
                    if isinstance(j, int) and j == STEPS - UN:
                        load_for_norm(c, l, act, c.late_in, late, 1, "ln2")
                    act.wait_ge(act_done, j + 3)
                    nc.scalar.activation(gel[:, :], act_bank[:, 0:TOK], ACT.Gelu_apprx_tanh).then_inc(gelu_done, 1)
                    act.wait_ge(wa_done, j + 1)
                    act.wait_ge(acc_done, 2 * j + 1)
                    nc.scalar.copy(was[:, u % 2, 0, :], wa[:, :]).then_inc(wa_hi, 1)
                    q = V_PIECE[u // 2]
                    act.wait_ge(c.ring_full[at_slot(q)], have(q, it))
                    for h in range(2):
                        cols = slice(512 * h, 512 * h + 512)
                        act.wait_ge(acc_done, 2 * j + (h + 2))
                        nc.scalar.copy(Vs[:, 0, cols], part_of(q, u)[:, cols]).then_inc(v_hi, 1)

                act.sem_inc(gelu_done, 1)
                with act.Fori(0, JG // UN) as it8:
                    for u in range(UN):
                        act.wait_ge(w_done, it8 * UN + (u + 3))
                        nc.scalar.copy(W[:, 0, bass.ds(it8 * (UN * BT) + u * BT, BT), :],
                                       w_bank[:, 0:BT * JG].rearrange("p (t n) -> p t n", t=BT)).then_inc(w_stored, 1)
                main_loop(act, step)

            @block.vector
            def _(dve):
                V = nc.vector

                def build_one_hot(m, it8, u, base):
                    tok = it8 * (UN * BT) + u * BT
                    numbers = iota[:, bass.ds(base, JG)].unsqueeze(1).to_broadcast([P, BT, JG])
                    dve.wait_ge(w_done, m + 1)
                    V.tensor_tensor(Bj[:, u % 2, 0, :, :], numbers,
                                    route[:, 1, bass.ds(tok, BT)].unsqueeze(2).to_broadcast([P, BT, JG]),
                                    ALU.is_equal).then_inc(bj_hot, 1)
                    V.tensor_tensor(Ai[:, u % 2, :, :], iota[:, 0:NK].unsqueeze(1).to_broadcast([P, BT, NK]),
                                    route[:, 0, bass.ds(tok, BT)].unsqueeze(2).to_broadcast([P, BT, NK]),
                                    ALU.is_equal).then_inc(ai_ready, 1)

                def store_w(m, it8, u, buf):
                    tok = it8 * (UN * BT) + u * BT
                    dve.wait_ge(w_done, m + 3)
                    V.tensor_copy(W[:, buf, bass.ds(tok, BT), :],
                                  w_bank[:, 0:BT * JG].rearrange("p (t n) -> p t n", t=BT)).then_inc(w_stored, 1)

                dve.sem_inc(wa_lo, 1)
                dve.sem_inc(w_stored, 1)
                dve.wait_ge(iota_in, 16)
                with dve.Fori(0, JG // UN) as it8:
                    for u in range(UN):
                        build_one_hot(it8 * UN + u, it8, u, 0)

                def split_u(it, u, j):
                    q = U_PIECE[u // 2]
                    dve.wait_ge(c.ring_full[at_slot(q)], have(q, it))
                    dve.wait_ge(act_done, j + 1)
                    V.tensor_copy(Us[:, u % 2, 0, :], part_of(q, u)).then_inc(u_hi, 1)
                    dve.wait_ge(u_hi, j + 1)
                    V.tensor_tensor(Us[:, u % 2, 1, :], part_of(q, u), Us[:, u % 2, 0, :].bitcast(F32),
                                    ALU.subtract).then_inc(u_lo, 1)

                def step(it, it8, chunk, u, j, last):
                    if chunk < CHUNKS - 1:
                        build_one_hot(j + JG, it8, u, (chunk + 1) * JG)
                    elif not last:
                        split_u(it + (u + 1) // UN, (u + 1) % UN, j + 1)
                    dve.wait_ge(gelu_done, j + 2)
                    dve.wait_ge(wa_lo, j + 1)
                    dve.wait_ge(w_stored, (chunk + 1) * JG + 1)
                    V.tensor_tensor(wa[:, :], gel[:, :], W[:, chunk % 2, :, bass.ds(it8 * UN + u, 1)].rearrange("p t a -> p (t a)"),
                                    ALU.mult).then_inc(wa_done, 1)
                    dve.wait_ge(wa_hi, j + 1)
                    V.tensor_tensor(was[:, u % 2, 1, :], wa[:, :], was[:, u % 2, 0, :].bitcast(F32), ALU.subtract).then_inc(wa_lo, 1)
                    if chunk < CHUNKS - 1:
                        split_u(it + (u + 1) // UN, (u + 1) % UN, j + 1)
                        store_w(j + JG, it8, u, 1 - chunk % 2)

                split_u(0, 0, 0)
                main_loop(dve, step)

            @block.tensor
            def _(pe):
                mm = nc.tensor.matmul

                def build_w(m, u):
                    pe.wait_ge(ai_ready, m + 1)
                    pe.wait_ge(bj_ready, m + 1)
                    pe.wait_ge(w_stored, m + 1)
                    for n in range(BT):
                        for i in range(3):
                            ins = mm(w_bank[:, n * JG:(n + 1) * JG], Ai[:, u % 2, n, :], Bj[:, u % 2, 1 + i, n, :],
                                     start=(i == 0), stop=(i == 2))
                    ins.then_inc(w_done, 1)

                def add_v(buf, first=False, last=False):
                    for h in range(2):
                        cols = slice(512 * h, 512 * h + 512)
                        for t in range(TILES):
                            tok = slice(t * P, (t + 1) * P)
                            for n, (a, v) in enumerate(((0, 0), (0, 1), (1, 0))):
                                ins = mm(acc[2 * t + h][:, :], was[:, buf, a, tok], Vs[:, v, cols],
                                         start=False, stop=last and n == 2)
                        ins.then_inc(acc_done, 1)

                pe.wait_ge(zeroed, 2)
                credits = [act_done, act_done, w_done, w_done, acc_done, None]
                for i, credit in enumerate(credits):
                    ins = mm(acc[i][:, :], was[:, 1, 0, 0:P], Vs[:, 0, 0:512], start=True, stop=False)
                    if credit is not None:
                        ins.then_inc(credit, 1)
                with pe.Fori(0, JG // UN) as it8:
                    for u in range(UN):
                        build_w(it8 * UN + u, u)

                def step(it, it8, chunk, u, j, last):
                    pe.wait_ge(u_lo, j + 1)
                    pe.wait_ge(gelu_done, j + 1)
                    for k in range(KD):
                        for n, (a, v) in enumerate(((0, 0), (0, 1), (1, 0))):
                            ins = mm(act_bank[:, 0:TOK], Us[:, u % 2, a, k * P:(k + 1) * P], xs[:, v, k, :],
                                     start=(k == 0 and n == 0), stop=(k == KD - 1 and n == 2))
                    ins.then_inc(act_done, 1)
                    pe.wait_ge(wa_lo, j + 1)
                    pe.wait_ge(v_lo, 2 * j + 1)
                    add_v((u + 1) % 2)
                    if chunk < CHUNKS - 1:
                        build_w(j + JG, u)

                main_loop(pe, step)
                pe.wait_ge(wa_lo, STEPS + 1)
                pe.wait_ge(v_lo, 2 * STEPS + 1)
                add_v(1, last=True)
        clear(nc, sems + c.ring_full)


def finish(c, l, acc, late):
    nc, dram = c.nc, c.dram
    G = N_EARLY
    turns = [("ada", G)] + feature_turns(0) + [("ada", G + 1), ("ada", G + 2)] + feature_turns(1)
    turns += [("ada", G + 3)] + feature_turns(2)
    with ExitStack() as ctx:
        s = Stage(c, ctx, "finish", turns, ["bias_in", "gate_stored", "vdone", "var_ready", "std_ready", "normed", "stored"], banks=2)
        S = s.named
        (x, gates, gb), x_in = late, c.late_in
        piece_full = [s.sem(f"piece_full{i}") for i in range(SLOTS)]
        part, gate_rows = s.sb("part", [P, TILES, D]), s.sb("gate_rows", [2, D])
        stats, mv, rstd = s.sb("stats", [P, TILES, 12]), s.sb("mv", [P, TILES, 2]), s.sb("rstd", [P, TILES])
        with nc.Block() as block:

            @block.scalar
            def _(act):
                def root(t):
                    act.wait_ge(S["var_ready"], t + 1)
                    nc.scalar.activation(rstd[:, t:t + 1], mv[:, t, 1:2], ACT.Sqrt).then_inc(S["std_ready"], 1)

                act.dma_start(gate_rows[0:1, :], dram["b_ada"][NEXT:NEXT + 1, 5 * D:6 * D]).then_inc(S["bias_in"], 16)
                root(0)
                root(1)
                ada_copy(c, s, act, gate_rows, G, G)
                for h in range(2):
                    modulate(c, s, act, 0, 0, h, True)
                ada_copy(c, s, act, gate_rows, G + 1, G)
                root(2)
                ada_copy(c, s, act, gate_rows, G + 2, G)
                for h in range(2):
                    modulate(c, s, act, 0, 1, h, True)
                ada_copy(c, s, act, gate_rows, G + 3, G)
                store_gate(c, s, act, gate_rows[:, :], 1, gate_place(c, l + 1, 1), S["gate_stored"])
                modulate(c, s, act, 0, 2, 1)
                act.wait_ge(S["gate_stored"], 16)

            @block.sync
            def _(sp):
                for n in range(N_GATE2):
                    sp.dma_start(c.ring[:, slot(n), :], dram["w_ada"][NEXT, G + n]).then_inc(piece_full[slot(n)], 16)
                for n in range(SLOTS):
                    b, r = s.steps.at("ada", G + n)
                    sp.wait_ge(s.full[b], r + 1)
                    fill_slot(c, sp, NEXT, n)
                    if n < TILES:
                        sp.wait_ge(S["normed"], n + 1)
                        sp.dma_start(c.x_dram[n], x[:, n, :]).then_inc(S["stored"], 16)
                        sp.dma_start(dram["y"][n], x[:, n, :]).then_inc(S["stored"], 16)
                sp.wait_ge(S["stored"], 32 * TILES)

            @block.vector
            def _(dve):
                link = in_order(dve, S["vdone"])
                dve.wait_ge(x_in, 16 * LOADS_FOR_NORM)
                for t in range(TILES):
                    for h in range(2):
                        cols = slice(512 * h, 512 * h + 512)
                        ins = nc.vector.tensor_tensor(part[:, t, cols], acc[2 * t + h][:, :], gates[:, SEQ_OF_TILE[t], cols], ALU.mult)
                    link(ins)
                    link(nc.vector.scalar_tensor_tensor(x[:, t, :], x[:, t, :], ALPHA, part[:, t, :], ALU.mult, ALU.add))
                    norm_steps(nc, dve, link, x[:, t, :], stats[:, t, :], mv[:, t, :], rstd[:, t:t + 1], S["var_ready"],
                               S["std_ready"], t + 1, gb[:, 0, :], gb[:, 1, :], x[:, t, :]).then_inc(S["normed"], 1)
                modulate(c, s, dve, 0, TILES - 1, 0)

            @block.tensor
            def _(pe):
                def features(t):
                    pe.wait_ge(S["normed"], t + 1)
                    transpose_x(c, s, pe, x, t)

                pe.wait_ge(S["bias_in"], 16)
                for n in range(N_GATE2):
                    ada_product(c, s, pe, gate_rows, piece_full[slot(n)], 16, slot(n), G + n, G)
                    if n == 0:
                        features(0)
                    if n == 2:
                        features(1)
                features(2)
        clear(nc, s.sems + [x_in])


def build(nc, dram):
    with ExitStack() as ctx:
        c = make_core(nc, ctx, dram)
        begin(c)
        with nc.Fori(0, DEPTH) as l:
            with ExitStack() as mid:
                pT = mid.enter_context(nc.sbuf_tensor("pT", [P, N_IN, TOK], F32))
                mixT = mid.enter_context(nc.sbuf_tensor("mixT", [P, KD, TOK], F32))
                rw = rwkv_tables(c, mid)
                with ExitStack() as until_attention:
                    att = attention_tables(c, until_attention)
                    project(c, l, pT, att, rw)
                    attention(c, l, pT, mixT, att)
                rwkv(c, l, pT, mixT, rw)
                output(c, l, pT, mixT)
            with ExitStack() as mid:
                xs = mid.enter_context(nc.sbuf_tensor("xs", [P, 2, KD, TOK], F32R))
                route = mid.enter_context(nc.sbuf_tensor("route", [P, 5, TOK], BF16))
                routing(c, l, xs, route)
                acc = [mid.enter_context(nc.psum_tensor(f"acc{i}", [P, 512], F32)) for i in range(6)]
                W = mid.enter_context(nc.sbuf_tensor("W", [P, 2, TOK, JG], F32))
                late = norm_inputs(W[:, 0].rearrange("p t n -> p (t n)"))
                experts(c, l, xs, route, acc, W, late)
                finish(c, l, acc, late)
        for full in c.ring_full:
            nc.sync.wait_ge(full, 16)


def shape_constants():
    f = np.float32
    half = HD // 4
    freqs = (f(10000.0) ** (-np.arange(half, dtype=f) / f(half))).astype(f)
    t = np.arange(2 * P)
    cosT, sinT = np.zeros((HD, 2 * P), f), np.zeros((HD, 2 * P), f)
    rot = np.zeros((P, P), f)
    for axis, pos in enumerate((t // HD, t % HD)):
        ang = pos.astype(f)[None, :] * freqs[:, None]
        for part in range(2):
            lo = axis * 2 * half + part * half
            cosT[lo:lo + half], sinT[lo:lo + half] = np.cos(ang), np.sin(ang)
    for head in range(2):
        for axis in range(2):
            for i in range(half):
                a = head * HD + axis * 2 * half + i
                rot[a + half, a], rot[a, a + half] = -1.0, 1.0
    q, k = np.arange(P)[:, None], np.arange(2 * P)[None, :]
    mask = np.zeros((P, 2, 3 * P), f)
    for n in range(2):
        mask[:, n, P:] = np.where(np.abs(k - (q + n * P)) <= 128, 0.0, NEG)
    s_, t_ = np.arange(P)[:, None], np.arange(P)[None, :]
    same = (s_ // CHUNK) == (t_ // CHUNK)
    gram, level = np.zeros((P, 2, 4, P), f), np.zeros((P, 2, N_LEVELS, P), f)
    for d in range(2):
        before = (s_ < t_) if d == 0 else (s_ > t_)
        strict, incl = same & before, same & (before | (s_ == t_))
        gram[:, d, 0], gram[:, d, 1], gram[:, d, 2], gram[:, d, 3] = strict, incl, strict, incl
        for lev in range(N_LEVELS):
            level[:, d, lev] = before & ((s_ >> (lev + 1)) == (t_ >> (lev + 1))) & ((s_ >> lev) != (t_ >> lev))
    resets = np.ones((P, 2 * TOK), f)
    resets[:, ::CHUNK] = 0.0
    return {
        "ident": np.eye(P, dtype=f), "cosT": np.tile(cosT, (2, 1)), "sinT": np.tile(sinT, (2, 1)), "rotate": rot,
        "att_mask": mask, "gram_mask": gram.reshape(P, 2, 4 * P), "level_mask": level,
        "headones": (s_ // HD == t_ // HD).astype(f), "resets": resets,
        "iota16": np.tile(np.arange(TOPK, dtype=f), (P, 1)),
    }


def lay_out(i):
    L = DEPTH
    cat, tile = np.concatenate, np.ascontiguousarray

    def blocks(w, n):
        N = w.shape[2]
        per = PIECE // KD // n
        return tile(w.reshape(L, KD, P, N // n // per, per, n).transpose(0, 3, 2, 4, 1, 5)).reshape(L, -1, P, PIECE)

    def halves(a):
        a = a.reshape(L, -1, 2, P)
        return a.transpose(0, 3, 1, 2).reshape(L, P, -1)

    order = np.concatenate([np.r_[b * HD:(b + 1) * HD, (4 + b) * HD:(5 + b) * HD] for b in range(4)])
    w_in = cat([i["w_in"][:, :, order], i["w_in"][:, :, 512:]], axis=2)
    starts = [0, 128, 256, 384, 512, 640, 768, 896, 1024, 1152, 1280, 1408, 1536, 1664, 1728, 1856, 1984, 2112, 2240, 2368]
    w_in = cat([w_in[:, :, a:a + P] for a in starts], axis=2)
    w_out = cat([i["w_out"][:, order, :], i["w_out"][:, 512:, :]], axis=1)
    out = {
        "x_in": cat([i["x_prompt"].reshape(1, P, D), i["x_sample"].reshape(2, P, D)]),
        "ln_in": np.stack([i["ln_in_g"], i["ln_in_b"]]),
        "cond": tile(np.stack([i["c_ctx"], i["c"][0]]).reshape(2, KD, P).transpose(2, 1, 0)),
        "b_ada": i["b_ada"],
        "w_ada": blocks(i["w_ada"], PIECE // KD), "w_in": blocks(w_in, P), "w_out": blocks(w_out, PIECE // KD),
        "wq": blocks(i["peer_wq"], P),
        "u": tile(i["peer_u"].reshape(L, P, NK // 2, 2, KD, P).transpose(0, 2, 5, 3, 4, 1)).reshape(L, NK // 2, P, PIECE),
        "v": tile(i["peer_v"].reshape(L, P, NK // 2, 2 * D).transpose(0, 2, 1, 3)),
        "cache_kT": tile(i["cache_k"][0].reshape(L, P, P).transpose(0, 2, 1)),
        "cache_v": i["cache_v"][0].reshape(L, P, P),
        "sink": np.repeat(i["att_sink"][:, None, :], P, axis=1),
        "conv_w": tile(i["conv_w"].reshape(L, 3, 2, P).transpose(0, 3, 2, 1)),
        "cols": cat([halves(i[n]) for n in ("rw_w0", "rw_a0", "rw_kk", "rw_ka", "rw_rk", "rw_lnx_g", "rw_lnx_b")]
                    + [np.zeros((L, P, N_COLS - 18), np.float32)], axis=2),
        "w_up": cat([i["rw_w_up"].reshape(L, 2 * RANK, 256), i["rw_a_up"].reshape(L, 2 * RANK, 256)], axis=1),
        "g_up": i["rw_g_up"],
        "state_T": tile(i["state_rwkv"][0].transpose(0, 1, 2, 4, 3)),
        "ln1": np.stack([i["ln1_g"], i["ln1_b"]], axis=1), "ln2": np.stack([i["ln2_g"], i["ln2_b"]], axis=1),
        "subkeys_T": tile(i["peer_subkeys"].reshape(L, 2 * PH, NK, P).transpose(0, 3, 1, 2)),
    }
    out.update(shape_constants())
    return {k: tile(v) for k, v in out.items()}


OUTS = {"y": [TILES, P, D], "new_k": [DEPTH, P, P], "new_v": [DEPTH, P, P], "new_state_T": [DEPTH, 2, 4, HD, HD]}


def kernel(**inputs):
    import concourse.bacc as bacc
    from concourse.bass_utils import run_bass_kernel_spmd as run
    import ml_dtypes

    arrays = lay_out({k: np.asarray(v) for k, v in inputs.items()})
    arrays["iota"] = np.tile(np.arange(NK + JG, dtype=np.float32), (P, 1)).astype(ml_dtypes.bfloat16)
    nc = bacc.Bacc("TRN2", target_bir_lowering=False, num_devices=1)
    dram = {k: nc.dram_tensor("in_" + k, v.shape, mybir.dt.from_np(v.dtype), kind="ExternalInput").ap() for k, v in arrays.items()}
    dram.update({k: nc.dram_tensor("out_" + k, v, F32, kind="ExternalOutput").ap() for k, v in OUTS.items()})
    build(nc, dram)
    r = run(nc, [{"in_" + k: v for k, v in arrays.items()}], core_ids=[0]).results[0]
    y, nk, nv = r["out_y"], r["out_new_k"], r["out_new_v"]
    return (y[0:1], y[1:3].reshape(1, 2 * P, D),
            nk.transpose(0, 2, 1).reshape(1, DEPTH, P, 2, HD), nv.transpose(0, 2, 1).reshape(1, DEPTH, P, 2, HD),
            r["out_new_state_T"].transpose(0, 1, 2, 4, 3)[None])
```
